# Optimizing a Trainium2 kernel written in Bass

```python
import math
import jax, jax.numpy as jnp
from jax import lax
import numpy as np

D_MODEL = 1024
BATCH = 1
SEQ = 256
DEPTH = 2

EPS = 1e-6
MIX_W = 512
N_BRANCH = 4
A_HEADS = 4
A_V_DIM = MIX_W // A_HEADS
A_QK_DIM = A_V_DIM // 2
ATTN_Q_BLOCK = 128
B_HEADS = 4
B_HEAD_DIM = MIX_W // B_HEADS
MOBA_BLOCK = 256
MOBA_TOPK = 3
MOBA_Q_CHUNK = 16
C_WIDTH = MIX_W
C_GROUPS = 8
C_GROUP_DIM = C_WIDTH // C_GROUPS
C_CONV = 4
LRU_C = 8.0
D_HEADS = 4
D_HEAD_DIM = MIX_W // D_HEADS
D_CONV = 4
DELTA_CHUNK = 64
IN_SIZES = (MIX_W, MIX_W, MIX_W,
            MIX_W, MIX_W, MIX_W,
            C_WIDTH, C_WIDTH,
            MIX_W, MIX_W, MIX_W, MIX_W,
            D_HEADS, D_HEADS)
IN_COLS = sum(IN_SIZES)
FFN_DENSE = 2816
N_EXPERTS = 8
TOP_K = 2
FFN_EXPERT = 3584
N_DENSE = (DEPTH + 1) // 2
N_MOE = DEPTH // 2

kernel_name = "hybrid_gated_parallel_mixers_moe"

def rmsnorm(x, g, eps=EPS):
    xf = x.astype(jnp.float32)
    y = xf * lax.rsqrt(jnp.mean(xf * xf, axis=-1, keepdims=True) + eps)
    return (y * g.astype(jnp.float32)).astype(x.dtype)

def l2norm(x):
    return x * lax.rsqrt(jnp.sum(x * x, axis=-1, keepdims=True) + 1e-6)

def causal_dwconv(x, w):
    K, C = w.shape
    return lax.conv_general_dilated(x, w[:, None, :].astype(x.dtype), window_strides=(1,),
                                    padding=[(K - 1, 0)], dimension_numbers=('NWC', 'WIO', 'NWC'),
                                    feature_group_count=C)

def split_in_proj(p):
    idx = [int(i) for i in np.cumsum(IN_SIZES)[:-1]]
    return jnp.split(p, idx, axis=-1)

def diff_attention(q, k, v, lam_q1, lam_k1, lam_q2, lam_k2, sub_g, layer_idx):
    B, S, H, _, dq = q.shape
    f32 = jnp.float32
    lam_init = 0.8 - 0.6 * math.exp(-0.3 * layer_idx)
    lam = (jnp.exp(jnp.sum(lam_q1.astype(f32) * lam_k1.astype(f32)))
           - jnp.exp(jnp.sum(lam_q2.astype(f32) * lam_k2.astype(f32))) + lam_init)
    scale = dq ** -0.5
    nqb = S // ATTN_Q_BLOCK
    qb = q.reshape(B, nqb, ATTN_Q_BLOCK, H, 2, dq).swapaxes(0, 1)
    kpos = jnp.arange(S)

    def block(args):
        qi, i = args
        s = jnp.einsum('bqhcd,bkhcd->bhcqk', qi, k).astype(f32) * scale
        qpos = i * ATTN_Q_BLOCK + jnp.arange(ATTN_Q_BLOCK)
        s = jnp.where(kpos[None, :] <= qpos[:, None], s, -jnp.inf)
        p = jax.nn.softmax(s, axis=-1)
        w = (p[:, :, 0] - lam * p[:, :, 1]).astype(v.dtype)
        return jnp.einsum('bhqk,bkhd->bqhd', w, v)

    o = lax.map(block, (qb, jnp.arange(nqb)))
    o = o.swapaxes(0, 1).reshape(B, S, H, -1)
    o = rmsnorm(o, sub_g, eps=1e-5) * (1.0 - lam_init)
    return o.reshape(B, S, -1)

def moba_attention(q, k, v):
    B, S, H, d = q.shape
    f32 = jnp.float32
    nb = -(-S // MOBA_BLOCK)
    pad = nb * MOBA_BLOCK - S
    kp = jnp.pad(k, ((0, 0), (0, pad), (0, 0), (0, 0)))
    vp = jnp.pad(v, ((0, 0), (0, pad), (0, 0), (0, 0)))
    kb = kp.reshape(B, nb, MOBA_BLOCK, H, d).transpose(0, 3, 1, 2, 4)
    vb = vp.reshape(B, nb, MOBA_BLOCK, H, d).transpose(0, 3, 1, 2, 4)
    n_cand = nb - 1
    k_sel = min(MOBA_TOPK, n_cand)
    n_chunk = S // MOBA_Q_CHUNK
    qc = q.reshape(B, n_chunk, MOBA_Q_CHUNK, H, d).swapaxes(0, 1)
    scale = d ** -0.5
    b_idx = jnp.arange(B)[:, None, None, None]
    h_idx = jnp.arange(H)[None, :, None, None]
    kmean = jnp.mean(kb[:, :, :max(n_cand, 1)].astype(f32), axis=3)

    def chunk(args):
        qi, c = args
        start = c * MOBA_Q_CHUNK
        own = start // MOBA_BLOCK
        qpos = start + jnp.arange(MOBA_Q_CHUNK)
        k_own = lax.dynamic_slice_in_dim(kp, own * MOBA_BLOCK, MOBA_BLOCK, axis=1)
        v_own = lax.dynamic_slice_in_dim(vp, own * MOBA_BLOCK, MOBA_BLOCK, axis=1)
        s_own = jnp.einsum('bqhd,blhd->bhql', qi, k_own).astype(f32) * scale
        kpos = own * MOBA_BLOCK + jnp.arange(MOBA_BLOCK)
        s_own = jnp.where(kpos[None, :] <= qpos[:, None], s_own, -jnp.inf)
        if k_sel == 0:
            p = jax.nn.softmax(s_own, axis=-1).astype(v.dtype)
            return jnp.einsum('bhql,blhd->bqhd', p, v_own)
        gate = jnp.einsum('bqhd,bhnd->bhqn', qi.astype(f32), kmean)
        gate = jnp.where(jnp.arange(n_cand) < own, gate, -jnp.inf)
        _, sel = lax.top_k(gate, k_sel)
        ksel = kb[b_idx, h_idx, sel]
        vsel = vb[b_idx, h_idx, sel]
        s_sel = jnp.einsum('bqhd,bhqkld->bhqkl', qi, ksel).astype(f32) * scale
        valid = jnp.arange(k_sel) < own
        s_sel = jnp.where(valid[:, None], s_sel, -jnp.inf).reshape(B, H, MOBA_Q_CHUNK, k_sel * MOBA_BLOCK)
        p = jax.nn.softmax(jnp.concatenate([s_sel, s_own], axis=-1), axis=-1).astype(v.dtype)
        p_sel = p[..., :k_sel * MOBA_BLOCK].reshape(B, H, MOBA_Q_CHUNK, k_sel, MOBA_BLOCK)
        p_own = p[..., k_sel * MOBA_BLOCK:]
        return (jnp.einsum('bhqkl,bhqkld->bqhd', p_sel, vsel)
                + jnp.einsum('bhql,blhd->bqhd', p_own, v_own))

    o = lax.map(chunk, (qc, jnp.arange(n_chunk)))
    return o.swapaxes(0, 1).reshape(B, S, H * d)

def rglru_mixer(xb, gb, conv_w, conv_b, w_a, b_a, w_x, b_x, lam):
    B, S, W = xb.shape
    f32 = jnp.float32
    xc = causal_dwconv(xb, conv_w) + conv_b
    xg = xc.reshape(B, S, C_GROUPS, C_GROUP_DIM)
    r = jax.nn.sigmoid(jnp.einsum('bsgi,gij->bsgj', xg, w_a) + b_a).reshape(B, S, W)
    i = jax.nn.sigmoid(jnp.einsum('bsgi,gij->bsgj', xg, w_x) + b_x).reshape(B, S, W)
    log_a = -LRU_C * r.astype(f32) * jax.nn.softplus(-lam.astype(f32))
    a = jnp.exp(log_a)
    u = jnp.sqrt(-jnp.expm1(2.0 * log_a)) * (i * xc).astype(f32)

    def combine(lhs, rhs):
        a1, u1 = lhs
        a2, u2 = rhs
        return a1 * a2, a2 * u1 + u2

    _, hs = lax.associative_scan(combine, (a, u), axis=1)
    return hs.astype(xb.dtype) * jax.nn.gelu(gb)

def chunk_gated_delta_rule(q, k, v, g, beta):
    B, S, H, dk = q.shape
    dv = v.shape[-1]
    C = DELTA_CHUNK
    N = S // C

    def chunks(t):
        return jnp.moveaxis(t.reshape(B, N, C, H, *t.shape[3:]), 3, 1)

    q, k, v, g, beta = (chunks(t) for t in (q, k, v, g, beta))
    g = jnp.cumsum(g, axis=-1)
    causal = jnp.tril(jnp.ones((C, C), dtype=bool))
    strict = jnp.tril(jnp.ones((C, C), dtype=bool), -1)
    decay = jnp.exp(jnp.where(causal, g[..., :, None] - g[..., None, :], -jnp.inf))
    kb = k * beta[..., None]
    low = jnp.where(strict, jnp.einsum('bhncd,bhnmd->bhncm', kb, k) * decay, 0.0)
    rhs = jnp.concatenate([v * beta[..., None], kb * jnp.exp(g)[..., None]], axis=-1)
    sol = lax.linalg.triangular_solve(low, rhs, left_side=True, lower=True, unit_diagonal=True)
    u, w = sol[..., :dv], sol[..., dv:]
    qk = jnp.einsum('bhncd,bhnmd->bhncm', q, k) * decay
    q_dec = q * jnp.exp(g)[..., None]
    g_last = g[..., -1]
    k_dec = k * jnp.exp(g_last[..., None] - g)[..., None]

    def step(state, inp):
        qd, kd, ui, wi, qki, gl = inp
        v_new = ui - jnp.einsum('bhcd,bhde->bhce', wi, state)
        o = jnp.einsum('bhcd,bhde->bhce', qd, state) + jnp.einsum('bhcm,bhme->bhce', qki, v_new)
        state = state * jnp.exp(gl)[..., None, None] + jnp.einsum('bhcd,bhce->bhde', kd, v_new)
        return state, o

    xs = tuple(jnp.moveaxis(t, 2, 0) for t in (q_dec, k_dec, u, w, qk, g_last))
    state0 = jnp.zeros((B, H, dk, dv), jnp.float32)
    _, o = lax.scan(step, state0, xs)
    return jnp.transpose(o, (1, 0, 3, 2, 4)).reshape(B, S, H, dv)

def gated_deltanet_mixer(q, k, v, z, beta_logit, a_logit, conv_w, A_log, dt_bias, norm_g):
    B, S, _ = q.shape
    f32 = jnp.float32
    qkv = jax.nn.silu(causal_dwconv(jnp.concatenate([q, k, v], axis=-1), conv_w))
    q, k, v = jnp.split(qkv.astype(f32), 3, axis=-1)
    q = l2norm(q.reshape(B, S, D_HEADS, D_HEAD_DIM)) * D_HEAD_DIM ** -0.5
    k = l2norm(k.reshape(B, S, D_HEADS, D_HEAD_DIM))
    v = v.reshape(B, S, D_HEADS, D_HEAD_DIM)
    beta = jax.nn.sigmoid(beta_logit.astype(f32))
    g = -jnp.exp(A_log.astype(f32)) * jax.nn.softplus(a_logit.astype(f32) + dt_bias.astype(f32))
    o = chunk_gated_delta_rule(q, k, v, g, beta)
    o = rmsnorm(o, norm_g) * jax.nn.silu(z.astype(f32).reshape(B, S, D_HEADS, D_HEAD_DIM))
    return o.reshape(B, S, -1).astype(z.dtype)

def swiglu(x, w1, w3, w2):
    return (jax.nn.silu(x @ w1) * (x @ w3)) @ w2

def moe_swiglu(x, w_router, w1, w3, w2):
    logits = jnp.einsum('bsd,de->bse', x, w_router).astype(jnp.float32)
    top_v, top_i = lax.top_k(logits, TOP_K)
    top_p = jax.nn.softmax(top_v, axis=-1)
    gates = jnp.sum(jax.nn.one_hot(top_i, N_EXPERTS, dtype=jnp.float32) * top_p[..., None], axis=-2)
    out = jnp.zeros_like(x)
    for e in range(N_EXPERTS):
        out = out + gates[..., e:e + 1].astype(x.dtype) * swiglu(x, w1[e], w3[e], w2[e])
    return out

def setup_inputs(seed: int = 0) -> dict:
    key = jax.random.key(seed)
    ks = iter(jax.random.split(key, 48))
    f32 = jnp.float32
    L = DEPTH

    def nrm(shape, scale):
        return jax.random.normal(next(ks), shape, f32) * scale

    def gain(shape):
        return 1.0 + 0.02 * jax.random.normal(next(ks), shape, f32)

    x = nrm((BATCH, SEQ, D_MODEL), 1.0)
    norm_mix = gain((L, D_MODEL))
    norm_ffn = gain((L, D_MODEL))
    norm_final = gain((D_MODEL,))
    w_in = nrm((L, D_MODEL, IN_COLS), D_MODEL ** -0.5)
    lam_q1 = nrm((L, A_QK_DIM), 0.1)
    lam_k1 = nrm((L, A_QK_DIM), 0.1)
    lam_q2 = nrm((L, A_QK_DIM), 0.1)
    lam_k2 = nrm((L, A_QK_DIM), 0.1)
    a_subln = gain((L, A_V_DIM))
    c_conv_w = nrm((L, C_CONV, C_WIDTH), C_CONV ** -0.5)
    c_conv_b = nrm((L, C_WIDTH), 0.01)
    c_w_a = nrm((L, C_GROUPS, C_GROUP_DIM, C_GROUP_DIM), C_GROUP_DIM ** -0.5)
    c_b_a = nrm((L, C_GROUPS, C_GROUP_DIM), 0.01)
    c_w_x = nrm((L, C_GROUPS, C_GROUP_DIM, C_GROUP_DIM), C_GROUP_DIM ** -0.5)
    c_b_x = nrm((L, C_GROUPS, C_GROUP_DIM), 0.01)
    a0 = jax.random.uniform(next(ks), (L, C_WIDTH), f32, 0.9, 0.999) ** (1.0 / LRU_C)
    c_lambda = jnp.log(a0) - jnp.log1p(-a0)
    d_conv_w = nrm((L, D_CONV, 3 * MIX_W), D_CONV ** -0.5)
    d_A_log = jnp.log(jax.random.uniform(next(ks), (L, D_HEADS), f32, 1.0, 16.0))
    dt = jnp.exp(jax.random.uniform(next(ks), (L, D_HEADS), f32, math.log(1e-3), math.log(1e-1)))
    d_dt_bias = dt + jnp.log(-jnp.expm1(-dt))
    d_norm = gain((L, D_HEAD_DIM))
    w_gate = nrm((L, D_MODEL, N_BRANCH, D_MODEL), D_MODEL ** -0.5)
    b_gate = nrm((L, N_BRANCH, D_MODEL), 0.01)
    w_branch = nrm((L, N_BRANCH, MIX_W, D_MODEL), MIX_W ** -0.5)
    w_out = nrm((L, D_MODEL, D_MODEL), D_MODEL ** -0.5)
    ffn_w1 = nrm((N_DENSE, D_MODEL, FFN_DENSE), D_MODEL ** -0.5)
    ffn_w3 = nrm((N_DENSE, D_MODEL, FFN_DENSE), D_MODEL ** -0.5)
    ffn_w2 = nrm((N_DENSE, FFN_DENSE, D_MODEL), FFN_DENSE ** -0.5)
    router = nrm((N_MOE, D_MODEL, N_EXPERTS), D_MODEL ** -0.5)
    moe_w1 = nrm((N_MOE, N_EXPERTS, D_MODEL, FFN_EXPERT), D_MODEL ** -0.5)
    moe_w3 = nrm((N_MOE, N_EXPERTS, D_MODEL, FFN_EXPERT), D_MODEL ** -0.5)
    moe_w2 = nrm((N_MOE, N_EXPERTS, FFN_EXPERT, D_MODEL), FFN_EXPERT ** -0.5)
    return {"x": x, "norm_mix": norm_mix, "norm_ffn": norm_ffn, "norm_final": norm_final,
            "w_in": w_in, "lam_q1": lam_q1, "lam_k1": lam_k1, "lam_q2": lam_q2, "lam_k2": lam_k2,
            "a_subln": a_subln, "c_conv_w": c_conv_w, "c_conv_b": c_conv_b, "c_w_a": c_w_a,
            "c_b_a": c_b_a, "c_w_x": c_w_x, "c_b_x": c_b_x, "c_lambda": c_lambda,
            "d_conv_w": d_conv_w, "d_A_log": d_A_log, "d_dt_bias": d_dt_bias, "d_norm": d_norm,
            "w_gate": w_gate, "b_gate": b_gate, "w_branch": w_branch, "w_out": w_out,
            "ffn_w1": ffn_w1, "ffn_w3": ffn_w3, "ffn_w2": ffn_w2, "router": router,
            "moe_w1": moe_w1, "moe_w3": moe_w3, "moe_w2": moe_w2}

def reference(x, norm_mix, norm_ffn, norm_final, w_in, lam_q1, lam_k1, lam_q2, lam_k2, a_subln,
              c_conv_w, c_conv_b, c_w_a, c_b_a, c_w_x, c_b_x, c_lambda, d_conv_w, d_A_log,
              d_dt_bias, d_norm, w_gate, b_gate, w_branch, w_out, ffn_w1, ffn_w3, ffn_w2, router,
              moe_w1, moe_w3, moe_w2):
    B, S, _ = x.shape
    h = x
    for l in range(DEPTH):
        xn = rmsnorm(h, norm_mix[l])
        (aq, ak, av, bq, bk, bv, cx, cg, dq, dk, dv, dz, dbeta, da) = split_in_proj(xn @ w_in[l])
        o_a = diff_attention(aq.reshape(B, S, A_HEADS, 2, A_QK_DIM), ak.reshape(B, S, A_HEADS, 2, A_QK_DIM),
                             av.reshape(B, S, A_HEADS, A_V_DIM), lam_q1[l], lam_k1[l], lam_q2[l],
                             lam_k2[l], a_subln[l], l)
        o_b = moba_attention(bq.reshape(B, S, B_HEADS, B_HEAD_DIM), bk.reshape(B, S, B_HEADS, B_HEAD_DIM),
                             bv.reshape(B, S, B_HEADS, B_HEAD_DIM))
        o_c = rglru_mixer(cx, cg, c_conv_w[l], c_conv_b[l], c_w_a[l], c_b_a[l], c_w_x[l], c_b_x[l],
                          c_lambda[l])
        o_d = gated_deltanet_mixer(dq, dk, dv, dz, dbeta, da, d_conv_w[l], d_A_log[l], d_dt_bias[l],
                                   d_norm[l])
        branches = jnp.stack([o_a, o_b, o_c, o_d], axis=2)
        y_br = jnp.einsum('bsnw,nwd->bsnd', branches, w_branch[l])
        gates = jax.nn.sigmoid(jnp.einsum('bsd,dne->bsne', xn, w_gate[l]) + b_gate[l])
        h = h + jnp.sum(gates * y_br, axis=2) @ w_out[l]
        xn = rmsnorm(h, norm_ffn[l])
        if l % 2 == 0:
            h = h + swiglu(xn, ffn_w1[l // 2], ffn_w3[l // 2], ffn_w2[l // 2])
        else:
            h = h + moe_swiglu(xn, router[l // 2], moe_w1[l // 2], moe_w3[l // 2], moe_w2[l // 2])
    return rmsnorm(h, norm_final)


_drawn_inputs = setup_inputs


def setup_inputs(seed=0):
    import zlib

    import numpy as np

    out = dict(_drawn_inputs(seed))
    spreads = {}
    factors = {'norm_final': 2.995, 'c_b_a': 8.0, 'c_b_x': 8.0, 'd_norm': 3.151, 'b_gate': 3.973}
    for name, (base, spread) in spreads.items():
        noise = np.random.default_rng([zlib.crc32(name.encode()), seed]).standard_normal(out[name].shape)
        drawn = base * np.exp(spread * noise) if base else spread * noise
        out[name] = __import__('jax').numpy.asarray(drawn.astype(out[name].dtype))
    for name, factor in factors.items():
        out[name] = (out[name] * factor).astype(out[name].dtype)
    return out
```

```python
import math
from contextlib import ExitStack

import concourse.bass as bass
from concourse import mybir

F32 = mybir.dt.float32
I32 = mybir.dt.int32
ALU = mybir.AluOpType
ACT = mybir.ActivationFunctionType
AX = mybir.AxisListType.X

P = 128
LAYERS, SEQ, DM = 2, 256, 1024
TT = SEQ // P
KD = DM // P
MIX = 512
NB = MIX // P
HEADS = 4
BRANCHES = 4
TAPS = 4
UC = 256
UNIT = KD * UC
SLOTS = 6
NEG = -1.0e30
LRU_C = 8.0
EXPERTS, TOP_K = 8, 2
FFN, FFE = 2816, 3584
CHUNK = UC
DENSE_CHUNKS, MOE_CHUNKS = FFN // CHUNK, FFE // CHUNK
OVERFLOWS = (TOP_K * SEQ) // (P + 1)
PASSES = EXPERTS + OVERFLOWS

U_C, U_D, U_Z, U_A, U_B, U_GATE = 0, 4, 10, 12, 18, 24
U_BR = U_GATE + BRANCHES * DM // UC
U_OUT = U_BR + BRANCHES * 2
MIX_UNITS = U_OUT + DM // UC
BRANCH_ORDER = (2, 0, 1, 3)

LEVELS = 7

C_IDENT, C_ONES, C_TRI, C_TRIX, C_CAUSAL, C_NEGT = 0, 128, 256, 384, 512, 768
C_LEVEL = 896
C_IOTA = C_LEVEL + LEVELS * P
C_EIDX, C_EREV = C_IOTA + P, C_IOTA + P + EXPERTS
C_HALF = C_EREV + EXPERTS
C_COLS = C_HALF + 32

PARTS = [("norm_mix", KD), ("norm_ffn", KD), ("c_conv_w", NB * TAPS), ("c_conv_b", NB),
         ("c_b_a", NB), ("c_b_x", NB), ("c_lambda", NB), ("d_conv_w", 3 * NB * TAPS),
         ("b_gate", BRANCHES * KD), ("a_subln", P), ("d_norm", P), ("lam", 256),
         ("d_A_log", HEADS), ("d_dt_bias", HEADS), ("w_ba", KD * 8), ("lam_init", 1),
         ("out_scale", 1), ("router", KD * EXPERTS)]
PCOL, _at = {}, 0
for _name, _n in PARTS:
    PCOL[_name] = (_at, _n)
    _at += _n
P_COLS = _at


class Order:

    def __init__(self, eng, own):
        self.eng, self.own, self.count, self.open = eng, own, {}, []

    def run(self, ins, sem=None):
        sem = self.own if sem is None else sem
        ins.then_inc(sem, 1)
        self.count[sem.name] = self.count.get(sem.name, 0) + 1
        if sem not in self.open:
            self.open.append(sem)

    def settle(self):
        for sem in self.open:
            self.eng.wait_ge(sem, self.count[sem.name])
        self.open = []

    def step(self, ins, sem=None):
        self.run(ins, sem)
        self.settle()


def mixer_schedule():
    chain = [("d_tok", 0), ("d_tok", 1), ("d_back", 0), ("d_cum", 0), ("d_kk", 0)]
    for s in range(LEVELS):
        chain += [("inv_p", s), ("inv_x", s)]
    chain += [("d_v0", 0), ("d_s", 0), ("d_ks", 0), ("d_v1", 0), ("d_o", 0), ("d_oT", 0)]
    attn = []
    for i in range(4 * HEADS + 1):
        attn += [("at_s", i)]
        if i:
            attn += [("at_o", i - 1)]
            if i % 8 == 0:
                attn += [("at_oT", i // 8 - 1)]
    out = [("norm", 0)]
    halves = [(u, f) for u in range(U_BR) for f in range(2)]
    for u, f in halves:
        if (u, f) == (8, 0):
            out.append(("c_gates", 0))
        if (u, f) == (U_Z, 0):
            out.append(("ba", 0))
        if u >= U_A and chain:
            out.append(chain.pop(0))
        if u >= U_GATE and attn:
            out.append(attn.pop(0))
        out.append(("proj", 2 * u + f))
    out += chain + attn
    out += [("branch", j) for j in range(BRANCHES * 4)]
    out += [("out", j) for j in range(DM // UC)]
    return out


def hybrid_trunk(nc, x, consts, params, cdiag, mix_units, dense_units, moe_units, norm_final, out):
    with ExitStack() as ctx:
        def sb(name, shape, dt=F32):
            return ctx.enter_context(nc.sbuf_tensor(name, shape, dt))

        sem_list = []

        def sem(name):
            s = ctx.enter_context(nc.semaphore(name))
            sem_list.append(s)
            return s

        con = sb("con", [P, C_COLS])
        par = sb("par", [P, P_COLS])
        h = sb("h", [P, TT, DM])
        xnT = sb("xnT", [P, KD, SEQ])
        ring = [sb(f"ring{i}", [P, UNIT]) for i in range(SLOTS)]
        small = sb("small", [P, 512])
        gates = sb("gates", [P, BRANCHES * KD, SEQ])
        xs = gates[:, 0:8, :].rearrange("p k t -> p (k t)").rearrange("p (a d) -> p a d", a=TT)
        oT = sb("oT", [P, BRANCHES, NB, SEQ])
        work_c = sb("work_c", [P, 6, NB, SEQ])
        work_d = sb("work_d", [P, 12 * (SEQ + 3)])
        work_e = sb("work_e", [P, 3, NB * SEQ])
        dcv = sb("dcv", [P, 12, SEQ])
        zt = sb("zt", [P, TT, MIX])
        dexp = sb("dexp", [P, TT, HEADS, P])
        cpad = (gates[:, 8:13, :].rearrange("p k t -> p (k t)")[:, 0:NB * (SEQ + 3)]
                .rearrange("p (b t) -> p b t", b=NB))
        cgate = gates[:, 16:20, :]
        cdg = gates[:, 20:24, :].rearrange("p k t -> p (k t)").rearrange("p (g c) -> p g c", g=8)
        dtmp, dusel = (gates[:, b:b + 4, :].rearrange("p k t -> p (k t)")
                       .rearrange("p (t h d) -> p t h d", t=TT, h=HEADS) for b in (24, 28))
        sm = sb("sm", [P, 2, 2, SEQ])
        wT = sb("wT", [P, 2, SEQ])
        ot = sb("ot", [P, TT, HEADS, P])

        banks_all = ctx.enter_context(nc.psum_tensor("banks_all", [P, 8, 512], F32))
        psum = [banks_all[:, i, :] for i in range(8)]

        ident = con[:, C_IDENT:C_IDENT + P]
        ones = con[:, C_ONES:C_ONES + P]
        tri = con[:, C_TRI:C_TRI + P]
        trix = con[:, C_TRIX:C_TRIX + P]
        neg_t = con[:, C_NEGT:C_NEGT + P]

        def par_of(name):
            a, n = PCOL[name]
            return par[:, a:a + n]

        c_xc, c_r, c_i, c_a, c_t, c_g = (work_c[:, i, :, :] for i in range(6))
        aq, ak, bq, bk = (work_c[:, i, :, :] for i in (0, 1, 3, 4))
        av, bv = (work_c[:, i, :, :].rearrange("p b t -> p (b t)").rearrange("p (a d) -> p a d", a=TT)
                  for i in (2, 5))
        acc = work_c[:, 0:2, :, :].rearrange("p a b t -> p (a b) t")
        acc_tmp = work_c[:, 2, 0:2, :]
        dpad = work_d[:, :].rearrange("p (b t) -> p b t", b=12)

        def heads_of(view):
            return view.rearrange("p (t h d) -> p t h d", t=TT, h=HEADS)

        SZ = TT * HEADS * P
        dX, dY, dP = (heads_of(work_d[:, i * SZ:(i + 1) * SZ]) for i in range(3))
        dth = work_e[:, :, :]
        ktok, vtok, dU = (heads_of(work_e[:, i, :]) for i in range(3))
        qtok = heads_of(work_d[:, 0:SZ])
        dK = dcv[:, 4:8, :]
        dQ = dcv[:, 0:4, :]
        tail = dcv[:, 8:12, :].rearrange("p b t -> p (b t)")
        dR = tail[:, 0:512].rearrange("p (h d) -> p h d", h=HEADS)
        dS = tail[:, 512:1024].rearrange("p (h d) -> p h d", h=HEADS)
        hT = [dexp[:, :, :, :].rearrange("p t h d -> p (t h d)")[:, i * 512:(i + 1) * 512] for i in range(2)]
        fth = [dusel[:, :, :, :].rearrange("p t h d -> p (t h d)")[:, i * 512:(i + 1) * 512] for i in range(2)]
        fs = [dtmp[:, :, :, :].rearrange("p t h d -> p (t h d)")[:, i * 512:(i + 1) * 512] for i in range(2)]
        sel = sm[:, 0, :, 0:P]
        selg = sm[:, 1, :, 0:P]
        selgT = wT[:, 0, :]
        xsel = zt[:, :, :].rearrange("p t d -> p (t d)").rearrange("p (k s) -> p k s", k=KD)
        yexp = ot[:, :, :, :].rearrange("p t h d -> p (t h d)")

        at = [0]

        def cols(n):
            at[0] += n
            return small[:, at[0] - n:at[0]]

        ss, rstd, rtmp = cols(16), cols(16), cols(16)
        half_b, half_ba, half_bx = cols(32), cols(NB), cols(NB)
        sp_z, sp_y, sp_s, sp_s2, sp_p = cols(8), cols(8), cols(8), cols(8), cols(8)
        lru, nlru = cols(NB), cols(NB)
        lam_prod, lam_sum, lam_e, lam_neg = cols(P), cols(2), cols(2), cols(1)
        ba, beta, expA, dg = cols(16), cols(8), cols(4), cols(8)
        gcum, darg, dfac = cols(8), cols(16), cols(16)
        a_scale = cols(P)
        mx, nmx, sums, rec, rec2 = (cols(4) for _ in range(5))
        assert at[0] <= 512
        small2 = sb("small2", [P, 512])
        at2 = [0]

        def cols2(n):
            at2[0] += n
            return small2[:, at2[0] - n:at2[0]]

        lg, eq, one1, one2, pick, gsel, member, vslot = (cols2(16) for _ in range(8))
        m0, m1, dm, em, p0, p1, fi = (cols2(2) for _ in range(7))
        cnt, over, pos, incl, tmp8, onesE = (cols2(EXPERTS) for _ in range(6))
        selq = cols2(OVERFLOWS * EXPERTS)
        slot_of, gate_of = cols2(TT * PASSES), cols2(TT * PASSES)
        table = cols2(PASSES + 1)
        table_i = sb("table_i", [P, PASSES + 1], I32)

        names = """in_loaded small_loaded act_own dve_own pool_own
            sumsq_ready rstd_ready xs_ready xT_psum xT_ready unit_done proj_evac
            sp_arg sp_exp c_conv_ready c_gates_psum c_tanh c_a_t c_coef c_sqrt c_gelu_arg c_gelu_tanh
            ba_psum ba_cols ba_act dg_ready
            d_conv_ready d_tanh_ready d_silu_ready d_tok_psum d_tok_ready d_ss_ready d_rs_ready
            d_unit_ready d_back_psum d_T_ready d_cum_psum d_gcum_ready d_args_ready d_exp_ready d_ub_ready
            d_kk_psum d_u_ready d_xy_init dusel_ready inv_p_psum inv_p_ready inv_x_psum xy_ready
            r0_ready v0_psum v0_ready s_psum s_ready ks_psum ks_taken r1_ready v1_psum v1_ready
            o_psum o_ss_ready o_rs_ready z_tanh d_out_ready d_oT_psum
            at_s_psum at_s_taken at_max_ready at_exp_ready at_w_ready at_t_psum at_t_ready at_o_psum
            at_o_taken a_ss_ready a_rs_ready a_out_ready at_oT_psum lam_arg lam_exp
            c_out_ready oA_ready oB_ready oD_ready br_psum br_taken acc_ready out_psum
            h13_psum f_tanh f_h_ready f_hT_ready y_psum w13_used w2_used f_out_taken
            rt_psum rt_arg rt_exp rt_member rank_psum table_ready
            sel_ready gather_psum gather_ready selT_psum selT_ready y_ready scat_psum scat_taken out_stored"""
        S = {}
        for name in names.split():
            S[name] = sem(name)
        slot_loaded = [sem(f"slot_loaded{i}") for i in range(SLOTS)]

        def clear_semaphores():
            nums = sorted(s.num for s in sem_list)
            assert nums == list(range(nums[0], nums[-1] + 1))
            with nc.Block() as block:
                @block.sync
                def _(sp):
                    sp.sem_clear(range(nums[0], nums[-1] + 1))

        with nc.Block() as block:
            @block.sync
            def _(sp):
                sp.dma_start(con[:, :], consts).then_inc(S["in_loaded"], 16)
                sp.dma_start(h[:, :, :], x.rearrange("(t p) d -> p t d", p=P)).then_inc(S["in_loaded"], 16)
                sp.wait_ge(S["in_loaded"], 32)
        clear_semaphores()

        def norm_act(act, o):
            for t in range(TT):
                o.run(act.activation(xnT[:, 0:4, :].rearrange("p k t -> p (k t)"), h[:, t, :], ACT.Square,
                                     scale=DM ** -0.5, accum_out=ss[:, t:t + 1]), S["sumsq_ready"])
                o.settle()

        def pool_rsqrt(pool, o, n, scale, eps, ready):
            o.step(pool.tensor_scalar(rtmp[:, 0:n], ss[:, 0:n], scale, eps, ALU.mult, ALU.add))
            o.run(pool.tensor_tensor(rstd[:, 0:n], rtmp[:, 0:n], con[:, C_HALF:C_HALF + n], ALU.pow), ready)

        def norm_pool(pool, o):
            pool.wait_ge(S["sumsq_ready"], TT)
            pool_rsqrt(pool, o, TT, 1.0, 1e-6, S["rstd_ready"])

        def norm_pe(pe):
            pe.wait_ge(S["xs_ready"], TT)
            for t in range(TT):
                for q in range(2):
                    for k in range(4):
                        last = pe.transpose(psum[2 + 2 * t + q][:, k * P:(k + 1) * P],
                                            xs[:, t, (4 * q + k) * P:(4 * q + k + 1) * P], ident)
                    last.then_inc(S["xT_psum"], 1)

        def norm_dve(dve, o, gain):
            dve.wait_ge(S["rstd_ready"], 1)
            for t in range(TT):
                o.run(dve.tensor_scalar(xs[:, t, :], h[:, t, :], rstd[:, t:t + 1], None, ALU.mult),
                      S["xs_ready"])
            for t in range(TT):
                for q in range(2):
                    dve.wait_ge(S["xT_psum"], 2 * t + q + 1)
                    o.run(dve.tensor_tensor(
                        xnT[:, 4 * q:4 * q + 4, t * P:(t + 1) * P],
                        psum[2 + 2 * t + q][:, :].rearrange("p (k s) -> p k s", k=4),
                        gain[:, 4 * q:4 * q + 4].unsqueeze(2).to_broadcast([P, 4, P]), ALU.mult),
                        S["xT_ready"])

        def softplus_dve(dve, o, n, sem_arg, sem_exp, count):
            z, y, s, s2, p = (c[:, 0:n] for c in (sp_z, sp_y, sp_s, sp_s2, sp_p))
            o.step(dve.tensor_scalar(s, z, -1.0, None, ALU.mult))
            o.step(dve.tensor_tensor(y, z, s, ALU.max), sem_arg)
            dve.wait_ge(sem_exp, count)
            o.step(dve.tensor_scalar(s, y, 2.0, None, ALU.add))
            o.step(dve.reciprocal(s, s))
            o.step(dve.tensor_tensor(s, y, s, ALU.mult))
            o.step(dve.tensor_tensor(s2, s, s, ALU.mult))
            o.step(dve.tensor_scalar(p, s2, 1.0 / 17, None, ALU.mult))
            for k in range(7, 0, -1):
                o.step(dve.scalar_tensor_tensor(p, p, 1.0 / (2 * k + 1), s2, ALU.add, ALU.mult))
            o.step(dve.scalar_tensor_tensor(p, p, 1.0, s, ALU.add, ALU.mult))
            o.step(dve.tensor_scalar(z, z, 0.0, None, ALU.max))
            o.step(dve.scalar_tensor_tensor(p, p, 2.0, z, ALU.mult, ALU.add))

        SCHED = mixer_schedule()

        def hb(view):
            return view[:, :].rearrange("p (h d) -> p h d", h=HEADS)

        def bc_row(col, n, width=P):
            return col.unsqueeze(2).to_broadcast([P, n, width])

        def mixer_block(layer):
            with nc.Block() as block:
                @block.sync
                def _(sp):
                    sp.dma_start(par[:, :], params[bass.ds(layer, 1), :, :].rearrange("l p c -> p (l c)")
                                 ).then_inc(S["small_loaded"], 16)
                    sp.dma_start(cdg[:, :, :], cdiag[bass.ds(layer, 1), :, :].rearrange("l p c -> p (l c)")
                                 .rearrange("p (g c) -> p g c", g=8)).then_inc(S["small_loaded"], 16)
                    for u in range(MIX_UNITS):
                        if u >= SLOTS:
                            sp.wait_ge(S["unit_done"], u - SLOTS + 1)
                        sp.dma_start(ring[u % SLOTS][:, :],
                                     mix_units[bass.ds(layer, 1), u, :, :].rearrange("l p c -> p (l c)")
                                     ).then_inc(slot_loaded[u % SLOTS], 16)
                    sp.wait_ge(S["unit_done"], MIX_UNITS)

                @block.tensor
                def _(pe):
                    def unit(u):
                        pe.wait_ge(slot_loaded[u % SLOTS], 16 * (u // SLOTS + 1))
                        return ring[u % SLOTS]

                    def proj(j):
                        u, f = divmod(j, 2)
                        w = unit(u)[:, :].rearrange("p (k c) -> p k c", k=KD)
                        bank = psum[u % 2]
                        if j == 0:
                            pe.wait_ge(S["xT_ready"], 4)
                        if f == 0 and u >= 2:
                            pe.wait_ge(S["proj_evac"], u - 1)
                        token_major = U_Z <= u < U_A or u in (16, 17, 22, 23)
                        for k in range(KD):
                            if token_major:
                                last = pe.matmul(bank[:, f * UC:(f + 1) * UC], xnT[:, k, f * P:(f + 1) * P],
                                                 w[:, k, :], start=(k == 0), stop=(k == KD - 1))
                            else:
                                last = pe.matmul(bank[:, f * SEQ:(f + 1) * SEQ], w[:, k, f * P:(f + 1) * P],
                                                 xnT[:, k, :], start=(k == 0), stop=(k == KD - 1))
                        if f == 1:
                            last.then_inc(S["unit_done"], 1)

                    def c_gates(_):
                        pe.wait_ge(S["c_conv_ready"], 1)
                        pe.wait_ge(S["small_loaded"], 32)
                        for g in range(2):
                            for m in range(NB):
                                last = pe.matmul(psum[2 + 2 * g + m // 2][:, (m % 2) * SEQ:(m % 2 + 1) * SEQ],
                                                 cdg[:, 4 * g + m, :], c_xc[:, m, :], start=True, stop=True)
                            last.then_inc(S["c_gates_psum"], 1)

                    def ba_cols(_):
                        pe.wait_ge(S["c_tanh"], 8)
                        w = par_of("w_ba").rearrange("p (k c) -> p k c", k=KD)
                        for t in range(TT):
                            for k in range(KD):
                                last = pe.matmul(psum[2][:, 8 * t:8 * t + 8], xnT[:, k, t * P:(t + 1) * P],
                                                 w[:, k, :], start=(k == 0), stop=(k == KD - 1))
                        last.then_inc(S["ba_psum"], 1)

                    def d_tok(part):
                        for g, t in (((0, 0), (0, 1), (1, 0), (1, 1)), ((2, 0), (2, 1)))[part]:
                            n = 2 * g + t
                            pe.wait_ge(S["d_silu_ready"], g + 1)
                            if n == 5:
                                pe.wait_ge(S["d_tok_ready"], 1)
                            for hd in range(HEADS):
                                last = pe.transpose(psum[3 + n % 5][:, hd * P:(hd + 1) * P],
                                                    dcv[:, 4 * g + hd, t * P:(t + 1) * P], ident)
                            last.then_inc(S["d_tok_psum"], 1)

                    def d_back(_):
                        pe.wait_ge(S["d_tok_ready"], 6)
                        pe.wait_ge(S["ba_cols"], 1)
                        for g in range(2):
                            for t in range(TT):
                                n = 2 * g + t
                                pe.wait_ge(S["d_unit_ready"], n + 1)
                                src = (qtok, ktok)[g]
                                for hd in range(HEADS):
                                    last = pe.transpose(psum[2 + n][:, hd * P:(hd + 1) * P],
                                                        src[:, t, hd, :], ident)
                                last.then_inc(S["d_back_psum"], 1)

                    def d_cum(_):
                        pe.wait_ge(S["dg_ready"], 1)
                        pe.wait_ge(S["d_T_ready"], 4)
                        for t in range(TT):
                            pe.matmul(psum[6][:, 4 * t:4 * t + 4], tri, dg[:, 4 * t:4 * t + 4], start=True, stop=True)
                        for t in range(TT):
                            for hd in range(HEADS):
                                c = 4 * t + hd
                                pe.matmul(psum[2 + t][:, hd * P:(hd + 1) * P],
                                          dg[:, c:c + 1].to_broadcast([P, P]), tri, start=True, stop=True)
                        for t in range(TT):
                            for hd in range(HEADS):
                                c = 4 * t + hd
                                last = pe.matmul(psum[4 + t][:, hd * P:(hd + 1) * P],
                                                 beta[:, c:c + 1].to_broadcast([P, P]), ident, start=True, stop=True)
                        last.then_inc(S["d_cum_psum"], 1)

                    def d_kk(_):
                        pe.wait_ge(S["d_args_ready"], 4)
                        for t in range(TT):
                            for hd in range(HEADS):
                                last = pe.matmul(psum[2 + t][:, hd * P:(hd + 1) * P], dK[:, hd, t * P:(t + 1) * P],
                                                 dK[:, hd, t * P:(t + 1) * P], start=True, stop=True)
                            last.then_inc(S["d_kk_psum"], 1)
                        for t in range(TT):
                            for hd in range(HEADS):
                                last = pe.matmul(psum[6 + t][:, hd * P:(hd + 1) * P], dK[:, hd, t * P:(t + 1) * P],
                                                 dQ[:, hd, t * P:(t + 1) * P], start=True, stop=True)
                            last.then_inc(S["d_kk_psum"], 1)

                    def inv_p(s):
                        pe.wait_ge(S["dusel_ready"], s + 1)
                        if s == 0:
                            pe.wait_ge(S["d_u_ready"], 4)
                        for t in range(TT):
                            pe.wait_ge(S["xy_ready"], 2 * s + t + 1)
                            for hd in range(HEADS):
                                last = pe.matmul(psum[2 + t][:, hd * P:(hd + 1) * P], dusel[:, t, hd, :],
                                                 dX[:, t, hd, :], start=True, stop=True)
                            last.then_inc(S["inv_p_psum"], 1)

                    def inv_x(s):
                        for t in range(TT):
                            pe.wait_ge(S["inv_p_ready"], 2 * s + t + 1)
                            if s == 0:
                                pe.wait_ge(S["d_ub_ready"], 2)
                            if s < LEVELS - 1:
                                for hd in range(HEADS):
                                    pe.matmul(psum[2 + t][:, hd * P:(hd + 1) * P], dY[:, t, hd, :],
                                              dP[:, t, hd, :], start=True, stop=True)
                            for hd in range(HEADS):
                                last = pe.matmul(psum[4 + t][:, hd * P:(hd + 1) * P], dP[:, t, hd, :],
                                                 dY[:, t, hd, :], start=True, stop=True)
                            last.then_inc(S["inv_x_psum"], 1)

                    def d_v0(_):
                        pe.wait_ge(S["r0_ready"], 1)
                        pe.wait_ge(S["xy_ready"], 2 * LEVELS + 2)
                        for hd in range(HEADS):
                            last = pe.matmul(psum[2][:, hd * P:(hd + 1) * P], dY[:, 0, hd, :], dR[:, hd, :],
                                             start=True, stop=True)
                        last.then_inc(S["v0_psum"], 1)

                    def d_s(_):
                        pe.wait_ge(S["v0_ready"], 1)
                        for hd in range(HEADS):
                            last = pe.matmul(psum[3][:, hd * P:(hd + 1) * P], ktok[:, 0, hd, :], dP[:, 0, hd, :],
                                             start=True, stop=True)
                        last.then_inc(S["s_psum"], 1)

                    def d_ks(_):
                        pe.wait_ge(S["s_ready"], 1)
                        for bank, src in ((2, dK), (4, dQ)):
                            for hd in range(HEADS):
                                last = pe.matmul(psum[bank][:, hd * P:(hd + 1) * P], src[:, hd, P:2 * P],
                                                 dS[:, hd, :], start=True, stop=True)
                        last.then_inc(S["ks_psum"], 1)

                    def d_v1(_):
                        pe.wait_ge(S["r1_ready"], 1)
                        for hd in range(HEADS):
                            last = pe.matmul(psum[3][:, hd * P:(hd + 1) * P], dY[:, 1, hd, :], dR[:, hd, :],
                                             start=True, stop=True)
                        last.then_inc(S["v1_psum"], 1)

                    def d_o(_):
                        pe.wait_ge(S["v1_ready"], 1)
                        pe.wait_ge(S["ks_taken"], 1)
                        for t, bank in ((0, 2), (1, 5)):
                            for hd in range(HEADS):
                                last = pe.matmul(psum[bank][:, hd * P:(hd + 1) * P], dexp[:, t, hd, :],
                                                 dP[:, t, hd, :], start=True, stop=True)
                        last.then_inc(S["o_psum"], 1)

                    def to_features(src, banks, ready):
                        for t in range(TT):
                            for hd in range(HEADS):
                                last = pe.transpose(psum[banks[t]][:, hd * P:(hd + 1) * P], src[:, t, hd, :], ident)
                            last.then_inc(ready, 1)

                    def d_oT(_):
                        pe.wait_ge(S["d_out_ready"], 1)
                        to_features(dtmp, (3, 4), S["d_oT_psum"])

                    def at_s(i):
                        if i < 4 * HEADS:
                            b, hd, qt = i // 8, (i % 8) // 2, i % 2
                            kw = (qt + 1) * P
                            pe.wait_ge(S["proj_evac"], U_A + 4 if b == 0 else U_GATE)
                            if i == 0:
                                pe.wait_ge(S["d_u_ready"], 4)
                                pe.wait_ge(S["o_ss_ready"], 1)
                            else:
                                pe.wait_ge(S["at_s_taken"], i)
                            if i == 9:
                                pe.wait_ge(S["oA_ready"], TT)
                            if b == 0:
                                for c in range(2):
                                    rows = slice(64 * c, 64 * c + 64)
                                    last = pe.matmul(psum[5 + c][:, 0:kw],
                                                     aq[rows, hd, qt * P:(qt + 1) * P], ak[rows, hd, 0:kw],
                                                     start=True, stop=True)
                            else:
                                last = pe.matmul(psum[6][:, 0:kw], bq[:, hd, qt * P:(qt + 1) * P], bk[:, hd, 0:kw],
                                                 start=True, stop=True)
                            last.then_inc(S["at_s_psum"], 1)
                        if i >= 1:
                            qt = (i - 1) % 2
                            pe.wait_ge(S["at_w_ready"], i)
                            if i >= 2:
                                pe.wait_ge(S["at_o_taken"], i - 1)
                            for kb in range(qt + 1):
                                last = pe.transpose(psum[7][:, kb * P:(kb + 1) * P],
                                                    sm[:, (i - 1) % 2, 0, kb * P:(kb + 1) * P], ident)
                            last.then_inc(S["at_t_psum"], 1)

                    def at_o(i):
                        b, hd, qt = i // 8, (i % 8) // 2, i % 2
                        v = (av, bv)[b]
                        pe.wait_ge(S["at_t_ready"], i + 1)
                        for kb in range(qt + 1):
                            last = pe.matmul(psum[7][:, 0:P], wT[:, i % 2, kb * P:(kb + 1) * P],
                                             v[:, kb, hd * P:(hd + 1) * P], start=(kb == 0), stop=(kb == qt))
                        last.then_inc(S["at_o_psum"], 1)

                    def at_oT(b):
                        pe.wait_ge(S["a_out_ready"], b + 1)
                        if b == 0:
                            pe.wait_ge(S["at_s_taken"], 9)
                        to_features(ot, (6, 7), S["at_oT_psum"])

                    def branch(j):
                        n, q = BRANCH_ORDER[j // 4], j % 4
                        u = U_BR + j // 2
                        w = unit(u)[:, :].rearrange("p (k c) -> p k c", k=NB)
                        if j < 2:
                            pe.wait_ge(S["proj_evac"], U_BR)
                        else:
                            pe.wait_ge(S["br_taken"], j - 1)
                        if j % 4 == 0:
                            ready = (S["oA_ready"], S["oB_ready"], S["c_out_ready"], S["oD_ready"])[n]
                            pe.wait_ge(ready, 1 if n == 2 else TT)
                        for f in range(2):
                            b = 2 * (q % 2) + f
                            for k in range(NB):
                                last = pe.matmul(psum[j % 2][:, f * SEQ:(f + 1) * SEQ], w[:, k, b * P:(b + 1) * P],
                                                 oT[:, n, k, :], start=(k == 0), stop=(k == NB - 1))
                        if j % 2 == 0:
                            last.then_inc(S["br_psum"], 1)
                        else:
                            last.then_inc(S["unit_done"], 1)

                    def project_out(j):
                        u = U_OUT + j
                        w = unit(u)[:, :].rearrange("p (k c) -> p k c", k=KD)
                        if j == 0:
                            pe.wait_ge(S["acc_ready"], 1)
                        if j >= 2:
                            pe.wait_ge(S["f_out_taken"], j - 1)
                        for t in range(TT):
                            for k in range(KD):
                                last = pe.matmul(psum[j % 2][:, t * UC:(t + 1) * UC], acc[:, k, t * P:(t + 1) * P],
                                                 w[:, k, :], start=(k == 0), stop=(k == KD - 1))
                        last.then_inc(S["unit_done"], 1)

                    steps = {"norm": lambda _: norm_pe(pe), "proj": proj, "c_gates": c_gates, "ba": ba_cols,
                             "d_tok": d_tok, "d_back": d_back, "d_cum": d_cum, "d_kk": d_kk, "inv_p": inv_p,
                             "inv_x": inv_x, "d_v0": d_v0, "d_s": d_s, "d_ks": d_ks, "d_v1": d_v1, "d_o": d_o,
                             "d_oT": d_oT, "at_s": at_s, "at_o": at_o, "at_oT": at_oT, "branch": branch,
                             "out": project_out}
                    for what, i in SCHED:
                        steps[what](i)

                @block.scalar
                def _(act):
                    o = Order(act, S["act_own"])

                    def copy(dst, src, ready=None, scale=1.0):
                        o.run(act.activation(dst, src, ACT.Copy, scale=scale), ready)

                    def prepare(_):
                        norm_act(act, o)
                        act.wait_ge(S["sp_arg"], 1)
                        o.run(act.activation(sp_y[:, 0:NB], sp_y[:, 0:NB], ACT.Exp, scale=-1.0), S["sp_exp"])
                        act.wait_ge(S["lam_arg"], 2)
                        o.run(act.activation(lam_e, lam_sum, ACT.Exp), S["lam_exp"])
                        act.wait_ge(S["small_loaded"], 32)
                        o.run(act.activation(expA, par_of("d_A_log"), ACT.Exp), S["lam_exp"])

                    def proj(j):
                        u, f = divmod(j, 2)
                        if f == 0:
                            return
                        act.wait_ge(S["unit_done"], u + 1)
                        bank = psum[u % 2][:, :].rearrange("p (b t) -> p b t", b=2)
                        ready = S["proj_evac"]
                        if u < U_C + 2:
                            copy(cpad[:, 2 * u:2 * u + 2, 3:3 + SEQ], bank, ready)
                        elif u < U_D:
                            copy(cgate[:, 2 * (u - 2):2 * (u - 2) + 2, :], bank, ready)
                        elif u < U_Z:
                            b = 2 * (u - U_D)
                            copy(dpad[:, b:b + 2, 3:3 + SEQ], bank, ready)
                        elif u < U_A:
                            c = UC * (u - U_Z)
                            copy(zt[:, :, c:c + UC], bank, ready)
                        elif u < U_GATE:
                            if u == U_A:
                                act.wait_ge(S["c_out_ready"], 1)
                            b, r = divmod(u - U_A, 6)
                            if r < 4:
                                dst = ((aq, ak), (bq, bk))[b][r // 2][:, 2 * (r % 2):2 * (r % 2) + 2, :]
                            else:
                                dst = (av, bv)[b][:, :, UC * (r - 4):UC * (r - 3)]
                            copy(dst, bank, ready)
                        else:
                            for f in range(2):
                                b = 2 * (u - U_GATE) + f
                                ins = act.activation(gates[:, b, :], bank[:, f, :], ACT.Tanh,
                                                     bias=half_b[:, b:b + 1], scale=0.5)
                                o.run(ins, ready if f else None)
                        if u == U_D - 1:
                            act.wait_ge(S["c_gelu_arg"], 1)
                            o.run(act.activation(c_g, c_g, ACT.Tanh, scale=math.sqrt(2 / math.pi)), S["c_gelu_tanh"])
                        if u in (U_D + 2, U_D + 4):
                            d_tanh((u - U_D) // 2 - 1)

                    def d_tanh(g):
                        act.wait_ge(S["d_conv_ready"], g + 1)
                        o.run(act.activation(dth[:, g, :], dcv[:, 4 * g:4 * g + 4, :].rearrange("p b t -> p (b t)"),
                                             ACT.Tanh, scale=0.5), S["d_tanh_ready"])

                    def c_gates(_):
                        for g, (dst, bias) in enumerate(((c_r, half_ba), (c_i, half_bx))):
                            act.wait_ge(S["c_gates_psum"], g + 1)
                            for m in range(NB):
                                o.run(act.activation(dst[:, m, :],
                                                     psum[2 + 2 * g + m // 2][:, (m % 2) * SEQ:(m % 2 + 1) * SEQ],
                                                     ACT.Tanh, bias=bias[:, m:m + 1], scale=0.5), S["c_tanh"])
                        o.settle()
                        for m in range(NB):
                            o.run(act.activation(c_a[:, m, :], c_r[:, m, :], ACT.Exp,
                                                 bias=nlru[:, m:m + 1], scale=nlru[:, m:m + 1]), S["c_a_t"])
                            o.run(act.activation(c_t[:, m, :], c_r[:, m, :], ACT.Tanh,
                                                 bias=lru[:, m:m + 1], scale=lru[:, m:m + 1]), S["c_a_t"])
                        act.wait_ge(S["c_coef"], 1)
                        o.run(act.activation(c_t, c_t, ACT.Sqrt, scale=0.5), S["c_sqrt"])

                    def ba_act(_):
                        act.wait_ge(S["ba_cols"], 1)
                        b3 = ba.rearrange("p (t c) -> p t c", t=TT)
                        o.run(act.activation(beta.rearrange("p (t c) -> p t c", t=TT), b3[:, :, 0:HEADS],
                                             ACT.Tanh, scale=0.5), S["ba_act"])
                        act.wait_ge(S["sp_arg"], 2)
                        o.run(act.activation(sp_y, sp_y, ACT.Exp, scale=-1.0), S["sp_exp"])

                    def d_tok(part):
                        if part == 0:
                            d_tanh(2)
                        for n in ((0, 1, 2, 3), (4, 5))[part]:
                            g, t = divmod(n, 2)
                            act.wait_ge(S["d_tok_psum"], n + 1)
                            act.wait_ge(S["d_silu_ready"], 3)
                            copy((qtok, ktok, vtok)[g][:, t], hb(psum[3 + n % 5]), S["d_tok_ready"],
                                 scale=0.5 if g == 2 else 1.0)

                    def d_back(_):
                        for n in range(4):
                            g, t = divmod(n, 2)
                            act.wait_ge(S["d_back_psum"], n + 1)
                            act.wait_ge(S["d_tok_psum"], 6)
                            copy((dQ, dK)[g][:, :, t * P:(t + 1) * P], hb(psum[2 + n]), S["d_T_ready"])

                    def d_cum(_):
                        act.wait_ge(S["d_args_ready"], 4)
                        o.run(act.activation(dexp[:, :, :, :], dexp[:, :, :, :], ACT.Exp), S["d_exp_ready"])
                        o.run(act.activation(dfac, darg, ACT.Exp), S["d_exp_ready"])

                    def inv_p(s):
                        for t in range(TT):
                            act.wait_ge(S["inv_p_psum"], 2 * s + t + 1)
                            copy(dP[:, t], hb(psum[2 + t]), S["inv_p_ready"])

                    def d_v0(_):
                        act.wait_ge(S["v0_psum"], 1)
                        act.wait_ge(S["inv_x_psum"], 2 * LEVELS)
                        copy(dP[:, 0], hb(psum[2]), S["v0_ready"])

                    def d_s(_):
                        act.wait_ge(S["s_psum"], 1)
                        copy(dS, hb(psum[3]), S["s_ready"])

                    def d_v1(_):
                        act.wait_ge(S["v1_psum"], 1)
                        copy(dP[:, 1], hb(psum[3]), S["v1_ready"])

                    def d_o(_):
                        act.wait_ge(S["proj_evac"], U_A)
                        act.wait_ge(S["d_u_ready"], 4)
                        act.wait_ge(S["xy_ready"], 2 * LEVELS + 2)
                        o.run(act.activation(dusel[:, :, :, :].rearrange("p t h d -> p (t h d)"),
                                             zt[:, :, :].rearrange("p t d -> p (t d)"), ACT.Tanh, scale=0.5),
                              S["z_tanh"])

                    def from_psum(n, banks, psum_ready):
                        for t in range(TT):
                            act.wait_ge(psum_ready[0], psum_ready[1] + t + 1)
                            copy(oT[:, n, :, t * P:(t + 1) * P], hb(psum[banks[t]]),
                                 {0: S["oA_ready"], 1: S["oB_ready"], 3: S["oD_ready"]}[n])

                    def at_s(i):
                        if i < 4 * HEADS:
                            kw = (i % 2 + 1) * P
                            act.wait_ge(S["at_max_ready"], i + 1)
                            for c in range(2 if i < 8 else 1):
                                o.run(act.activation(sm[:, i % 2, c, 0:kw], sm[:, i % 2, c, 0:kw], ACT.Exp,
                                                     bias=nmx[:, c:c + 1], accum_out=sums[:, c:c + 1]),
                                      S["at_exp_ready"])
                        if i >= 1:
                            kw = ((i - 1) % 2 + 1) * P
                            act.wait_ge(S["at_t_psum"], i)
                            if i >= 3:
                                act.wait_ge(S["at_o_psum"], i - 2)
                            copy(wT[:, (i - 1) % 2, 0:kw], psum[7][:, 0:kw], S["at_t_ready"])

                    def at_oT(b):
                        from_psum(b, (6, 7), (S["at_oT_psum"], 2 * b))

                    def d_oT(_):
                        from_psum(3, (3, 4), (S["d_oT_psum"], 0))

                    steps = {"norm": prepare, "proj": proj, "c_gates": c_gates, "ba": ba_act, "d_tok": d_tok,
                             "d_back": d_back, "d_cum": d_cum, "inv_p": inv_p, "d_v0": d_v0, "d_s": d_s,
                             "d_v1": d_v1, "d_o": d_o, "at_s": at_s, "at_oT": at_oT, "d_oT": d_oT}
                    for what, i in SCHED:
                        if what in steps:
                            steps[what](i)

                @block.gpsimd
                def _(pool):
                    o = Order(pool, S["pool_own"])

                    def select_level(s):
                        if s == 0:
                            pool.wait_ge(S["d_u_ready"], 4)
                        else:
                            pool.wait_ge(S["inv_p_psum"], 2 * s)
                        mask = con[:, C_LEVEL + s * P:C_LEVEL + (s + 1) * P]
                        o.run(pool.tensor_tensor(
                            dusel[:, :, :, :].rearrange("p t h d -> p (t h) d"),
                            dU.rearrange("p t h d -> p (t h) d"),
                            mask.unsqueeze(1).to_broadcast([P, TT * HEADS, P]), ALU.mult), S["dusel_ready"])

                    def d_tok(part):
                        if part == 1:
                            pool.wait_ge(S["d_ss_ready"], 1)
                            pool_rsqrt(pool, o, 16, 0.25, 1e-6, S["d_rs_ready"])

                    def d_o(_):
                        pool.wait_ge(S["o_ss_ready"], 1)
                        pool_rsqrt(pool, o, 8, 1.0 / P, 1e-6, S["o_rs_ready"])

                    def at_oT(b):
                        if b == 0:
                            pool.wait_ge(S["a_ss_ready"], 1)
                            pool_rsqrt(pool, o, 8, 1.0 / P, 1e-5, S["a_rs_ready"])

                    steps = {"norm": lambda _: norm_pool(pool, o), "d_tok": d_tok, "inv_p": select_level,
                             "d_o": d_o, "at_oT": at_oT}
                    for what, i in SCHED:
                        if what in steps:
                            steps[what](i)

                @block.vector
                def _(dve):
                    o = Order(dve, S["dve_own"])
                    TMPD = dtmp[:, :, :, :]

                    def prepare(_):
                        dve.wait_ge(S["small_loaded"], 32)
                        o.run(dve.tensor_scalar(half_b, par_of("b_gate"), 0.5, None, ALU.mult))
                        o.run(dve.tensor_scalar(half_ba, par_of("c_b_a"), 0.5, None, ALU.mult))
                        o.run(dve.tensor_scalar(half_bx, par_of("c_b_x"), 0.5, None, ALU.mult))
                        o.run(dve.memset(dpad[:, :, 0:3], 0.0))
                        o.run(dve.memset(cpad[:, :, 0:3], 0.0))
                        norm_dve(dve, o, par_of("norm_mix"))
                        o.settle()
                        o.step(dve.tensor_scalar(sp_z[:, 0:NB], par_of("c_lambda"), -1.0, None, ALU.mult))
                        softplus_dve(dve, o, NB, S["sp_arg"], S["sp_exp"], 1)
                        o.run(dve.tensor_scalar(lru, sp_p[:, 0:NB], LRU_C / 2, None, ALU.mult))
                        o.run(dve.tensor_scalar(nlru, sp_p[:, 0:NB], -LRU_C / 2, None, ALU.mult))
                        lam4 = par_of("lam").rearrange("p (a b c) -> p a b c", a=2, b=2)
                        o.step(dve.tensor_tensor(lam_prod.rearrange("p (a c) -> p a c", a=2), lam4[:, :, 0, :],
                                                 lam4[:, :, 1, :], ALU.mult))
                        for c in range(2):
                            o.run(dve.tensor_reduce(lam_sum[:, c:c + 1], lam_prod[:, 64 * c:64 * c + 64], AX, ALU.add),
                                  S["lam_arg"])
                        dve.wait_ge(S["lam_exp"], 2)
                        o.step(dve.tensor_tensor(lam_neg, lam_e[:, 1:2], lam_e[:, 0:1], ALU.subtract))
                        o.step(dve.tensor_tensor(lam_neg, lam_neg, par_of("lam_init"), ALU.subtract))
                        o.run(dve.tensor_scalar(a_scale, par_of("a_subln"), par_of("out_scale"), None, ALU.mult))
                        o.settle()

                    def conv(dst, src, w, n0, n1, bias, ready):
                        for tap in range(TAPS):
                            for b in range(n0, n1):
                                col = w[:, b * TAPS + tap:b * TAPS + tap + 1]
                                if tap == 0 and bias is None:
                                    ins = dve.tensor_scalar(dst[:, b, :], src[:, b, 0:SEQ], col, None, ALU.mult)
                                elif tap == 0:
                                    ins = dve.tensor_scalar(dst[:, b, :], src[:, b, 0:SEQ], col, bias[:, b:b + 1],
                                                            ALU.mult, ALU.add)
                                else:
                                    ins = dve.scalar_tensor_tensor(dst[:, b, :], src[:, b, tap:tap + SEQ], col,
                                                                   dst[:, b, :], ALU.mult, ALU.add)
                                o.run(ins, ready if tap == TAPS - 1 and b == n1 - 1 else None)
                            if tap < TAPS - 1:
                                o.settle()

                    def proj(j):
                        u, f = divmod(j, 2)
                        if f == 0:
                            return
                        if u == 1:
                            dve.wait_ge(S["proj_evac"], 2)
                            conv(c_xc, cpad, par_of("c_conv_w"), 0, NB, par_of("c_conv_b"), S["c_conv_ready"])
                        if u == 3:
                            dve.wait_ge(S["proj_evac"], 4)
                            o.step(dve.tensor_tensor(c_g, cgate, cgate, ALU.mult))
                            o.step(dve.tensor_scalar(c_g, c_g, 0.044715, 1.0, ALU.mult, ALU.add))
                            o.step(dve.tensor_tensor(c_g, c_g, cgate, ALU.mult), S["c_gelu_arg"])
                        if u in (U_D + 1, U_D + 3, U_D + 5):
                            g = (u - U_D) // 2
                            dve.wait_ge(S["proj_evac"], u + 1)
                            o.settle()
                            conv(dcv, dpad, par_of("d_conv_w"), 4 * g, 4 * g + 4, None, S["d_conv_ready"])
                            if g:
                                silu(g - 1)
                        if u == U_D:
                            dve.wait_ge(S["c_gelu_tanh"], 1)
                            o.step(dve.scalar_tensor_tensor(c_g, c_g, 1.0, cgate, ALU.add, ALU.mult))

                    def silu(g):
                        dve.wait_ge(S["d_tanh_ready"], g + 1)
                        o.settle()
                        v = dcv[:, 4 * g:4 * g + 4, :].rearrange("p b t -> p (b t)")
                        o.step(dve.scalar_tensor_tensor(v, dth[:, g, :], 1.0, v, ALU.add, ALU.mult),
                               S["d_silu_ready"])

                    def c_gates(_):
                        dve.wait_ge(S["c_tanh"], 8)
                        o.run(dve.scalar_tensor_tensor(c_i, c_i, 1.0, c_xc, ALU.add, ALU.mult))
                        dve.wait_ge(S["c_a_t"], 8)
                        o.step(dve.tensor_scalar(c_r, c_t, 1.0, None, ALU.add))
                        o.step(dve.reciprocal(c_r, c_r))
                        o.step(dve.scalar_tensor_tensor(c_t, c_t, 1.0e-30, c_r, ALU.max, ALU.mult), S["c_coef"])
                        dve.wait_ge(S["c_sqrt"], 1)
                        o.step(dve.tensor_tensor(c_i, c_i, c_t, ALU.mult))
                        for m in range(NB):
                            o.run(dve.tensor_tensor_scan(c_r[:, m, :], c_a[:, m, :], c_i[:, m, :], 0.0,
                                                         ALU.mult, ALU.add))
                        o.settle()
                        o.run(dve.scalar_tensor_tensor(oT[:, 2, :, :], c_r, 0.5, c_g, ALU.mult, ALU.mult),
                              S["c_out_ready"])

                    def ba_dve(_):
                        dve.wait_ge(S["ba_psum"], 1)
                        o.step(dve.tensor_copy(ba, psum[2][:, 0:16]), S["ba_cols"])
                        b3 = ba.rearrange("p (t c) -> p t c", t=TT)
                        z3 = sp_z.rearrange("p (t c) -> p t c", t=TT)
                        bias = par_of("d_dt_bias").unsqueeze(1).to_broadcast([P, TT, HEADS])
                        o.step(dve.tensor_tensor(z3, b3[:, :, HEADS:], bias, ALU.add))
                        softplus_dve(dve, o, 8, S["sp_arg"], S["sp_exp"], 2)
                        dve.wait_ge(S["ba_act"], 1)
                        o.step(dve.tensor_scalar(beta, beta, 0.5, 0.5, ALU.mult, ALU.add))
                        o.run(dve.scalar_tensor_tensor(
                            dg.rearrange("p (t c) -> p t c", t=TT), sp_p.rearrange("p (t c) -> p t c", t=TT), -1.0,
                            expA.unsqueeze(1).to_broadcast([P, TT, HEADS]), ALU.mult, ALU.mult), S["dg_ready"])

                    def d_tok(part):
                        if part == 0:
                            silu(2)
                            for n in range(4):
                                g, t = divmod(n, 2)
                                dve.wait_ge(S["d_tok_ready"], n + 1)
                                src = (qtok, ktok)[g][:, t]
                                o.step(dve.tensor_tensor(TMPD[:, t], src, src, ALU.mult))
                                o.step(dve.tensor_reduce(ss[:, 4 * n:4 * n + 4], TMPD[:, t], AX, ALU.add),
                                       S["d_ss_ready"] if n == 3 else None)
                            return
                        dve.wait_ge(S["d_rs_ready"], 1)
                        o.run(dve.tensor_scalar(rtmp[:, 0:8], rstd[:, 0:8], 0.5 * P ** -0.5, None, ALU.mult))
                        o.step(dve.tensor_scalar(rtmp[:, 8:16], rstd[:, 8:16], 0.5, None, ALU.mult))
                        for n in range(4):
                            g, t = divmod(n, 2)
                            v = (qtok, ktok)[g][:, t]
                            o.run(dve.tensor_tensor(v, v, bc_row(rtmp[:, 4 * n:4 * n + 4], HEADS), ALU.mult),
                                  S["d_unit_ready"])

                    def d_cum(_):
                        dve.wait_ge(S["d_cum_psum"], 1)
                        o.step(dve.tensor_copy(gcum, psum[6][:, 0:8]))
                        for t in range(TT):
                            for hd in range(HEADS):
                                c = 4 * t + hd
                                o.run(dve.scalar_tensor_tensor(dexp[:, t, hd, :], psum[2 + t][:, hd * P:(hd + 1) * P],
                                                               gcum[:, c:c + 1], neg_t, ALU.subtract, ALU.add),
                                      S["d_args_ready"] if hd == HEADS - 1 else None)
                        o.run(dve.tensor_copy(darg[:, 0:8], gcum))
                        for t in range(TT):
                            o.run(dve.tensor_tensor(darg[:, 8 + 4 * t:12 + 4 * t], hb(psum[2 + t])[:, :, P - 1],
                                                    gcum[:, 4 * t:4 * t + 4], ALU.subtract), S["d_args_ready"])
                        dve.wait_ge(S["d_exp_ready"], 2)
                        for t in range(TT):
                            o.run(dve.tensor_tensor(dU[:, t], dexp[:, t], hb(psum[4 + t]), ALU.mult), S["d_ub_ready"])
                        o.settle()
                        dve.wait_ge(S["d_tok_ready"], 6)
                        dve.wait_ge(S["d_back_psum"], 4)
                        o.run(dve.tensor_tensor(dR, vtok[:, 0], bc_row(beta[:, 0:4], HEADS), ALU.mult), S["r0_ready"])
                        o.run(dve.tensor_tensor(ktok[:, 0], ktok[:, 0], bc_row(dfac[:, 8:12], HEADS), ALU.mult))
                        for t in range(TT):
                            eye = ident.unsqueeze(1).to_broadcast([P, HEADS, P])
                            o.run(dve.tensor_copy(dX[:, t], eye))
                            o.run(dve.tensor_copy(dY[:, t], eye), S["xy_ready"])

                    def d_kk(_):
                        o.settle()
                        for t in range(TT):
                            dve.wait_ge(S["d_kk_psum"], t + 1)
                            o.run(dve.tensor_tensor(dU[:, t], dU[:, t], hb(psum[2 + t]), ALU.mult), S["d_u_ready"])
                        for t in range(TT):
                            dve.wait_ge(S["d_kk_psum"], 2 + t + 1)
                            o.run(dve.tensor_tensor(dexp[:, t], dexp[:, t], hb(psum[6 + t]), ALU.mult), S["d_u_ready"])

                    def inv_x(s):
                        o.settle()
                        for t in range(TT):
                            dve.wait_ge(S["inv_x_psum"], 2 * s + t + 1)
                            if s < LEVELS - 1:
                                o.run(dve.tensor_tensor(dX[:, t], dX[:, t], hb(psum[2 + t]), ALU.subtract))
                                o.settle()
                            o.run(dve.tensor_tensor(dY[:, t], dY[:, t], hb(psum[4 + t]), ALU.subtract), S["xy_ready"])

                    def d_ks(_):
                        o.settle()
                        dve.wait_ge(S["ks_psum"], 1)
                        dve.wait_ge(S["v0_psum"], 1)
                        o.step(dve.tensor_tensor(TMPD[:, 0], hb(psum[2]), bc_row(dfac[:, 4:8], HEADS), ALU.mult))
                        o.step(dve.tensor_tensor(TMPD[:, 0], vtok[:, 1], TMPD[:, 0], ALU.subtract))
                        o.step(dve.tensor_tensor(dR, TMPD[:, 0], bc_row(beta[:, 4:8], HEADS), ALU.mult), S["r1_ready"])
                        o.step(dve.tensor_tensor(TMPD[:, 1], hb(psum[4]), bc_row(dfac[:, 4:8], HEADS), ALU.mult),
                               S["ks_taken"])

                    def d_o(_):
                        dve.wait_ge(S["o_psum"], 1)
                        o.run(dve.tensor_copy(TMPD[:, 0], hb(psum[2])))
                        o.step(dve.tensor_tensor(TMPD[:, 1], hb(psum[5]), TMPD[:, 1], ALU.add))
                        sq = dX
                        o.step(dve.tensor_tensor(sq, TMPD, TMPD, ALU.mult))
                        o.step(dve.tensor_reduce(ss[:, 0:8], sq.rearrange("p t h d -> p (t h) d"), AX, ALU.add),
                               S["o_ss_ready"])
                        dve.wait_ge(S["z_tanh"], 1)
                        z2 = zt[:, :, :].rearrange("p t d -> p (t d)")
                        o.run(dve.scalar_tensor_tensor(z2, dusel[:, :, :, :].rearrange("p t h d -> p (t h d)"), 1.0,
                                                       z2, ALU.add, ALU.mult))
                        dve.wait_ge(S["o_rs_ready"], 1)
                        o.step(dve.tensor_scalar(rtmp[:, 0:8], rstd[:, 0:8], 0.5, None, ALU.mult))
                        v = TMPD.rearrange("p t h d -> p (t h) d")
                        o.step(dve.tensor_tensor(v, v, bc_row(rtmp[:, 0:8], 8), ALU.mult))
                        o.step(dve.tensor_tensor(v, v, par_of("d_norm").unsqueeze(1).to_broadcast([P, 8, P]), ALU.mult))
                        o.step(dve.tensor_tensor(v, v, z2.rearrange("p (n d) -> p n d", n=8), ALU.mult),
                               S["d_out_ready"])

                    def at_s(i):
                        if i >= 4 * HEADS:
                            return
                        qt, b = i % 2, i // 8
                        kw, nc_ = (qt + 1) * P, 2 - b
                        o.settle()
                        dve.wait_ge(S["at_s_psum"], i + 1)
                        if i >= 2:
                            dve.wait_ge(S["at_t_psum"], i - 1)
                        mask = con[:, C_CAUSAL + SEQ - kw:C_CAUSAL + SEQ]
                        s = sm[:, i % 2, 0:nc_, 0:kw]
                        src = banks_all[:, 5 + b:7, 0:kw]
                        scale = (64 if b == 0 else P) ** -0.5
                        o.step(dve.scalar_tensor_tensor(s, src, scale, mask.unsqueeze(1).to_broadcast([P, nc_, kw]),
                                                        ALU.mult, ALU.add), S["at_s_taken"])
                        o.step(dve.tensor_reduce(mx[:, 0:nc_], s, AX, ALU.max))
                        o.step(dve.tensor_scalar(nmx[:, 0:nc_], mx[:, 0:nc_], -1.0, None, ALU.mult), S["at_max_ready"])
                        dve.wait_ge(S["at_exp_ready"], 2 * i + 2 if b == 0 else 16 + i - 8 + 1)
                        if b == 0:
                            o.step(dve.reciprocal(rec[:, 0:2], sums[:, 0:2]))
                            o.run(dve.tensor_scalar(rec2[:, 0:1], rec[:, 1:2], lam_neg, None, ALU.mult))
                            o.step(dve.tensor_scalar(s[:, 0, :], s[:, 0, :], rec[:, 0:1], None, ALU.mult))
                            o.step(dve.scalar_tensor_tensor(s[:, 0, :], s[:, 1, :], rec2[:, 0:1], s[:, 0, :],
                                                            ALU.mult, ALU.add), S["at_w_ready"])
                        else:
                            o.step(dve.reciprocal(rec[:, 2 + qt:3 + qt], sums[:, 0:1]), S["at_w_ready"])

                    def at_o(i):
                        b, hd, qt = i // 8, (i % 8) // 2, i % 2
                        dve.wait_ge(S["at_o_psum"], i + 1)
                        if b == 1 and i == 8:
                            dve.wait_ge(S["at_oT_psum"], 2)
                        if b == 0:
                            o.run(dve.tensor_copy(ot[:, qt, hd, :], psum[7][:, 0:P]), S["at_o_taken"])
                        else:
                            o.settle()
                            o.run(dve.tensor_scalar(ot[:, qt, hd, :], psum[7][:, 0:P], rec[:, 2 + qt:3 + qt], None,
                                                    ALU.mult), S["at_o_taken"])

                    def at_oT(b):
                        if b == 0:
                            o.settle()
                            dve.wait_ge(S["d_oT_psum"], TT)
                            sq = TMPD
                            o.step(dve.tensor_tensor(sq, ot[:, :, :, :], ot[:, :, :, :], ALU.mult))
                            o.step(dve.tensor_reduce(ss[:, 0:8], sq.rearrange("p t h d -> p (t h) d"), AX, ALU.add),
                                   S["a_ss_ready"])
                            dve.wait_ge(S["a_rs_ready"], 1)
                            v = ot[:, :, :, :].rearrange("p t h d -> p (t h) d")
                            o.step(dve.tensor_tensor(v, v, bc_row(rstd[:, 0:8], 8), ALU.mult))
                            o.run(dve.tensor_tensor(v, v, a_scale.unsqueeze(1).to_broadcast([P, 8, P]), ALU.mult),
                                  S["a_out_ready"])
                        else:
                            o.settle()
                            dve.sem_inc(S["a_out_ready"], 1)

                    def branch(j):
                        n, q = BRANCH_ORDER[j // 4], j % 4
                        if j % 2 == 0:
                            dve.wait_ge(S["br_psum"], j // 2 + 1)
                        else:
                            dve.wait_ge(S["unit_done"], U_BR + j // 2 + 1)
                        src = psum[j % 2][:, :].rearrange("p (b t) -> p b t", b=2)
                        g = gates[:, KD * n + 2 * q:KD * n + 2 * q + 2, :]
                        a = acc[:, 2 * q:2 * q + 2, :]
                        if j == 0:
                            o.settle()
                            dve.wait_ge(S["proj_evac"], U_BR)
                            dve.wait_ge(S["at_s_psum"], 16)
                        if j < 4:
                            o.run(dve.scalar_tensor_tensor(a, g, 1.0, src, ALU.add, ALU.mult), S["br_taken"])
                        else:
                            o.settle()
                            o.run(dve.scalar_tensor_tensor(acc_tmp, g, 1.0, src, ALU.add, ALU.mult), S["br_taken"])
                            o.settle()
                            o.run(dve.tensor_tensor(a, a, acc_tmp, ALU.add),
                                  S["acc_ready"] if j == 15 else None)

                    def project_out(j):
                        dve.wait_ge(S["unit_done"], U_OUT + j + 1)
                        v = h[:, :, j * UC:(j + 1) * UC]
                        o.run(dve.scalar_tensor_tensor(v, psum[j % 2][:, :].rearrange("p (t c) -> p t c", t=TT), 0.5,
                                                       v, ALU.mult, ALU.add), S["f_out_taken"])

                    steps = {"norm": prepare, "proj": proj, "c_gates": c_gates, "ba": ba_dve, "d_tok": d_tok,
                             "d_cum": d_cum, "d_kk": d_kk, "inv_x": inv_x, "d_ks": d_ks, "d_o": d_o, "at_s": at_s,
                             "at_o": at_o, "at_oT": at_oT, "branch": branch, "out": project_out}
                    for what, i in SCHED:
                        if what in steps:
                            steps[what](i)
                    o.settle()

        AHEAD = 2

        def over_chunks(eng, n, step):
            with eng.Fori(0, n // 2) as j:
                step(2 * j, 0, j)
                step(2 * j + 1, 1, j)
            if n % 2:
                step(n - 1, 0, n // 2)

        def load_chunk(sp, source, base, base_half):
            def step(c, half, j):
                sp.wait_ge(S["h13_psum"], base + c + 1)
                for i in range(2):
                    sp.dma_start(ring[3 * half + i][:, :], source(3 * c + i)).then_inc(slot_loaded[3 * half + i], 16)
                sp.wait_ge(S["w2_used"], base + c + 1)
                sp.dma_start(ring[3 * half + 2][:, :], source(3 * c + 2)).then_inc(slot_loaded[3 * half + 2], 16)
            return step

        def pe_chunks(pe, n, base, base_half, xT, width, product):
            def up(c, half, j):
                pe.wait_ge(S["f_hT_ready"], base + c + 1)
                for i in range(2):
                    pe.wait_ge(slot_loaded[3 * half + i], (base_half + j + 1) * 16)
                    w = ring[3 * half + i][:, :].rearrange("p (k c) -> p k c", k=KD)
                    for f in range(2):
                        for k in range(KD):
                            last = pe.matmul(psum[2 * half + i][:, f * width:(f + 1) * width],
                                             w[:, k, f * P:(f + 1) * P], xT[:, k, :], start=(k == 0),
                                             stop=(k == KD - 1))
                last.then_inc(S["h13_psum"], 1)

            def down(c, half, j, first=False, final=False):
                pe.wait_ge(S["f_hT_ready"], base + c + AHEAD + 1)
                pe.wait_ge(slot_loaded[3 * half + 2], (base_half + j + 1) * 16)
                w = ring[3 * half + 2][:, :].rearrange("p (f c) -> p f c", f=2)
                for f in range(2):
                    last = product(hT[half][:, f * width:(f + 1) * width], w[:, f, :], first and f == 0,
                                   final and f == 1)
                last.then_inc(S["w2_used"], 1)

            up(0, 0, 0)
            up(1, 1, 0)
            down(0, 0, 0, first=True)
            with pe.Fori(0, (n - 2) // 2) as j:
                up(2 * j + 2, 0, j + 1)
                down(2 * j + 1, 1, j)
                up(2 * j + 3, 1, j + 1)
                down(2 * j + 2, 0, j + 1)
            if n % 2:
                up(n - 1, 0, n // 2)
                down(n - 2, 1, n // 2 - 1)
                down(n - 1, 0, n // 2, final=True)
            else:
                down(n - 1, 1, n // 2 - 1, final=True)

        def act_chunk(act, base, width):
            def step(c, half, j):
                act.wait_ge(S["h13_psum"], base + c + AHEAD + 1)
                act.wait_ge(S["f_hT_ready"], base + c + 1)
                act.activation(fth[half][:, 0:2 * width], psum[2 * half][:, 0:2 * width], ACT.Tanh,
                               scale=0.5).then_inc(S["f_tanh"], 1)
            return step

        def dve_chunk(dve, base, width):
            def step(c, half, j):
                n = 2 * width
                dve.wait_ge(S["f_tanh"], base + c + 1)
                dve.scalar_tensor_tensor(fs[half][:, 0:n], fth[half][:, 0:n], 1.0, psum[2 * half][:, 0:n],
                                         ALU.add, ALU.mult).then_inc(S["f_h_ready"], 1)
                dve.wait_ge(S["w2_used"], base + c + 1)
                dve.wait_ge(S["f_h_ready"], base + c + 1)
                dve.tensor_tensor(hT[half][:, 0:n], fs[half][:, 0:n], psum[2 * half + 1][:, 0:n],
                                  ALU.mult).then_inc(S["f_hT_ready"], 1)
            return step

        def dense_block():
            with nc.Block() as block:
                @block.sync
                def _(sp):
                    over_chunks(sp, DENSE_CHUNKS, load_chunk(
                        sp, lambda u: dense_units[bass.ds(u, 1), :, :].rearrange("l p c -> p (l c)"), 0, 0))
                    sp.wait_ge(S["w2_used"], DENSE_CHUNKS + AHEAD)

                @block.tensor
                def _(pe):
                    pe.sem_inc(S["h13_psum"], AHEAD)
                    pe.sem_inc(S["w2_used"], AHEAD)
                    norm_pe(pe)
                    pe.wait_ge(S["xT_ready"], 4)

                    def product(lhsT, w, first, final):
                        for t in range(TT):
                            for n in range(2):
                                last = pe.matmul(psum[4 + 2 * t + n][:, :], lhsT[:, t * P:(t + 1) * P],
                                                 w[:, n * 512:(n + 1) * 512], start=first, stop=final)
                        return last

                    pe_chunks(pe, DENSE_CHUNKS, 0, 0, xnT, SEQ, product)

                @block.scalar
                def _(act):
                    norm_act(act, Order(act, S["act_own"]))
                    over_chunks(act, DENSE_CHUNKS, act_chunk(act, 0, SEQ))

                @block.gpsimd
                def _(pool):
                    norm_pool(pool, Order(pool, S["pool_own"]))

                @block.vector
                def _(dve):
                    o = Order(dve, S["dve_own"])
                    dve.sem_inc(S["f_hT_ready"], AHEAD)
                    norm_dve(dve, o, par_of("norm_ffn"))
                    over_chunks(dve, DENSE_CHUNKS, dve_chunk(dve, 0, SEQ))
                    dve.wait_ge(S["w2_used"], DENSE_CHUNKS + AHEAD)
                    for t in range(TT):
                        for n in range(2):
                            v = h[:, t, n * 512:(n + 1) * 512]
                            o.run(dve.scalar_tensor_tensor(v, psum[4 + 2 * t + n][:, :], 0.5, v, ALU.mult, ALU.add))
                    o.settle()

        def moe_block():
            n_passes = PASSES
            with nc.Block() as block:
                @block.sync
                def _(sp):
                    sp.wait_ge(S["table_ready"], 1)
                    total = sp.value_load(table_i[0:1, PASSES:PASSES + 1], min_val=EXPERTS, max_val=PASSES)
                    with sp.Fori(0, n_passes) as p:
                        expert = sp.value_load(table_i[0:1, bass.ds(p, 1)], min_val=0, max_val=EXPERTS - 1)
                        with sp.If(p < total):
                            over_chunks(sp, MOE_CHUNKS, load_chunk(
                                sp, lambda u: moe_units[bass.ds(expert * (3 * MOE_CHUNKS) + u, 1), :, :]
                                .rearrange("l p c -> p (l c)"), p * MOE_CHUNKS, p * (MOE_CHUNKS // 2)))
                        with sp.Else():
                            sp.nop()

                @block.tensor
                def _(pe):
                    pe.sem_inc(S["h13_psum"], AHEAD)
                    pe.sem_inc(S["w2_used"], AHEAD)
                    norm_pe(pe)
                    pe.wait_ge(S["xT_ready"], 4)
                    r = par_of("router").rearrange("p (k e) -> p k e", k=KD)
                    for t in range(TT):
                        for k in range(KD):
                            last = pe.matmul(psum[0][:, 8 * t:8 * t + 8], xnT[:, k, t * P:(t + 1) * P], r[:, k, :],
                                             start=(k == 0), stop=(k == KD - 1))
                    last.then_inc(S["rt_psum"], 1)
                    pe.wait_ge(S["rt_member"], 1)
                    m = member.rearrange("p (t e) -> p t e", t=TT)
                    pe.matmul(psum[1][:, 0:8], trix, m[:, 0, :], start=True, stop=True)
                    pe.matmul(psum[1][:, 8:16], ones, m[:, 0, :], start=True, stop=False)
                    pe.matmul(psum[1][:, 8:16], trix, m[:, 1, :], start=False, stop=True)
                    pe.matmul(psum[1][:, 16:24], ones, m[:, 0, :], start=True, stop=False)
                    pe.matmul(psum[1][:, 16:24], ones, m[:, 1, :], start=False, stop=True).then_inc(S["rank_psum"], 1)
                    pe.wait_ge(S["table_ready"], 1)
                    total = pe.value_load(table_i[0:1, PASSES:PASSES + 1], min_val=EXPERTS, max_val=PASSES)
                    with pe.Fori(0, n_passes) as p:
                        with pe.If(p < total):
                            pe.wait_ge(S["sel_ready"], p + 1)
                            pe.wait_ge(S["scat_taken"], p * 4 + 4)
                            for k in range(KD):
                                for t in range(TT):
                                    last = pe.matmul(psum[6 + k // 4][:, (k % 4) * P:(k % 4 + 1) * P],
                                                     xs[:, t, k * P:(k + 1) * P], sel[:, t, :], start=(t == 0),
                                                     stop=(t == TT - 1))
                            last.then_inc(S["gather_psum"], 1)
                            for t in range(TT):
                                last = pe.transpose(psum[4][:, t * P:(t + 1) * P], selg[:, t, :], ident)
                            last.then_inc(S["selT_psum"], 1)
                            pe.wait_ge(S["gather_ready"], p * 2 + 2)
                            pe.wait_ge(S["selT_ready"], p + 1)

                            def product(lhsT, w, first, final):
                                for n in range(2):
                                    last = pe.matmul(psum[4 + n][:, :], lhsT, w[:, n * 512:(n + 1) * 512],
                                                     start=first, stop=final)
                                return last

                            pe_chunks(pe, MOE_CHUNKS, p * MOE_CHUNKS, p * (MOE_CHUNKS // 2), xsel, P, product)
                            pe.wait_ge(S["y_ready"], p * 2 + 2)
                            for t in range(TT):
                                if t == 1:
                                    pe.wait_ge(S["scat_taken"], p * 4 + 6)
                                for n in range(2):
                                    last = pe.matmul(psum[6 + n][:, :], selgT[:, t * P:(t + 1) * P],
                                                     yexp[:, n * 512:(n + 1) * 512], start=True, stop=True)
                                last.then_inc(S["scat_psum"], 1)
                        with pe.Else():
                            pe.nop()

                @block.scalar
                def _(act):
                    norm_act(act, Order(act, S["act_own"]))
                    act.wait_ge(S["rt_arg"], 1)
                    act.activation(em, dm, ACT.Exp).then_inc(S["rt_exp"], 1)
                    act.wait_ge(S["table_ready"], 1)
                    total = act.value_load(table_i[0:1, PASSES:PASSES + 1], min_val=EXPERTS, max_val=PASSES)
                    with act.Fori(0, n_passes) as p:
                        with act.If(p < total):
                            act.wait_ge(S["selT_psum"], p + 1)
                            act.activation(selgT, psum[4][:, 0:SEQ], ACT.Copy).then_inc(S["selT_ready"], 1)
                            over_chunks(act, MOE_CHUNKS, act_chunk(act, p * MOE_CHUNKS, P))
                            act.wait_ge(S["w2_used"], p * MOE_CHUNKS + MOE_CHUNKS + AHEAD)
                            for n in range(2):
                                act.activation(yexp[:, n * 512:(n + 1) * 512], psum[4 + n][:, :],
                                               ACT.Copy).then_inc(S["y_ready"], 1)
                        with act.Else():
                            act.nop()

                @block.gpsimd
                def _(pool):
                    norm_pool(pool, Order(pool, S["pool_own"]))

                @block.vector
                def _(dve):
                    o = Order(dve, S["dve_own"])
                    dve.sem_inc(S["f_hT_ready"], AHEAD)
                    dve.sem_inc(S["scat_taken"], 4)
                    norm_dve(dve, o, par_of("norm_ffn"))
                    o.settle()
                    eidx = con[:, C_EIDX:C_EIDX + EXPERTS]
                    erev = con[:, C_EREV:C_EREV + EXPERTS]

                    def te(c):
                        return c.rearrange("p (t e) -> p t e", t=TT)

                    def each_t(row):
                        return row.unsqueeze(1).to_broadcast([P, TT, EXPERTS])

                    def each_e(c):
                        return c.unsqueeze(2).to_broadcast([P, TT, EXPERTS])

                    def best(src, value, chosen):
                        o.step(dve.tensor_reduce(value, te(src), AX, ALU.max))
                        o.step(dve.tensor_tensor(te(eq), te(src), each_e(value), ALU.is_equal))
                        o.step(dve.tensor_tensor(te(eq), te(eq), each_t(erev), ALU.mult))
                        o.step(dve.tensor_reduce(fi, te(eq), AX, ALU.max))
                        o.step(dve.tensor_tensor(te(chosen), each_t(erev), each_e(fi), ALU.is_equal))

                    dve.wait_ge(S["rt_psum"], 1)
                    o.step(dve.tensor_copy(lg, psum[0][:, 0:16]))
                    best(lg, m0, one1)
                    o.step(dve.scalar_tensor_tensor(lg, one1, -3.0e38, lg, ALU.mult, ALU.add))
                    best(lg, m1, one2)
                    o.run(dve.tensor_tensor(member, one1, one2, ALU.add), S["rt_member"])
                    o.step(dve.tensor_tensor(dm, m1, m0, ALU.subtract), S["rt_arg"])
                    dve.wait_ge(S["rt_exp"], 1)
                    o.step(dve.tensor_scalar(p0, em, 1.0, None, ALU.add))
                    o.step(dve.reciprocal(p0, p0))
                    o.step(dve.tensor_tensor(p1, em, p0, ALU.mult))
                    o.step(dve.tensor_tensor(te(one1), te(one1), each_e(p0), ALU.mult))
                    o.step(dve.tensor_tensor(te(one2), te(one2), each_e(p1), ALU.mult))
                    o.step(dve.tensor_tensor(gsel, one1, one2, ALU.add))
                    dve.wait_ge(S["rank_psum"], 1)
                    o.step(dve.scalar_tensor_tensor(vslot, psum[1][:, 0:16], 1.0, member, ALU.add, ALU.mult))
                    o.step(dve.tensor_scalar(vslot, vslot, -1.0, None, ALU.add))
                    o.step(dve.tensor_scalar(over, psum[1][:, 16:24], float(P), None, ALU.is_gt))
                    o.step(dve.memset(onesE, 1.0))
                    o.step(dve.tensor_tensor_scan(incl, onesE, over, 0.0, ALU.mult, ALU.add))
                    o.step(dve.tensor_tensor(pos, incl, over, ALU.subtract))
                    so = slot_of.rearrange("p (t q) -> p t q", t=TT)
                    go = gate_of.rearrange("p (t q) -> p t q", t=TT)
                    o.run(dve.tensor_copy(so[:, :, 0:EXPERTS], te(vslot)))
                    o.run(dve.tensor_copy(go[:, :, 0:EXPERTS], te(gsel)))
                    o.run(dve.tensor_copy(table[:, 0:EXPERTS], eidx))
                    o.run(dve.tensor_scalar(table[:, PASSES:PASSES + 1], incl[:, EXPERTS - 1:EXPERTS], float(EXPERTS),
                                            None, ALU.add))
                    for q in range(OVERFLOWS):
                        sq = selq[:, q * EXPERTS:(q + 1) * EXPERTS]
                        o.step(dve.scalar_tensor_tensor(sq, pos, float(q), over, ALU.is_equal, ALU.mult))
                        o.step(dve.tensor_tensor(tmp8, sq, eidx, ALU.mult))
                        o.step(dve.tensor_reduce(table[:, EXPERTS + q:EXPERTS + q + 1], tmp8, AX, ALU.add))
                        for src, dst, shift in ((vslot, so, -float(P)), (gsel, go, 0.0)):
                            o.step(dve.tensor_tensor(te(pick), te(src), each_t(sq), ALU.mult))
                            o.step(dve.tensor_reduce(fi, te(pick), AX, ALU.add))
                            o.step(dve.tensor_scalar(dst[:, :, EXPERTS + q], fi, shift, None, ALU.add))
                    o.settle()
                    o.step(dve.tensor_copy(table_i[:, :], table), S["table_ready"])
                    total = dve.value_load(table_i[0:1, PASSES:PASSES + 1], min_val=EXPERTS, max_val=PASSES)
                    iota = con[:, C_IOTA:C_IOTA + P]
                    gain = par_of("norm_ffn")
                    with dve.Fori(0, n_passes) as p:
                        with dve.If(p < total):
                            for t in range(TT):
                                dve.tensor_scalar(sel[:, t, :], iota, so[:, t, bass.ds(p, 1)], None, ALU.is_equal)
                            for t in range(TT):
                                ins = dve.tensor_scalar(selg[:, t, :], iota, so[:, t, bass.ds(p, 1)],
                                                        go[:, t, bass.ds(p, 1)], ALU.is_equal, ALU.mult)
                            ins.then_inc(S["sel_ready"], 1)
                            dve.wait_ge(S["gather_psum"], p + 1)
                            for q in range(2):
                                dve.tensor_tensor(xsel[:, 4 * q:4 * q + 4, :],
                                                  psum[6 + q][:, :].rearrange("p (k s) -> p k s", k=4),
                                                  gain[:, 4 * q:4 * q + 4].unsqueeze(2).to_broadcast([P, 4, P]),
                                                  ALU.mult).then_inc(S["gather_ready"], 1)
                            over_chunks(dve, MOE_CHUNKS, dve_chunk(dve, p * MOE_CHUNKS, P))
                            dve.wait_ge(S["scat_taken"], p * 4 + 4)
                            for t in range(TT):
                                dve.wait_ge(S["scat_psum"], p * 2 + t + 1)
                                for n in range(2):
                                    v = h[:, t, n * 512:(n + 1) * 512]
                                    dve.scalar_tensor_tensor(v, psum[6 + n][:, :], 0.5, v, ALU.mult,
                                                             ALU.add).then_inc(S["scat_taken"], 1)
                        with dve.Else():
                            dve.nop()

        with nc.Fori(0, LAYERS) as layer:
            mixer_block(layer)
            clear_semaphores()
            with nc.If(layer < 1):
                dense_block()
            with nc.Else():
                moe_block()
            clear_semaphores()

        with nc.Block() as block:
            gain_row = ring[0][:, 0:DM]

            @block.sync
            def _(sp):
                sp.dma_start(gain_row, norm_final).then_inc(S["in_loaded"], 16)
                for t in range(TT):
                    sp.wait_ge(S["xs_ready"], t + 1)
                    sp.dma_start(out[t * P:(t + 1) * P, :], xs[:, t, :]).then_inc(S["out_stored"], 16)
                sp.wait_ge(S["out_stored"], TT * 16)

            @block.scalar
            def _(act):
                norm_act(act, Order(act, S["act_own"]))

            @block.gpsimd
            def _(pool):
                norm_pool(pool, Order(pool, S["pool_own"]))

            @block.vector
            def _(dve):
                dve.wait_ge(S["in_loaded"], 16)
                dve.wait_ge(S["rstd_ready"], 1)
                for t in range(TT):
                    dve.scalar_tensor_tensor(xs[:, t, :], h[:, t, :], rstd[:, t:t + 1], gain_row, ALU.mult,
                                             ALU.mult).then_inc(S["xs_ready"], 1)


def _constants(np):
    c = np.zeros((P, C_COLS), np.float32)
    j, i = np.arange(P)[:, None], np.arange(P)[None, :]
    c[:, C_IDENT:C_IDENT + P] = j == i
    c[:, C_ONES:C_ONES + P] = 1
    c[:, C_TRI:C_TRI + P] = j <= i
    c[:, C_TRIX:C_TRIX + P] = j < i
    c[:, C_CAUSAL + P:C_CAUSAL + 2 * P] = np.where(i <= j, 0, NEG)
    c[:, C_NEGT:C_NEGT + P] = np.where(j <= i, 0, NEG)
    for s in range(LEVELS):
        size = 1 << s
        c[:, C_LEVEL + s * P:C_LEVEL + (s + 1) * P] = (i // size % 2 == 1) & (j // size == i // size - 1)
    c[:, C_IOTA:C_IOTA + P] = i
    c[:, C_EIDX:C_EIDX + EXPERTS] = np.arange(EXPERTS)
    c[:, C_EREV:C_EREV + EXPERTS] = EXPERTS - np.arange(EXPERTS)
    c[:, C_HALF:] = -0.5
    return c


def _units(np, w, cols):
    rows, n = w.shape
    return w.reshape(rows // P, P, n // cols, cols).transpose(2, 1, 0, 3).reshape(n // cols, P, -1)


def _chunks(np, w1, w3, w2):
    a, b = _units(np, w1, CHUNK), _units(np, w3, CHUNK)
    c = w2.reshape(-1, CHUNK // P, P, DM).transpose(0, 2, 1, 3).reshape(a.shape[0], P, -1)
    return np.stack([a, b, c], 1).reshape(-1, P, UNIT)


def _layer_params(np, v, layer):
    parts = {}

    def channels(a, n):
        return a.reshape(n, P, -1).transpose(1, 0, 2).reshape(P, -1)

    def rows(a):
        return np.broadcast_to(a.reshape(1, -1), (P, a.size))

    lam_init = 0.8 - 0.6 * math.exp(-0.3 * layer)
    parts["norm_mix"] = channels(v["norm_mix"][layer], KD)
    parts["norm_ffn"] = channels(v["norm_ffn"][layer], KD)
    parts["c_conv_w"] = channels(v["c_conv_w"][layer].T, NB)
    parts["c_conv_b"] = channels(v["c_conv_b"][layer], NB)
    parts["c_b_a"] = channels(v["c_b_a"][layer].reshape(-1), NB)
    parts["c_b_x"] = channels(v["c_b_x"][layer].reshape(-1), NB)
    parts["c_lambda"] = channels(v["c_lambda"][layer], NB)
    parts["d_conv_w"] = channels(v["d_conv_w"][layer].T, 3 * NB)
    parts["b_gate"] = channels(v["b_gate"][layer].reshape(-1), BRANCHES * KD)
    parts["a_subln"] = rows(v["a_subln"][layer])
    parts["d_norm"] = rows(v["d_norm"][layer])
    parts["lam"] = rows(np.stack([v[n][layer] for n in ("lam_q1", "lam_k1", "lam_q2", "lam_k2")]))
    parts["d_A_log"] = rows(v["d_A_log"][layer])
    parts["d_dt_bias"] = rows(v["d_dt_bias"][layer])
    parts["w_ba"] = channels(v["w_in"][layer][:, 12 * MIX:], KD)
    parts["lam_init"] = np.full((P, 1), lam_init, np.float32)
    parts["out_scale"] = np.full((P, 1), 1.0 - lam_init, np.float32)
    moe = layer % 2 == 1
    parts["router"] = channels(v["router"][layer // 2], KD) if moe else np.zeros((P, KD * EXPERTS), np.float32)
    return np.concatenate([parts[n] for n, _ in PARTS], 1)


def kernel(**inputs):
    import numpy as np
    import concourse.bacc as bacc
    from concourse.bass_utils import run_bass_kernel_spmd

    v = {k: np.asarray(a) for k, a in inputs.items()}
    arrays = {"x": v["x"].reshape(SEQ, DM), "consts": _constants(np),
              "params": np.stack([_layer_params(np, v, layer) for layer in range(LAYERS)])}
    cd = np.zeros((LAYERS, P, 2, NB, P), np.float32)
    for g, name in enumerate(("c_w_a", "c_w_x")):
        w = v[name].reshape(LAYERS, NB, 2, 64, 64)
        for half in range(2):
            s = slice(64 * half, 64 * half + 64)
            cd[:, s, g, :, s] = w[:, :, half].transpose(0, 2, 1, 3)
    arrays["cdiag"] = cd.reshape(LAYERS, P, -1)
    mix = []
    for layer in range(LAYERS):
        w_in = _units(np, v["w_in"][layer][:, :12 * MIX], UC)
        per = MIX // UC
        order = [b * per + i for b in (6, 7, 8, 9, 10, 11, 0, 1, 2, 3, 4, 5) for i in range(per)]
        mix += [w_in[order], _units(np, v["w_gate"][layer].reshape(DM, -1), UC)]
        mix += [_units(np, v["w_branch"][layer][n], 2 * UC) for n in BRANCH_ORDER]
        mix += [_units(np, v["w_out"][layer], UC)]
    arrays["mix_units"] = np.concatenate(mix).reshape(LAYERS, MIX_UNITS, P, UNIT)
    arrays["dense_units"] = _chunks(np, v["ffn_w1"][0], v["ffn_w3"][0], v["ffn_w2"][0])
    arrays["moe_units"] = np.concatenate([_chunks(np, v["moe_w1"][0][e], v["moe_w3"][0][e], v["moe_w2"][0][e])
                                          for e in range(EXPERTS)])
    arrays["norm_final"] = np.ascontiguousarray(np.broadcast_to(v["norm_final"][None], (P, DM)))

    nc = bacc.Bacc("TRN2", target_bir_lowering=False, num_devices=1)
    aps = {n: nc.dram_tensor(n, a.shape, F32, kind="ExternalInput").ap() for n, a in arrays.items()}
    out = nc.dram_tensor("out", (SEQ, DM), F32, kind="ExternalOutput").ap()
    hybrid_trunk(nc, **aps, out=out)
    got = run_bass_kernel_spmd(nc, [arrays], core_ids=[0])
    return got.results[0]["out"].reshape(1, SEQ, DM)
```

```python
import math
from contextlib import ExitStack

import concourse.bass as bass
from concourse import mybir

F32 = mybir.dt.float32
F32R = mybir.dt.float32r
I32 = mybir.dt.int32
ALU = mybir.AluOpType
ACT = mybir.ActivationFunctionType
AX = mybir.AxisListType.X

P = 128
LAYERS, SEQ, DM = 2, 256, 1024
TT = SEQ // P
KD = DM // P
MIX = 512
NB = MIX // P
HEADS = 4
BRANCHES = 4
TAPS = 4
UC = 256
UNIT = KD * UC
MIX_SLOTS, FFN_SLOTS = 2, 6
NEG = -1.0e30
LRU_C = 8.0
EXPERTS, TOP_K = 8, 2
FFN, FFE = 2816, 3584
CHUNK = UC
DENSE_CHUNKS, MOE_CHUNKS = FFN // CHUNK, FFE // CHUNK
OVERFLOWS = (TOP_K * SEQ) // (P + 1)
PASSES = EXPERTS + OVERFLOWS

U_C, U_D, U_Z, U_A, U_B, U_GATE = 0, 4, 10, 12, 18, 24
U_BR = U_GATE + BRANCHES * DM // UC
U_OUT = U_BR + BRANCHES * 2
MIX_UNITS = U_OUT + DM // UC
BRANCH_ORDER = (2, 0, 1, 3)

LEVELS = 7

C_IDENT, C_ONES, C_TRI, C_TRIX, C_CAUSAL, C_NEGT = 0, 128, 256, 384, 512, 768
C_LEVEL = 896
C_IOTA = C_LEVEL + LEVELS * P
C_EIDX, C_EREV = C_IOTA + P, C_IOTA + P + EXPERTS
C_HALF = C_EREV + EXPERTS
C_COLS = C_HALF + 32

PARTS = [("norm_mix", KD), ("norm_ffn", KD), ("c_conv_w", NB * TAPS), ("c_conv_b", NB),
         ("c_b_a", NB), ("c_b_x", NB), ("c_lambda", NB), ("d_conv_w", 3 * NB * TAPS),
         ("b_gate", BRANCHES * KD), ("a_subln", P), ("d_norm", P), ("lam", 256),
         ("d_A_log", HEADS), ("d_dt_bias", HEADS), ("w_ba", KD * 8), ("lam_init", 1),
         ("out_scale", 1), ("router", KD * EXPERTS)]
PCOL, _at = {}, 0
for _name, _n in PARTS:
    PCOL[_name] = (_at, _n)
    _at += _n
P_COLS = _at


class Order:

    def __init__(self, eng, own):
        self.eng, self.own, self.count, self.open = eng, own, {}, []

    def run(self, ins, sem=None):
        sem = self.own if sem is None else sem
        ins.then_inc(sem, 1)
        self.count[sem.name] = self.count.get(sem.name, 0) + 1
        if sem not in self.open:
            self.open.append(sem)

    def settle(self):
        for sem in self.open:
            self.eng.wait_ge(sem, self.count[sem.name])
        self.open = []

    def step(self, ins, sem=None):
        self.run(ins, sem)
        self.settle()


def mixer_schedule():
    wait = ("-", 0)
    chain = [("d_tok", 0), ("d_tok", 1), wait, ("d_back", 0), ("d_cum", 0), wait, ("d_kk", 0)]
    for s in range(LEVELS):
        chain += [("inv_p", s), ("inv_x", s)]
    chain += [("d_v0", 0), ("d_s", 0), ("d_ks", 0), ("d_v1", 0), ("d_o", 0), wait, ("d_oT", 0)]
    attn = []
    for i in range(4 * HEADS + 1):
        attn += [("at_s", i)]
        if i:
            attn += [("at_o", i - 1)]
            if i % 8 == 0:
                attn += [("at_oT", i // 8 - 1)]
    at_half = {2 * U_Z: [("ba", 0)]}

    def put(half, *steps):
        for i, step in enumerate(steps):
            at_half.setdefault(half + i, []).append(step)

    put(4, *[("c_conv", tap) for tap in range(TAPS)])
    put(9, ("c_gates", 0), ("c_decay", 0), ("c_coef", 0), ("c_scan", 0))
    put(8, ("c_gelu_arg", 0), ("c_gelu_tanh", 0), ("c_gelu", 0))
    for g in range(3):
        put(2 * (U_D + 2 + 2 * g), *[("d_conv", TAPS * g + tap) for tap in range(TAPS)])
    for g in range(2):
        put(2 * (U_D + 4 + 2 * g), ("d_tanh", g), ("d_silu", g))
    out = [("norm", 0)]
    for half in range(2 * U_BR):
        out += at_half.get(half, [])
        if half >= 2 * U_A and chain:
            out.append(chain.pop(0))
        elif half >= 2 * U_GATE and attn:
            out.append(attn.pop(0))
        out.append(("proj", half))
    out += chain + [("stage", 0)]
    for j in range(BRANCHES * 4):
        out.append(("branch", j))
        if j in (0, 8):
            out.append(("stage", j // 4 + 1))
        if attn:
            out.append(attn.pop(0))
            assert j < 8
            if j == 7:
                out += attn
                attn = []
        if j == 7:
            out.append(("stage", 2))
    out += [("out", j) for j in range(DM // UC)]
    return out


def lo_by_pool(u):
    return 2 <= u < U_A or u > U_GATE


def lo_count(half):
    return sum(1 for i in range(half + 1) if lo_by_pool(i // 2) == lo_by_pool(half // 2))


def product3(pe, out, operands, n, hi_ready=None, lo_ready=None, count=None, lo_at=None):
    if lo_at is None:
        lo_at = count
    for i, (a, b) in enumerate(((0, 0), (0, 1), (1, 0))):
        for k in range(n):
            if k % (n // 2) == 0 and b == 0 and count is not None:
                pe.wait_ge(lo_ready if a else hi_ready, (lo_at if a else count) + k // (n // 2))
            lhsT, rhs = operands(a, b, k)
            last = pe.matmul(out, lhsT, rhs, start=(i == 0 and k == 0), stop=(i == 2 and k == n - 1))
    return last


def hybrid_trunk(nc, x, consts, params, cdiag, mix_units, dense_units, moe_units, norm_final, out):
    with ExitStack() as ctx:
        def sb(name, shape, dt=F32):
            return ctx.enter_context(nc.sbuf_tensor(name, shape, dt))

        sem_list = []

        def sem(name):
            s = ctx.enter_context(nc.semaphore(name))
            sem_list.append(s)
            return s

        con = sb("con", [P, C_COLS])
        par = sb("par", [P, P_COLS])
        h = sb("h", [P, TT, DM])
        raw = [sb(f"raw{i}", [P, UNIT])[:, :] for i in range(MIX_SLOTS)]
        w_hi = [sb(f"w_hi{i}", [P, UNIT])[:, :].bitcast(F32R) for i in range(2)]
        w_lo = [sb(f"w_lo{i}", [P, UNIT])[:, :].bitcast(F32R) for i in range(2)]
        x_hi, x_lo = (sb(n, [P, KD, SEQ])[:, :, :].bitcast(F32R) for n in ("x_hi", "x_lo"))
        st_hi, st_lo = (sb(n, [P, 4 * SEQ])[:, :].bitcast(F32R) for n in ("st_hi", "st_lo"))
        ht_hi, ht_lo = ([v[:, i * CHUNK:(i + 1) * CHUNK].bitcast(F32R) for i in range(2)]
                        for v in (sb("ht_hi", [P, 2 * CHUNK]), sb("ht_lo", [P, 2 * CHUNK])))
        small = sb("small", [P, 512])
        gates = sb("gates", [P, BRANCHES * KD, SEQ])
        oT_c = sb("oT_c", [P, NB, SEQ])
        work_c = sb("work_c", [P, 6, NB, SEQ])
        work_d = sb("work_d", [P, 12 * (SEQ + 3)])
        work_e = sb("work_e", [P, 3, NB * SEQ])
        dcv = sb("dcv", [P, 12, SEQ])
        zt = sb("zt", [P, TT, MIX])
        dexp = sb("dexp", [P, TT, HEADS, P])
        sm = sb("sm", [P, 2, 2, SEQ])
        wT = sb("wT", [P, 2, SEQ])

        def in_gates(b0, b1):
            return gates[:, b0:b1, :].rearrange("p k t -> p (k t)")

        xs = in_gates(0, 8).rearrange("p (a d) -> p a d", a=TT)
        xraw = gates[:, 8:16, :]
        cgate = gates[:, 16:20, :]
        cdg = in_gates(20, 24).rearrange("p (g c) -> p g c", g=8)
        cpad = in_gates(24, 29)[:, 0:NB * (SEQ + 3)].rearrange("p (b t) -> p b t", b=NB)
        dtmp, dusel = (in_gates(b, b + 4).rearrange("p (t h d) -> p t h d", t=TT, h=HEADS) for b in (24, 28))
        ot = zt[:, :, :].rearrange("p t (h d) -> p t h d", h=HEADS)

        banks_all = ctx.enter_context(nc.psum_tensor("banks_all", [P, 8, 512], F32))
        psum = [banks_all[:, i, :] for i in range(8)]

        ident = con[:, C_IDENT:C_IDENT + P]
        ones = con[:, C_ONES:C_ONES + P]
        tri = con[:, C_TRI:C_TRI + P]
        trix = con[:, C_TRIX:C_TRIX + P]
        neg_t = con[:, C_NEGT:C_NEGT + P]

        def par_of(name):
            a, n = PCOL[name]
            return par[:, a:a + n]

        c_xc, c_r, c_i, c_a, c_t, c_g = (work_c[:, i, :, :] for i in range(6))
        aq, ak, bq, bk = (work_c[:, i, :, :] for i in (0, 1, 3, 4))
        av, bv = (work_c[:, i, :, :].rearrange("p b t -> p (b t)").rearrange("p (a d) -> p a d", a=TT)
                  for i in (2, 5))
        acc = work_c[:, 0:2, :, :].rearrange("p a b t -> p (a b) t")
        acc_tmp = work_c[:, 2, 0:2, :]
        dpad = work_d[:, :].rearrange("p (b t) -> p b t", b=12)

        def heads_of(view):
            return view.rearrange("p (t h d) -> p t h d", t=TT, h=HEADS)

        SZ = TT * HEADS * P
        dX, dY, dP = (heads_of(work_d[:, i * SZ:(i + 1) * SZ]) for i in range(3))
        dth = work_e[:, :, :]
        ktok, vtok, dU = (heads_of(work_e[:, i, :]) for i in range(3))
        qtok = heads_of(work_d[:, 0:SZ])
        dK = dcv[:, 4:8, :]
        dQ = dcv[:, 0:4, :]
        tail = dcv[:, 8:12, :].rearrange("p b t -> p (b t)")
        dR = tail[:, 0:512].rearrange("p (h d) -> p h d", h=HEADS)
        dS = tail[:, 512:1024].rearrange("p (h d) -> p h d", h=HEADS)
        oT = [view.rearrange("p (b t) -> p b t", b=NB) if view is not None else oT_c[:, :, :]
              for view in (work_e[:, 0, :], work_e[:, 1, :], None, work_e[:, 2, :])]
        staged = [(x_hi[:, 0:NB, :], x_lo[:, 0:NB, :]),
                  tuple(v.rearrange("p (b t) -> p b t", b=NB) for v in (st_hi, st_lo))]
        ffn_raw = raw + [work_c[:, 2 * i:2 * i + 2, :, :].rearrange("p a b t -> p (a b t)") for i in range(3)]
        ffn_raw += [dcv[:, 0:8, :].rearrange("p b t -> p (b t)")]
        hT = [dexp[:, :, :, :].rearrange("p t h d -> p (t h d)")[:, i * 512:(i + 1) * 512] for i in range(2)]
        fth = [in_gates(28, 32)[:, i * 512:(i + 1) * 512] for i in range(2)]
        fs = [in_gates(24, 28)[:, i * 512:(i + 1) * 512] for i in range(2)]
        hf = [zt[:, i, 0:CHUNK] for i in range(2)]
        w_parts = [(w_hi[0], w_lo[0]), (w_hi[1], w_lo[1]),
                   tuple(v.rearrange("p k t -> p (k t)") for v in (x_hi, x_lo))]
        xsel_hi, xsel_lo = (v.rearrange("p (k s) -> p k s", k=KD) for v in (st_hi, st_lo))
        sel = sm[:, 0, :, 0:P]
        selg = sm[:, 1, :, 0:P]
        selgT = wT[:, 0, :]
        xsel = in_gates(16, 20).rearrange("p (k s) -> p k s", k=KD)
        yexp = in_gates(20, 24)

        at = [0]

        def cols(n):
            at[0] += n
            return small[:, at[0] - n:at[0]]

        ss, rstd, rtmp = cols(16), cols(16), cols(16)
        half_b, half_ba, half_bx = cols(32), cols(NB), cols(NB)
        sp_z, sp_y, sp_s, sp_s2, sp_p = cols(8), cols(8), cols(8), cols(8), cols(8)
        lru, nlru = cols(NB), cols(NB)
        lam_prod, lam_sum, lam_e, lam_neg = cols(P), cols(2), cols(2), cols(1)
        ba, beta, expA, dg = cols(16), cols(8), cols(4), cols(8)
        gcum, darg, dfac = cols(8), cols(16), cols(16)
        a_scale = cols(P)
        mx, nmx, sums, rec, rec2 = (cols(4) for _ in range(5))
        assert at[0] <= 512
        at2 = [0]

        def cols2(n):
            at2[0] += n
            return work_d[:, at2[0] - n:at2[0]]

        lg, eq, one1, one2, pick, gsel, member, vslot = (cols2(16) for _ in range(8))
        m0, m1, dm, em, p0, p1, fi = (cols2(2) for _ in range(7))
        cnt, over, pos, incl, tmp8, onesE = (cols2(EXPERTS) for _ in range(6))
        selq = cols2(OVERFLOWS * EXPERTS)
        slot_of, gate_of = cols2(TT * (PASSES + 1)), cols2(TT * (PASSES + 1))
        table = cols2(PASSES + 2)
        table_i = sb("table_i", [P, PASSES + 2], I32)

        names = """in_loaded small_loaded act_own dve_own pool_own
            sumsq_ready rstd_ready xs_ready xT_psum xraw_ready x_hi_ready x_lo_ready
            unit_hi unit_lo unit_lo_pool unit_done proj_evac st_hi_ready st_lo_ready acc_hi_ready acc_lo_ready
            sp_arg sp_exp c_conv_ready c_gates_psum c_tanh c_a_t c_coef c_sqrt c_gelu_arg c_gelu_tanh
            ba_psum ba_cols ba_act dg_ready
            d_conv_ready d_tanh_ready d_silu_ready d_tok_psum d_tok_ready d_ss_ready d_rs_ready
            d_unit_ready d_back_psum d_T_ready d_cum_psum d_gcum_ready d_args_ready d_exp_ready d_ub_ready
            d_kk_psum d_u_ready d_xy_init dusel_ready inv_p_psum inv_p_ready inv_x_psum xy_ready
            r0_ready v0_psum v0_ready s_psum s_ready ks_psum ks_taken r1_ready v1_psum v1_ready
            o_psum o_ss_ready o_rs_ready z_tanh d_out_ready d_oT_psum
            at_s_psum at_s_taken at_max_ready at_exp_ready at_w_ready at_t_psum at_t_ready at_o_psum
            at_o_taken a_ss_ready a_rs_ready a_out_ready at_oT_psum lam_arg lam_exp
            c_out_ready oA_ready oB_ready oD_ready br_psum br_taken acc_ready out_psum
            h13_psum f_tanh f_h_ready f_hT_ready y_psum w13_used w2_used f_out_taken
            h1_psum h3_psum hT_psum f_s_ready f_hi_ready f_lo_ready
            loads_over w1_hi w1_lo w3_hi w3_lo w2_hi w2_lo xsel_ready xsel_hi_ready xsel_lo_ready
            rt_psum rt_arg rt_exp rt_member rank_psum table_ready
            sel_ready gather_psum gather_ready selT_psum selT_ready y_ready scat_psum scat_taken out_stored"""
        S = {}
        for name in names.split():
            S[name] = sem(name)
        slot_loaded = [sem(f"slot_loaded{i}") for i in range(FFN_SLOTS)]

        def clear_semaphores():
            nums = sorted(s.num for s in sem_list)
            assert nums == list(range(nums[0], nums[-1] + 1))
            with nc.Block() as block:
                @block.sync
                def _(sp):
                    sp.sem_clear(range(nums[0], nums[-1] + 1))

        with nc.Block() as block:
            @block.sync
            def _(sp):
                sp.dma_start(con[:, :], consts).then_inc(S["in_loaded"], 16)
                sp.dma_start(h[:, :, :], x.rearrange("(t p) d -> p t d", p=P)).then_inc(S["in_loaded"], 16)
                sp.wait_ge(S["in_loaded"], 32)
        clear_semaphores()

        def norm_act(act, o):
            for t in range(TT):
                o.run(act.activation(in_gates(8, 12), h[:, t, :], ACT.Square,
                                     scale=DM ** -0.5, accum_out=ss[:, t:t + 1]), S["sumsq_ready"])
                o.settle()

        def pool_rsqrt(pool, o, n, scale, eps, ready):
            o.step(pool.tensor_scalar(rtmp[:, 0:n], ss[:, 0:n], scale, eps, ALU.mult, ALU.add))
            o.run(pool.tensor_tensor(rstd[:, 0:n], rtmp[:, 0:n], con[:, C_HALF:C_HALF + n], ALU.pow), ready)

        def norm_pool(pool, o):
            pool.wait_ge(S["sumsq_ready"], TT)
            pool_rsqrt(pool, o, TT, 1.0, 1e-6, S["rstd_ready"])

        def norm_pe(pe):
            pe.wait_ge(S["xs_ready"], TT)
            for t in range(TT):
                for q in range(2):
                    for k in range(4):
                        last = pe.transpose(psum[2 + 2 * t + q][:, k * P:(k + 1) * P],
                                            xs[:, t, (4 * q + k) * P:(4 * q + k + 1) * P], ident)
                    last.then_inc(S["xT_psum"], 1)

        def norm_dve(dve, o, gain):
            dve.wait_ge(S["rstd_ready"], 1)
            for t in range(TT):
                o.run(dve.tensor_scalar(xs[:, t, :], h[:, t, :], rstd[:, t:t + 1], None, ALU.mult),
                      S["xs_ready"])
            for t in range(TT):
                for q in range(2):
                    dve.wait_ge(S["xT_psum"], 2 * t + q + 1)
                    o.run(dve.tensor_tensor(
                        xraw[:, 4 * q:4 * q + 4, t * P:(t + 1) * P],
                        psum[2 + 2 * t + q][:, :].rearrange("p (k s) -> p k s", k=4),
                        gain[:, 4 * q:4 * q + 4].unsqueeze(2).to_broadcast([P, 4, P]), ALU.mult),
                        S["xraw_ready"])

        def norm_split_act(act, o):
            for t in range(TT):
                for q in range(2):
                    act.wait_ge(S["xraw_ready"], 2 * t + q + 1)
                    cut = (slice(None), slice(4 * q, 4 * q + 4), slice(t * P, (t + 1) * P))
                    o.run(act.activation(x_hi[cut], xraw[cut], ACT.Copy), S["x_hi_ready"])

        def norm_split_dve(dve, o):
            for t in range(TT):
                for q in range(2):
                    dve.wait_ge(S["x_hi_ready"], 2 * t + q + 1)
                    dve.wait_ge(S["xraw_ready"], 2 * t + q + 1)
                    cut = (slice(None), slice(4 * q, 4 * q + 4), slice(t * P, (t + 1) * P))
                    o.run(dve.tensor_tensor(x_lo[cut], xraw[cut], x_hi[cut].bitcast(F32), ALU.subtract),
                          S["x_lo_ready"])

        def softplus_dve(dve, o, n, sem_arg, sem_exp, count):
            z, y, s, s2, p = (c[:, 0:n] for c in (sp_z, sp_y, sp_s, sp_s2, sp_p))
            o.step(dve.tensor_scalar(s, z, -1.0, None, ALU.mult))
            o.step(dve.tensor_tensor(y, z, s, ALU.max), sem_arg)
            dve.wait_ge(sem_exp, count)
            o.step(dve.tensor_scalar(s, y, 2.0, None, ALU.add))
            o.step(dve.reciprocal(s, s))
            o.step(dve.tensor_tensor(s, y, s, ALU.mult))
            o.step(dve.tensor_tensor(s2, s, s, ALU.mult))
            o.step(dve.tensor_scalar(p, s2, 1.0 / 17, None, ALU.mult))
            for k in range(7, 0, -1):
                o.step(dve.scalar_tensor_tensor(p, p, 1.0 / (2 * k + 1), s2, ALU.add, ALU.mult))
            o.step(dve.scalar_tensor_tensor(p, p, 1.0, s, ALU.add, ALU.mult))
            o.step(dve.tensor_scalar(z, z, 0.0, None, ALU.max))
            o.step(dve.scalar_tensor_tensor(p, p, 2.0, z, ALU.mult, ALU.add))

        SCHED = mixer_schedule()

        def lo_sem(u):
            return S["unit_lo_pool" if lo_by_pool(u) else "unit_lo"]

        def hb(view):
            return view[:, :].rearrange("p (h d) -> p h d", h=HEADS)

        def bc_row(col, n, width=P):
            return col.unsqueeze(2).to_broadcast([P, n, width])

        def mixer_block(layer):
            with nc.Block() as block:
                @block.sync
                def _(sp):
                    sp.dma_start(par[:, :], params[bass.ds(layer, 1), :, :].rearrange("l p c -> p (l c)")
                                 ).then_inc(S["small_loaded"], 16)
                    sp.dma_start(cdg[:, :, :], cdiag[bass.ds(layer, 1), :, :].rearrange("l p c -> p (l c)")
                                 .rearrange("p (g c) -> p g c", g=8)).then_inc(S["small_loaded"], 16)
                    for u in range(MIX_UNITS):
                        for f in range(2):
                            if u >= MIX_SLOTS:
                                sp.wait_ge(lo_sem(u - MIX_SLOTS), lo_count(2 * (u - MIX_SLOTS) + f))
                            cut = (slice(None), slice(f * UNIT // 2, (f + 1) * UNIT // 2))
                            sp.dma_start(raw[u % MIX_SLOTS][cut],
                                         mix_units[bass.ds(layer, 1), u, :, cut[1]].rearrange("l p c -> p (l c)")
                                         ).then_inc(slot_loaded[u % MIX_SLOTS * 2 + f], 16)

                @block.tensor
                def _(pe):
                    def unit(u, k):
                        return [w[u % 2].rearrange("p (k c) -> p k c", k=k) for w in (w_hi, w_lo)]

                    def proj(j):
                        u, f = divmod(j, 2)
                        w, x = unit(u, KD), (x_hi, x_lo)
                        bank = psum[u % 2]
                        if j == 0:
                            pe.wait_ge(S["x_lo_ready"], 4)
                        if f == 0 and u >= 2:
                            pe.wait_ge(S["proj_evac"], u - 1)
                        if U_Z <= u < U_A or u in (16, 17, 22, 23):
                            def operands(a, b, k):
                                return x[b][:, k, f * P:(f + 1) * P], w[a][:, k, :]
                        else:
                            def operands(a, b, k):
                                return w[a][:, k, f * P:(f + 1) * P], x[b][:, k, :]
                        last = product3(pe, bank[:, f * UC:(f + 1) * UC], operands, KD,
                                        S["unit_hi"], lo_sem(u), 2 * u + 1, lo_count(2 * u))
                        if f == 1:
                            last.then_inc(S["unit_done"], 1)

                    def c_gates(_):
                        pe.wait_ge(S["c_conv_ready"], 1)
                        pe.wait_ge(S["small_loaded"], 32)
                        for g in range(2):
                            for m in range(NB):
                                last = pe.matmul(psum[2 + 2 * g + m // 2][:, (m % 2) * SEQ:(m % 2 + 1) * SEQ],
                                                 cdg[:, 4 * g + m, :], c_xc[:, m, :], start=True, stop=True)
                            last.then_inc(S["c_gates_psum"], 1)

                    def ba_cols(_):
                        pe.wait_ge(S["c_tanh"], 8)
                        w = par_of("w_ba").rearrange("p (k c) -> p k c", k=KD)
                        for t in range(TT):
                            for k in range(KD):
                                last = pe.matmul(psum[2][:, 8 * t:8 * t + 8], xraw[:, k, t * P:(t + 1) * P],
                                                 w[:, k, :], start=(k == 0), stop=(k == KD - 1))
                        last.then_inc(S["ba_psum"], 1)

                    def d_tok(part):
                        for g, t in (((0, 0), (0, 1), (1, 0), (1, 1)), ((2, 0), (2, 1)))[part]:
                            n = 2 * g + t
                            pe.wait_ge(S["d_silu_ready"], g + 1)
                            if n == 5:
                                pe.wait_ge(S["d_tok_ready"], 1)
                            for hd in range(HEADS):
                                last = pe.transpose(psum[3 + n % 5][:, hd * P:(hd + 1) * P],
                                                    dcv[:, 4 * g + hd, t * P:(t + 1) * P], ident)
                            last.then_inc(S["d_tok_psum"], 1)

                    def d_back(_):
                        pe.wait_ge(S["d_tok_ready"], 6)
                        pe.wait_ge(S["ba_cols"], 1)
                        for g in range(2):
                            for t in range(TT):
                                n = 2 * g + t
                                pe.wait_ge(S["d_unit_ready"], n + 1)
                                src = (qtok, ktok)[g]
                                for hd in range(HEADS):
                                    last = pe.transpose(psum[2 + n][:, hd * P:(hd + 1) * P],
                                                        src[:, t, hd, :], ident)
                                last.then_inc(S["d_back_psum"], 1)

                    def d_cum(_):
                        pe.wait_ge(S["dg_ready"], 1)
                        pe.wait_ge(S["d_T_ready"], 4)
                        for t in range(TT):
                            pe.matmul(psum[6][:, 4 * t:4 * t + 4], tri, dg[:, 4 * t:4 * t + 4], start=True, stop=True)
                        for t in range(TT):
                            for hd in range(HEADS):
                                c = 4 * t + hd
                                pe.matmul(psum[2 + t][:, hd * P:(hd + 1) * P],
                                          dg[:, c:c + 1].to_broadcast([P, P]), tri, start=True, stop=True)
                        for t in range(TT):
                            for hd in range(HEADS):
                                c = 4 * t + hd
                                last = pe.matmul(psum[4 + t][:, hd * P:(hd + 1) * P],
                                                 beta[:, c:c + 1].to_broadcast([P, P]), ident, start=True, stop=True)
                        last.then_inc(S["d_cum_psum"], 1)

                    def d_kk(_):
                        pe.wait_ge(S["d_args_ready"], 4)
                        for t in range(TT):
                            for hd in range(HEADS):
                                last = pe.matmul(psum[2 + t][:, hd * P:(hd + 1) * P], dK[:, hd, t * P:(t + 1) * P],
                                                 dK[:, hd, t * P:(t + 1) * P], start=True, stop=True)
                            last.then_inc(S["d_kk_psum"], 1)
                        for t in range(TT):
                            for hd in range(HEADS):
                                last = pe.matmul(psum[6 + t][:, hd * P:(hd + 1) * P], dK[:, hd, t * P:(t + 1) * P],
                                                 dQ[:, hd, t * P:(t + 1) * P], start=True, stop=True)
                            last.then_inc(S["d_kk_psum"], 1)

                    def inv_p(s):
                        pe.wait_ge(S["dusel_ready"], s + 1)
                        if s == 0:
                            pe.wait_ge(S["d_u_ready"], 4)
                        for t in range(TT):
                            pe.wait_ge(S["xy_ready"], 2 * s + t + 1)
                            for hd in range(HEADS):
                                last = pe.matmul(psum[2 + t][:, hd * P:(hd + 1) * P], dusel[:, t, hd, :],
                                                 dX[:, t, hd, :], start=True, stop=True)
                            last.then_inc(S["inv_p_psum"], 1)

                    def inv_x(s):
                        for t in range(TT):
                            pe.wait_ge(S["inv_p_ready"], 2 * s + t + 1)
                            if s == 0:
                                pe.wait_ge(S["d_ub_ready"], 2)
                            if s < LEVELS - 1:
                                for hd in range(HEADS):
                                    pe.matmul(psum[2 + t][:, hd * P:(hd + 1) * P], dY[:, t, hd, :],
                                              dP[:, t, hd, :], start=True, stop=True)
                            for hd in range(HEADS):
                                last = pe.matmul(psum[4 + t][:, hd * P:(hd + 1) * P], dP[:, t, hd, :],
                                                 dY[:, t, hd, :], start=True, stop=True)
                            last.then_inc(S["inv_x_psum"], 1)

                    def d_v0(_):
                        pe.wait_ge(S["r0_ready"], 1)
                        pe.wait_ge(S["xy_ready"], 2 * LEVELS + 2)
                        for hd in range(HEADS):
                            last = pe.matmul(psum[2][:, hd * P:(hd + 1) * P], dY[:, 0, hd, :], dR[:, hd, :],
                                             start=True, stop=True)
                        last.then_inc(S["v0_psum"], 1)

                    def d_s(_):
                        pe.wait_ge(S["v0_ready"], 1)
                        for hd in range(HEADS):
                            last = pe.matmul(psum[3][:, hd * P:(hd + 1) * P], ktok[:, 0, hd, :], dP[:, 0, hd, :],
                                             start=True, stop=True)
                        last.then_inc(S["s_psum"], 1)

                    def d_ks(_):
                        pe.wait_ge(S["s_ready"], 1)
                        for bank, src in ((2, dK), (4, dQ)):
                            for hd in range(HEADS):
                                last = pe.matmul(psum[bank][:, hd * P:(hd + 1) * P], src[:, hd, P:2 * P],
                                                 dS[:, hd, :], start=True, stop=True)
                        last.then_inc(S["ks_psum"], 1)

                    def d_v1(_):
                        pe.wait_ge(S["r1_ready"], 1)
                        for hd in range(HEADS):
                            last = pe.matmul(psum[3][:, hd * P:(hd + 1) * P], dY[:, 1, hd, :], dR[:, hd, :],
                                             start=True, stop=True)
                        last.then_inc(S["v1_psum"], 1)

                    def d_o(_):
                        pe.wait_ge(S["v1_ready"], 1)
                        pe.wait_ge(S["ks_taken"], 1)
                        for t, bank in ((0, 2), (1, 5)):
                            for hd in range(HEADS):
                                last = pe.matmul(psum[bank][:, hd * P:(hd + 1) * P], dexp[:, t, hd, :],
                                                 dP[:, t, hd, :], start=True, stop=True)
                        last.then_inc(S["o_psum"], 1)

                    def to_features(src, banks, ready):
                        for t in range(TT):
                            for hd in range(HEADS):
                                last = pe.transpose(psum[banks[t]][:, hd * P:(hd + 1) * P], src[:, t, hd, :], ident)
                            last.then_inc(ready, 1)

                    def d_oT(_):
                        pe.wait_ge(S["d_out_ready"], 1)
                        to_features(dtmp, (3, 4), S["d_oT_psum"])

                    def at_s(i):
                        if i < 4 * HEADS:
                            b, hd, qt = i // 8, (i % 8) // 2, i % 2
                            kw = (qt + 1) * P
                            pe.wait_ge(S["proj_evac"], U_A + 4 if b == 0 else U_GATE)
                            if i == 0:
                                pe.wait_ge(S["d_u_ready"], 4)
                                pe.wait_ge(S["o_ss_ready"], 1)
                            else:
                                pe.wait_ge(S["at_s_taken"], i)
                            if i == 9:
                                pe.wait_ge(S["oA_ready"], TT)
                            if b == 0:
                                for c in range(2):
                                    rows = slice(64 * c, 64 * c + 64)
                                    last = pe.matmul(psum[5 + c][:, 0:kw],
                                                     aq[rows, hd, qt * P:(qt + 1) * P], ak[rows, hd, 0:kw],
                                                     start=True, stop=True)
                            else:
                                last = pe.matmul(psum[6][:, 0:kw], bq[:, hd, qt * P:(qt + 1) * P], bk[:, hd, 0:kw],
                                                 start=True, stop=True)
                            last.then_inc(S["at_s_psum"], 1)
                        if i >= 1:
                            qt = (i - 1) % 2
                            pe.wait_ge(S["at_w_ready"], i)
                            if i >= 2:
                                pe.wait_ge(S["at_o_taken"], i - 1)
                            for kb in range(qt + 1):
                                last = pe.transpose(psum[7][:, kb * P:(kb + 1) * P],
                                                    sm[:, (i - 1) % 2, 0, kb * P:(kb + 1) * P], ident)
                            last.then_inc(S["at_t_psum"], 1)

                    def at_o(i):
                        b, hd, qt = i // 8, (i % 8) // 2, i % 2
                        v = (av, bv)[b]
                        pe.wait_ge(S["at_t_ready"], i + 1)
                        for kb in range(qt + 1):
                            last = pe.matmul(psum[7][:, 0:P], wT[:, i % 2, kb * P:(kb + 1) * P],
                                             v[:, kb, hd * P:(hd + 1) * P], start=(kb == 0), stop=(kb == qt))
                        last.then_inc(S["at_o_psum"], 1)

                    def at_oT(b):
                        pe.wait_ge(S["a_out_ready"], b + 1)
                        if b == 0:
                            pe.wait_ge(S["at_s_taken"], 9)
                        to_features(ot, (6, 7), S["at_oT_psum"])

                    def branch(j):
                        q = j % 4
                        u = U_BR + j // 2
                        w, x = unit(u, NB), staged[j // 4 % 2]
                        if j < 2:
                            pe.wait_ge(S["proj_evac"], U_BR)
                        else:
                            pe.wait_ge(S["br_taken"], j - 1)
                        pe.wait_ge(S["st_lo_ready"], j // 4 + 1)
                        for f in range(2):
                            b = 2 * (q % 2) + f
                            last = product3(pe, psum[j % 2][:, f * SEQ:(f + 1) * SEQ],
                                            lambda i, l, k: (w[i][:, k, b * P:(b + 1) * P], x[l][:, k, :]), NB,
                                            S["unit_hi"], lo_sem(u), 2 * u + 1, lo_count(2 * u))
                        if j % 2 == 0:
                            last.then_inc(S["br_psum"], 1)
                        else:
                            last.then_inc(S["unit_done"], 1)

                    def project_out(j):
                        u = U_OUT + j
                        w, x = unit(u, KD), (x_hi, x_lo)
                        if j == 0:
                            pe.wait_ge(S["acc_lo_ready"], 4)
                        if j >= 2:
                            pe.wait_ge(S["f_out_taken"], j - 1)
                        for t in range(TT):
                            last = product3(pe, psum[j % 2][:, t * UC:(t + 1) * UC],
                                            lambda i, l, k: (x[l][:, k, t * P:(t + 1) * P], w[i][:, k, :]), KD,
                                            S["unit_hi"], lo_sem(u), 2 * u + 1, lo_count(2 * u))
                        last.then_inc(S["unit_done"], 1)

                    steps = {"norm": lambda _: norm_pe(pe), "proj": proj, "c_gates": c_gates, "ba": ba_cols,
                             "d_tok": d_tok, "d_back": d_back, "d_cum": d_cum, "d_kk": d_kk, "inv_p": inv_p,
                             "inv_x": inv_x, "d_v0": d_v0, "d_s": d_s, "d_ks": d_ks, "d_v1": d_v1, "d_o": d_o,
                             "d_oT": d_oT, "at_s": at_s, "at_o": at_o, "at_oT": at_oT, "branch": branch,
                             "out": project_out}
                    for what, i in SCHED:
                        if what in steps:
                            steps[what](i)

                @block.scalar
                def _(act):
                    o = Order(act, S["act_own"])

                    def copy(dst, src, ready=None, scale=1.0):
                        o.run(act.activation(dst, src, ACT.Copy, scale=scale), ready)

                    def split_hi(half):
                        u, f = divmod(half, 2)
                        if u < MIX_UNITS:
                            if u >= 2:
                                act.wait_ge(S["unit_done"], u - 1)
                            act.wait_ge(slot_loaded[u % MIX_SLOTS * 2 + f], 16 * (u // MIX_SLOTS + 1))
                            cut = (slice(None), slice(f * UNIT // 2, (f + 1) * UNIT // 2))
                            copy(w_hi[u % 2][cut], raw[u % MIX_SLOTS][cut], S["unit_hi"])

                    def prepare(_):
                        norm_act(act, o)
                        split_hi(0)
                        split_hi(1)
                        norm_split_act(act, o)
                        split_hi(2)
                        act.wait_ge(S["sp_arg"], 1)
                        o.run(act.activation(sp_y[:, 0:NB], sp_y[:, 0:NB], ACT.Exp, scale=-1.0), S["sp_exp"])
                        act.wait_ge(S["lam_arg"], 2)
                        o.run(act.activation(lam_e, lam_sum, ACT.Exp), S["lam_exp"])
                        act.wait_ge(S["small_loaded"], 32)
                        o.run(act.activation(expA, par_of("d_A_log"), ACT.Exp), S["lam_exp"])

                    def proj(j):
                        u, f = divmod(j, 2)
                        split_hi(j + 3)
                        if f == 0:
                            return
                        act.wait_ge(S["unit_done"], u + 1)
                        bank = psum[u % 2][:, :].rearrange("p (b t) -> p b t", b=2)
                        ready = S["proj_evac"]
                        if u < U_C + 2:
                            copy(cpad[:, 2 * u:2 * u + 2, 3:3 + SEQ], bank, ready)
                        elif u < U_D:
                            copy(cgate[:, 2 * (u - 2):2 * (u - 2) + 2, :], bank, ready)
                        elif u < U_Z:
                            b = 2 * (u - U_D)
                            copy(dpad[:, b:b + 2, 3:3 + SEQ], bank, ready)
                        elif u < U_A:
                            c = UC * (u - U_Z)
                            copy(zt[:, :, c:c + UC], bank, ready)
                        elif u < U_GATE:
                            if u == U_A:
                                act.wait_ge(S["c_out_ready"], 1)
                            b, r = divmod(u - U_A, 6)
                            if r < 4:
                                dst = ((aq, ak), (bq, bk))[b][r // 2][:, 2 * (r % 2):2 * (r % 2) + 2, :]
                            else:
                                dst = (av, bv)[b][:, :, UC * (r - 4):UC * (r - 3)]
                            copy(dst, bank, ready)
                        else:
                            for f in range(2):
                                b = 2 * (u - U_GATE) + f
                                ins = act.activation(gates[:, b, :], bank[:, f, :], ACT.Tanh,
                                                     bias=half_b[:, b:b + 1], scale=0.5)
                                o.run(ins, ready if f else None)

                    def c_gelu_tanh(_):
                        act.wait_ge(S["c_gelu_arg"], 1)
                        o.run(act.activation(c_g, c_g, ACT.Tanh, scale=math.sqrt(2 / math.pi)), S["c_gelu_tanh"])

                    def d_tanh(g):
                        act.wait_ge(S["d_conv_ready"], g + 1)
                        o.run(act.activation(dth[:, g, :], dcv[:, 4 * g:4 * g + 4, :].rearrange("p b t -> p (b t)"),
                                             ACT.Tanh, scale=0.5), S["d_tanh_ready"])

                    def c_gates(_):
                        for g, (dst, bias) in enumerate(((c_r, half_ba), (c_i, half_bx))):
                            act.wait_ge(S["c_gates_psum"], g + 1)
                            for m in range(NB):
                                o.run(act.activation(dst[:, m, :],
                                                     psum[2 + 2 * g + m // 2][:, (m % 2) * SEQ:(m % 2 + 1) * SEQ],
                                                     ACT.Tanh, bias=bias[:, m:m + 1], scale=0.5), S["c_tanh"])

                    def c_decay(_):
                        o.settle()
                        for m in range(NB):
                            o.run(act.activation(c_a[:, m, :], c_r[:, m, :], ACT.Exp,
                                                 bias=nlru[:, m:m + 1], scale=nlru[:, m:m + 1]), S["c_a_t"])
                            o.run(act.activation(c_t[:, m, :], c_r[:, m, :], ACT.Tanh,
                                                 bias=lru[:, m:m + 1], scale=lru[:, m:m + 1]), S["c_a_t"])

                    def c_coef(_):
                        act.wait_ge(S["c_coef"], 1)
                        o.run(act.activation(c_t, c_t, ACT.Sqrt, scale=0.5), S["c_sqrt"])

                    def ba_act(_):
                        act.wait_ge(S["ba_cols"], 1)
                        b3 = ba.rearrange("p (t c) -> p t c", t=TT)
                        o.run(act.activation(beta.rearrange("p (t c) -> p t c", t=TT), b3[:, :, 0:HEADS],
                                             ACT.Tanh, scale=0.5), S["ba_act"])
                        act.wait_ge(S["sp_arg"], 2)
                        o.run(act.activation(sp_y, sp_y, ACT.Exp, scale=-1.0), S["sp_exp"])

                    def d_tok(part):
                        if part == 0:
                            d_tanh(2)
                        for n in ((0, 1, 2, 3), (4, 5))[part]:
                            g, t = divmod(n, 2)
                            act.wait_ge(S["d_tok_psum"], n + 1)
                            act.wait_ge(S["d_silu_ready"], 3)
                            copy((qtok, ktok, vtok)[g][:, t], hb(psum[3 + n % 5]), S["d_tok_ready"],
                                 scale=0.5 if g == 2 else 1.0)

                    def d_back(_):
                        for n in range(4):
                            g, t = divmod(n, 2)
                            act.wait_ge(S["d_back_psum"], n + 1)
                            act.wait_ge(S["d_tok_psum"], 6)
                            copy((dQ, dK)[g][:, :, t * P:(t + 1) * P], hb(psum[2 + n]), S["d_T_ready"])

                    def d_cum(_):
                        act.wait_ge(S["d_args_ready"], 4)
                        o.run(act.activation(dexp[:, :, :, :], dexp[:, :, :, :], ACT.Exp), S["d_exp_ready"])
                        o.run(act.activation(dfac, darg, ACT.Exp), S["d_exp_ready"])

                    def inv_p(s):
                        for t in range(TT):
                            act.wait_ge(S["inv_p_psum"], 2 * s + t + 1)
                            copy(dP[:, t], hb(psum[2 + t]), S["inv_p_ready"])

                    def d_v0(_):
                        act.wait_ge(S["v0_psum"], 1)
                        act.wait_ge(S["inv_x_psum"], 2 * LEVELS)
                        copy(dP[:, 0], hb(psum[2]), S["v0_ready"])

                    def d_s(_):
                        act.wait_ge(S["s_psum"], 1)
                        copy(dS, hb(psum[3]), S["s_ready"])

                    def d_v1(_):
                        act.wait_ge(S["v1_psum"], 1)
                        copy(dP[:, 1], hb(psum[3]), S["v1_ready"])

                    def d_o(_):
                        act.wait_ge(S["proj_evac"], U_A)
                        act.wait_ge(S["d_u_ready"], 4)
                        act.wait_ge(S["xy_ready"], 2 * LEVELS + 2)
                        o.run(act.activation(dusel.rearrange("p t h d -> p (t h d)"),
                                             zt[:, :, :].rearrange("p t d -> p (t d)"), ACT.Tanh, scale=0.5),
                              S["z_tanh"])

                    def from_psum(n, banks, psum_ready):
                        for t in range(TT):
                            act.wait_ge(psum_ready[0], psum_ready[1] + t + 1)
                            copy(oT[n][:, :, t * P:(t + 1) * P], hb(psum[banks[t]]),
                                 {0: S["oA_ready"], 1: S["oB_ready"], 3: S["oD_ready"]}[n])

                    def at_s(i):
                        if i < 4 * HEADS:
                            kw = (i % 2 + 1) * P
                            act.wait_ge(S["at_max_ready"], i + 1)
                            for c in range(2 if i < 8 else 1):
                                o.run(act.activation(sm[:, i % 2, c, 0:kw], sm[:, i % 2, c, 0:kw], ACT.Exp,
                                                     bias=nmx[:, c:c + 1], accum_out=sums[:, c:c + 1]),
                                      S["at_exp_ready"])
                        if i >= 1:
                            kw = ((i - 1) % 2 + 1) * P
                            act.wait_ge(S["at_t_psum"], i)
                            if i >= 3:
                                act.wait_ge(S["at_o_psum"], i - 2)
                            copy(wT[:, (i - 1) % 2, 0:kw], psum[7][:, 0:kw], S["at_t_ready"])

                    def at_oT(b):
                        from_psum(b, (6, 7), (S["at_oT_psum"], 2 * b))

                    def d_oT(_):
                        from_psum(3, (3, 4), (S["d_oT_psum"], 0))

                    def stage(m):
                        n = BRANCH_ORDER[m]
                        if n == 2:
                            act.wait_ge(S["c_out_ready"], 1)
                        if m == 0:
                            act.wait_ge(S["unit_done"], U_BR)
                        elif m >= 2:
                            act.wait_ge(S["unit_done"], U_BR + 2 * (m - 1))
                        o.settle()
                        copy(staged[m % 2][0], oT[n], S["st_hi_ready"])

                    def branch(j):
                        split_hi(2 * U_BR + j + 3)
                        if j >= 12:
                            q = j - 12
                            act.wait_ge(S["unit_done"], U_BR + 6)
                            act.wait_ge(S["acc_ready"], q + 1)
                            copy(x_hi[:, 2 * q:2 * q + 2, :], acc[:, 2 * q:2 * q + 2, :], S["acc_hi_ready"])

                    def project_out(j):
                        split_hi(2 * (U_OUT + j) + 3)
                        split_hi(2 * (U_OUT + j) + 4)

                    steps = {"stage": stage, "branch": branch, "out": project_out,
                             "c_decay": c_decay, "c_coef": c_coef, "c_gelu_tanh": c_gelu_tanh, "d_tanh": d_tanh,
                             "norm": prepare, "proj": proj, "c_gates": c_gates, "ba": ba_act, "d_tok": d_tok,
                             "d_back": d_back, "d_cum": d_cum, "inv_p": inv_p, "d_v0": d_v0, "d_s": d_s,
                             "d_v1": d_v1, "d_o": d_o, "at_s": at_s, "at_oT": at_oT, "d_oT": d_oT}
                    for what, i in SCHED:
                        if what in steps:
                            steps[what](i)

                @block.gpsimd
                def _(pool):
                    o = Order(pool, S["pool_own"])

                    def split_lo(half):
                        u, f = divmod(half, 2)
                        if u < MIX_UNITS and lo_by_pool(u):
                            pool.wait_ge(S["unit_hi"], half + 1)
                            cut = (slice(None), slice(f * UNIT // 2, (f + 1) * UNIT // 2))
                            o.run(pool.tensor_tensor(w_lo[u % 2][cut], raw[u % MIX_SLOTS][cut],
                                                     w_hi[u % 2][cut].bitcast(F32), ALU.subtract),
                                  S["unit_lo_pool"])

                    def project_out(j):
                        split_lo(2 * (U_OUT + j) + 3)
                        split_lo(2 * (U_OUT + j) + 4)

                    def select_level(s):
                        if s == 0:
                            pool.wait_ge(S["d_u_ready"], 4)
                        else:
                            pool.wait_ge(S["inv_p_psum"], 2 * s)
                        mask = con[:, C_LEVEL + s * P:C_LEVEL + (s + 1) * P]
                        o.run(pool.tensor_tensor(
                            dusel.rearrange("p t h d -> p (t h) d"),
                            dU.rearrange("p t h d -> p (t h) d"),
                            mask.unsqueeze(1).to_broadcast([P, TT * HEADS, P]), ALU.mult), S["dusel_ready"])

                    def d_tok(part):
                        if part == 1:
                            pool.wait_ge(S["d_ss_ready"], 1)
                            pool_rsqrt(pool, o, 16, 0.25, 1e-6, S["d_rs_ready"])

                    def d_o(_):
                        pool.wait_ge(S["o_ss_ready"], 1)
                        pool_rsqrt(pool, o, 8, 1.0 / P, 1e-6, S["o_rs_ready"])

                    def at_oT(b):
                        if b == 0:
                            pool.wait_ge(S["a_ss_ready"], 1)
                            pool_rsqrt(pool, o, 8, 1.0 / P, 1e-5, S["a_rs_ready"])

                    steps = {"norm": lambda _: norm_pool(pool, o), "d_tok": d_tok, "inv_p": select_level,
                             "d_o": d_o, "at_oT": at_oT, "proj": lambda j: split_lo(j + 3),
                             "branch": lambda j: split_lo(2 * U_BR + j + 3), "out": project_out}
                    for what, i in SCHED:
                        if what in steps:
                            steps[what](i)

                @block.vector
                def _(dve):
                    o = Order(dve, S["dve_own"])
                    TMPD = dtmp

                    def split_lo(half):
                        u, f = divmod(half, 2)
                        if u < MIX_UNITS and not lo_by_pool(u):
                            dve.wait_ge(S["unit_hi"], half + 1)
                            cut = (slice(None), slice(f * UNIT // 2, (f + 1) * UNIT // 2))
                            o.run(dve.tensor_tensor(w_lo[u % 2][cut], raw[u % MIX_SLOTS][cut],
                                                    w_hi[u % 2][cut].bitcast(F32),
                                                    ALU.subtract), S["unit_lo"])

                    def prepare(_):
                        dve.wait_ge(S["small_loaded"], 32)
                        o.run(dve.tensor_scalar(half_b, par_of("b_gate"), 0.5, None, ALU.mult))
                        o.run(dve.tensor_scalar(half_ba, par_of("c_b_a"), 0.5, None, ALU.mult))
                        o.run(dve.tensor_scalar(half_bx, par_of("c_b_x"), 0.5, None, ALU.mult))
                        o.run(dve.memset(dpad[:, :, 0:3], 0.0))
                        o.run(dve.memset(cpad[:, :, 0:3], 0.0))
                        norm_dve(dve, o, par_of("norm_mix"))
                        split_lo(0)
                        split_lo(1)
                        norm_split_dve(dve, o)
                        split_lo(2)
                        o.settle()
                        o.step(dve.tensor_scalar(sp_z[:, 0:NB], par_of("c_lambda"), -1.0, None, ALU.mult))
                        softplus_dve(dve, o, NB, S["sp_arg"], S["sp_exp"], 1)
                        o.run(dve.tensor_scalar(lru, sp_p[:, 0:NB], LRU_C / 2, None, ALU.mult))
                        o.run(dve.tensor_scalar(nlru, sp_p[:, 0:NB], -LRU_C / 2, None, ALU.mult))
                        lam4 = par_of("lam").rearrange("p (a b c) -> p a b c", a=2, b=2)
                        o.step(dve.tensor_tensor(lam_prod.rearrange("p (a c) -> p a c", a=2), lam4[:, :, 0, :],
                                                 lam4[:, :, 1, :], ALU.mult))
                        for c in range(2):
                            o.run(dve.tensor_reduce(lam_sum[:, c:c + 1], lam_prod[:, 64 * c:64 * c + 64], AX, ALU.add),
                                  S["lam_arg"])
                        dve.wait_ge(S["lam_exp"], 2)
                        o.step(dve.tensor_tensor(lam_neg, lam_e[:, 1:2], lam_e[:, 0:1], ALU.subtract))
                        o.step(dve.tensor_tensor(lam_neg, lam_neg, par_of("lam_init"), ALU.subtract))
                        o.run(dve.tensor_scalar(a_scale, par_of("a_subln"), par_of("out_scale"), None, ALU.mult))
                        o.settle()

                    def conv(dst, src, w, n0, n1, bias, tap, ready):
                        o.settle()
                        for b in range(n0, n1):
                            col = w[:, b * TAPS + tap:b * TAPS + tap + 1]
                            if tap == 0 and bias is None:
                                ins = dve.tensor_scalar(dst[:, b, :], src[:, b, 0:SEQ], col, None, ALU.mult)
                            elif tap == 0:
                                ins = dve.tensor_scalar(dst[:, b, :], src[:, b, 0:SEQ], col, bias[:, b:b + 1],
                                                        ALU.mult, ALU.add)
                            else:
                                ins = dve.scalar_tensor_tensor(dst[:, b, :], src[:, b, tap:tap + SEQ], col,
                                                               dst[:, b, :], ALU.mult, ALU.add)
                            o.run(ins, ready if tap == TAPS - 1 and b == n1 - 1 else None)

                    def c_conv(tap):
                        if tap == 0:
                            dve.wait_ge(S["proj_evac"], 2)
                        conv(c_xc, cpad, par_of("c_conv_w"), 0, NB, par_of("c_conv_b"), tap, S["c_conv_ready"])

                    def d_conv(i):
                        g, tap = divmod(i, TAPS)
                        if tap == 0:
                            dve.wait_ge(S["proj_evac"], U_D + 2 * g + 2)
                        conv(dcv, dpad, par_of("d_conv_w"), 4 * g, 4 * g + 4, None, tap, S["d_conv_ready"])

                    def c_gelu_arg(_):
                        dve.wait_ge(S["proj_evac"], 4)
                        o.step(dve.tensor_tensor(c_g, cgate, cgate, ALU.mult))
                        o.step(dve.tensor_scalar(c_g, c_g, 0.044715, 1.0, ALU.mult, ALU.add))
                        o.step(dve.tensor_tensor(c_g, c_g, cgate, ALU.mult), S["c_gelu_arg"])

                    def c_gelu(_):
                        dve.wait_ge(S["c_gelu_tanh"], 1)
                        o.step(dve.scalar_tensor_tensor(c_g, c_g, 1.0, cgate, ALU.add, ALU.mult))

                    def silu(g):
                        dve.wait_ge(S["d_tanh_ready"], g + 1)
                        o.settle()
                        v = dcv[:, 4 * g:4 * g + 4, :].rearrange("p b t -> p (b t)")
                        o.step(dve.scalar_tensor_tensor(v, dth[:, g, :], 1.0, v, ALU.add, ALU.mult),
                               S["d_silu_ready"])

                    def c_gates(_):
                        dve.wait_ge(S["c_tanh"], 8)
                        o.run(dve.scalar_tensor_tensor(c_i, c_i, 1.0, c_xc, ALU.add, ALU.mult))

                    def c_coef(_):
                        o.settle()
                        dve.wait_ge(S["c_a_t"], 8)
                        o.step(dve.tensor_scalar(c_r, c_t, 1.0, None, ALU.add))
                        o.step(dve.reciprocal(c_r, c_r))
                        o.step(dve.scalar_tensor_tensor(c_t, c_t, 1.0e-30, c_r, ALU.max, ALU.mult), S["c_coef"])

                    def c_scan(_):
                        dve.wait_ge(S["c_sqrt"], 1)
                        o.step(dve.tensor_tensor(c_i, c_i, c_t, ALU.mult))
                        for m in range(NB):
                            o.run(dve.tensor_tensor_scan(c_r[:, m, :], c_a[:, m, :], c_i[:, m, :], 0.0,
                                                         ALU.mult, ALU.add))
                        o.settle()
                        o.run(dve.scalar_tensor_tensor(oT_c[:, :, :], c_r, 0.5, c_g, ALU.mult, ALU.mult),
                              S["c_out_ready"])

                    def ba_dve(_):
                        dve.wait_ge(S["ba_psum"], 1)
                        o.step(dve.tensor_copy(ba, psum[2][:, 0:16]), S["ba_cols"])
                        b3 = ba.rearrange("p (t c) -> p t c", t=TT)
                        z3 = sp_z.rearrange("p (t c) -> p t c", t=TT)
                        bias = par_of("d_dt_bias").unsqueeze(1).to_broadcast([P, TT, HEADS])
                        o.step(dve.tensor_tensor(z3, b3[:, :, HEADS:], bias, ALU.add))
                        softplus_dve(dve, o, 8, S["sp_arg"], S["sp_exp"], 2)
                        dve.wait_ge(S["ba_act"], 1)
                        o.step(dve.tensor_scalar(beta, beta, 0.5, 0.5, ALU.mult, ALU.add))
                        o.run(dve.scalar_tensor_tensor(
                            dg.rearrange("p (t c) -> p t c", t=TT), sp_p.rearrange("p (t c) -> p t c", t=TT), -1.0,
                            expA.unsqueeze(1).to_broadcast([P, TT, HEADS]), ALU.mult, ALU.mult), S["dg_ready"])

                    def d_tok(part):
                        if part == 0:
                            silu(2)
                            for n in range(4):
                                g, t = divmod(n, 2)
                                dve.wait_ge(S["d_tok_ready"], n + 1)
                                src = (qtok, ktok)[g][:, t]
                                o.step(dve.tensor_tensor(TMPD[:, t], src, src, ALU.mult))
                                o.step(dve.tensor_reduce(ss[:, 4 * n:4 * n + 4], TMPD[:, t], AX, ALU.add),
                                       S["d_ss_ready"] if n == 3 else None)
                            return
                        dve.wait_ge(S["d_rs_ready"], 1)
                        o.run(dve.tensor_scalar(rtmp[:, 0:8], rstd[:, 0:8], 0.5 * P ** -0.5, None, ALU.mult))
                        o.step(dve.tensor_scalar(rtmp[:, 8:16], rstd[:, 8:16], 0.5, None, ALU.mult))
                        for n in range(4):
                            g, t = divmod(n, 2)
                            v = (qtok, ktok)[g][:, t]
                            o.run(dve.tensor_tensor(v, v, bc_row(rtmp[:, 4 * n:4 * n + 4], HEADS), ALU.mult),
                                  S["d_unit_ready"])

                    def d_cum(_):
                        dve.wait_ge(S["d_cum_psum"], 1)
                        o.step(dve.tensor_copy(gcum, psum[6][:, 0:8]))
                        for t in range(TT):
                            for hd in range(HEADS):
                                c = 4 * t + hd
                                o.run(dve.scalar_tensor_tensor(dexp[:, t, hd, :], psum[2 + t][:, hd * P:(hd + 1) * P],
                                                               gcum[:, c:c + 1], neg_t, ALU.subtract, ALU.add),
                                      S["d_args_ready"] if hd == HEADS - 1 else None)
                        o.run(dve.tensor_copy(darg[:, 0:8], gcum))
                        for t in range(TT):
                            o.run(dve.tensor_tensor(darg[:, 8 + 4 * t:12 + 4 * t], hb(psum[2 + t])[:, :, P - 1],
                                                    gcum[:, 4 * t:4 * t + 4], ALU.subtract), S["d_args_ready"])
                        dve.wait_ge(S["d_exp_ready"], 2)
                        for t in range(TT):
                            o.run(dve.tensor_tensor(dU[:, t], dexp[:, t], hb(psum[4 + t]), ALU.mult), S["d_ub_ready"])
                        o.settle()
                        dve.wait_ge(S["d_tok_ready"], 6)
                        dve.wait_ge(S["d_back_psum"], 4)
                        o.run(dve.tensor_tensor(dR, vtok[:, 0], bc_row(beta[:, 0:4], HEADS), ALU.mult), S["r0_ready"])
                        o.run(dve.tensor_tensor(ktok[:, 0], ktok[:, 0], bc_row(dfac[:, 8:12], HEADS), ALU.mult))
                        for t in range(TT):
                            eye = ident.unsqueeze(1).to_broadcast([P, HEADS, P])
                            o.run(dve.tensor_copy(dX[:, t], eye))
                            o.run(dve.tensor_copy(dY[:, t], eye), S["xy_ready"])

                    def d_kk(_):
                        o.settle()
                        for t in range(TT):
                            dve.wait_ge(S["d_kk_psum"], t + 1)
                            o.run(dve.tensor_tensor(dU[:, t], dU[:, t], hb(psum[2 + t]), ALU.mult), S["d_u_ready"])
                        for t in range(TT):
                            dve.wait_ge(S["d_kk_psum"], 2 + t + 1)
                            o.run(dve.tensor_tensor(dexp[:, t], dexp[:, t], hb(psum[6 + t]), ALU.mult), S["d_u_ready"])

                    def inv_x(s):
                        o.settle()
                        for t in range(TT):
                            dve.wait_ge(S["inv_x_psum"], 2 * s + t + 1)
                            if s < LEVELS - 1:
                                o.run(dve.tensor_tensor(dX[:, t], dX[:, t], hb(psum[2 + t]), ALU.subtract))
                                o.settle()
                            o.run(dve.tensor_tensor(dY[:, t], dY[:, t], hb(psum[4 + t]), ALU.subtract), S["xy_ready"])

                    def d_ks(_):
                        o.settle()
                        dve.wait_ge(S["ks_psum"], 1)
                        dve.wait_ge(S["v0_psum"], 1)
                        o.step(dve.tensor_tensor(TMPD[:, 0], hb(psum[2]), bc_row(dfac[:, 4:8], HEADS), ALU.mult))
                        o.step(dve.tensor_tensor(TMPD[:, 0], vtok[:, 1], TMPD[:, 0], ALU.subtract))
                        o.step(dve.tensor_tensor(dR, TMPD[:, 0], bc_row(beta[:, 4:8], HEADS), ALU.mult), S["r1_ready"])
                        o.step(dve.tensor_tensor(TMPD[:, 1], hb(psum[4]), bc_row(dfac[:, 4:8], HEADS), ALU.mult),
                               S["ks_taken"])

                    def d_o(_):
                        dve.wait_ge(S["o_psum"], 1)
                        o.run(dve.tensor_copy(TMPD[:, 0], hb(psum[2])))
                        o.step(dve.tensor_tensor(TMPD[:, 1], hb(psum[5]), TMPD[:, 1], ALU.add))
                        sq = dX
                        o.step(dve.tensor_tensor(sq, TMPD, TMPD, ALU.mult))
                        o.step(dve.tensor_reduce(ss[:, 0:8], sq.rearrange("p t h d -> p (t h) d"), AX, ALU.add),
                               S["o_ss_ready"])
                        dve.wait_ge(S["z_tanh"], 1)
                        z2 = zt[:, :, :].rearrange("p t d -> p (t d)")
                        o.run(dve.scalar_tensor_tensor(z2, dusel.rearrange("p t h d -> p (t h d)"), 1.0,
                                                       z2, ALU.add, ALU.mult))
                        dve.wait_ge(S["o_rs_ready"], 1)
                        o.step(dve.tensor_scalar(rtmp[:, 0:8], rstd[:, 0:8], 0.5, None, ALU.mult))
                        v = TMPD.rearrange("p t h d -> p (t h) d")
                        o.step(dve.tensor_tensor(v, v, bc_row(rtmp[:, 0:8], 8), ALU.mult))
                        o.step(dve.tensor_tensor(v, v, par_of("d_norm").unsqueeze(1).to_broadcast([P, 8, P]), ALU.mult))
                        o.step(dve.tensor_tensor(v, v, z2.rearrange("p (n d) -> p n d", n=8), ALU.mult),
                               S["d_out_ready"])

                    def at_s(i):
                        if i >= 4 * HEADS:
                            return
                        qt, b = i % 2, i // 8
                        kw, nc_ = (qt + 1) * P, 2 - b
                        o.settle()
                        dve.wait_ge(S["at_s_psum"], i + 1)
                        if i >= 2:
                            dve.wait_ge(S["at_t_psum"], i - 1)
                        mask = con[:, C_CAUSAL + SEQ - kw:C_CAUSAL + SEQ]
                        s = sm[:, i % 2, 0:nc_, 0:kw]
                        src = banks_all[:, 5 + b:7, 0:kw]
                        scale = (64 if b == 0 else P) ** -0.5
                        o.step(dve.scalar_tensor_tensor(s, src, scale, mask.unsqueeze(1).to_broadcast([P, nc_, kw]),
                                                        ALU.mult, ALU.add), S["at_s_taken"])
                        o.step(dve.tensor_reduce(mx[:, 0:nc_], s, AX, ALU.max))
                        o.step(dve.tensor_scalar(nmx[:, 0:nc_], mx[:, 0:nc_], -1.0, None, ALU.mult), S["at_max_ready"])
                        dve.wait_ge(S["at_exp_ready"], 2 * i + 2 if b == 0 else 16 + i - 8 + 1)
                        if b == 0:
                            o.step(dve.reciprocal(rec[:, 0:2], sums[:, 0:2]))
                            o.run(dve.tensor_scalar(rec2[:, 0:1], rec[:, 1:2], lam_neg, None, ALU.mult))
                            o.step(dve.tensor_scalar(s[:, 0, :], s[:, 0, :], rec[:, 0:1], None, ALU.mult))
                            o.step(dve.scalar_tensor_tensor(s[:, 0, :], s[:, 1, :], rec2[:, 0:1], s[:, 0, :],
                                                            ALU.mult, ALU.add), S["at_w_ready"])
                        else:
                            o.step(dve.reciprocal(rec[:, 2 + qt:3 + qt], sums[:, 0:1]), S["at_w_ready"])

                    def at_o(i):
                        b, hd, qt = i // 8, (i % 8) // 2, i % 2
                        dve.wait_ge(S["at_o_psum"], i + 1)
                        if b == 1 and i == 8:
                            dve.wait_ge(S["at_oT_psum"], 2)
                        if b == 0:
                            o.run(dve.tensor_copy(ot[:, qt, hd, :], psum[7][:, 0:P]), S["at_o_taken"])
                        else:
                            o.settle()
                            o.run(dve.tensor_scalar(ot[:, qt, hd, :], psum[7][:, 0:P], rec[:, 2 + qt:3 + qt], None,
                                                    ALU.mult), S["at_o_taken"])

                    def at_oT(b):
                        if b == 0:
                            o.settle()
                            dve.wait_ge(S["d_oT_psum"], TT)
                            sq = TMPD
                            o.step(dve.tensor_tensor(sq, ot, ot, ALU.mult))
                            o.step(dve.tensor_reduce(ss[:, 0:8], sq.rearrange("p t h d -> p (t h) d"), AX, ALU.add),
                                   S["a_ss_ready"])
                            dve.wait_ge(S["a_rs_ready"], 1)
                            v = ot.rearrange("p t h d -> p (t h) d")
                            o.step(dve.tensor_tensor(v, v, bc_row(rstd[:, 0:8], 8), ALU.mult))
                            o.run(dve.tensor_tensor(v, v, a_scale.unsqueeze(1).to_broadcast([P, 8, P]), ALU.mult),
                                  S["a_out_ready"])
                        else:
                            o.settle()
                            dve.sem_inc(S["a_out_ready"], 1)

                    def branch(j):
                        n, q = BRANCH_ORDER[j // 4], j % 4
                        split_lo(2 * U_BR + j + 3)
                        if j % 2 == 0:
                            dve.wait_ge(S["br_psum"], j // 2 + 1)
                        else:
                            dve.wait_ge(S["unit_done"], U_BR + j // 2 + 1)
                        src = psum[j % 2][:, :].rearrange("p (b t) -> p b t", b=2)
                        g = gates[:, KD * n + 2 * q:KD * n + 2 * q + 2, :]
                        a = acc[:, 2 * q:2 * q + 2, :]
                        if j == 0:
                            o.settle()
                            dve.wait_ge(S["proj_evac"], U_BR)
                            dve.wait_ge(S["at_o_psum"], 8)
                        if j < 4:
                            o.run(dve.scalar_tensor_tensor(a, g, 1.0, src, ALU.add, ALU.mult), S["br_taken"])
                        else:
                            o.settle()
                            o.run(dve.scalar_tensor_tensor(acc_tmp, g, 1.0, src, ALU.add, ALU.mult), S["br_taken"])
                            o.settle()
                            o.run(dve.tensor_tensor(a, a, acc_tmp, ALU.add),
                                  S["acc_ready"] if j >= 12 else None)
                        if j > 12:
                            acc_lo(q - 1)
                        if j == 15:
                            acc_lo(q)

                    def stage(m):
                        dve.wait_ge(S["st_hi_ready"], m + 1)
                        dve.wait_ge(S["c_out_ready"], 1)
                        hi, lo = staged[m % 2]
                        o.run(dve.tensor_tensor(lo, oT[BRANCH_ORDER[m]], hi.bitcast(F32), ALU.subtract),
                              S["st_lo_ready"])

                    def acc_lo(q):
                        dve.wait_ge(S["acc_ready"], q + 1)
                        dve.wait_ge(S["acc_hi_ready"], q + 1)
                        pair = (slice(None), slice(2 * q, 2 * q + 2), slice(None))
                        o.run(dve.tensor_tensor(x_lo[pair], acc[pair], x_hi[pair].bitcast(F32), ALU.subtract),
                              S["acc_lo_ready"])

                    def project_out(j):
                        split_lo(2 * (U_OUT + j) + 3)
                        split_lo(2 * (U_OUT + j) + 4)
                        dve.wait_ge(S["unit_done"], U_OUT + j + 1)
                        v = h[:, :, j * UC:(j + 1) * UC]
                        o.run(dve.scalar_tensor_tensor(v, psum[j % 2][:, :].rearrange("p (t c) -> p t c", t=TT), 0.5,
                                                       v, ALU.mult, ALU.add), S["f_out_taken"])

                    steps = {"stage": stage, "c_coef": c_coef, "c_scan": c_scan, "c_conv": c_conv,
                             "d_conv": d_conv, "c_gelu_arg": c_gelu_arg, "c_gelu": c_gelu, "d_silu": silu,
                             "proj": lambda j: split_lo(j + 3),
                             "norm": prepare, "c_gates": c_gates, "ba": ba_dve, "d_tok": d_tok,
                             "d_cum": d_cum, "d_kk": d_kk, "inv_x": inv_x, "d_ks": d_ks, "d_o": d_o, "at_s": at_s,
                             "at_o": at_o, "at_oT": at_oT, "branch": branch, "out": project_out}
                    for what, i in SCHED:
                        if what in steps:
                            steps[what](i)
                    o.settle()

        AHEAD = 2

        def over_chunks(eng, n, step):
            with eng.Fori(0, n // 2) as j:
                step(2 * j, 0, j)
                step(2 * j + 1, 1, j)
            if n % 2:
                step(n - 1, 0, n // 2)

        def load_chunk(sp, source, base, base_half):
            def step(c, half, j):
                sp.wait_ge(S["h13_psum"], base + c + 1)
                for i in range(2):
                    sp.dma_start(ffn_raw[3 * half + i], source(3 * c + i)).then_inc(slot_loaded[3 * half + i], 16)
                sp.wait_ge(S["w2_used"], base + c + 1)
                sp.dma_start(ffn_raw[3 * half + 2], source(3 * c + 2)).then_inc(slot_loaded[3 * half + 2], 16)
            return step

        def pe_chunks(pe, n, base, base_half, xT, width, product):
            def up(c, half, j):
                pe.wait_ge(S["f_hT_ready"], base + c + 1)
                for i in range(2):
                    pe.wait_ge(slot_loaded[3 * half + i], (base_half + j + 1) * 16)
                    w = ffn_raw[3 * half + i].rearrange("p (k c) -> p k c", k=KD)
                    for f in range(2):
                        for k in range(KD):
                            last = pe.matmul(psum[2 * half + i][:, f * width:(f + 1) * width],
                                             w[:, k, f * P:(f + 1) * P], xT[:, k, :], start=(k == 0),
                                             stop=(k == KD - 1))
                last.then_inc(S["h13_psum"], 1)

            def down(c, half, j, first=False, final=False):
                pe.wait_ge(S["f_hT_ready"], base + c + AHEAD + 1)
                pe.wait_ge(slot_loaded[3 * half + 2], (base_half + j + 1) * 16)
                w = ffn_raw[3 * half + 2].rearrange("p (f c) -> p f c", f=2)
                for f in range(2):
                    last = product(hT[half][:, f * width:(f + 1) * width], w[:, f, :], first and f == 0,
                                   final and f == 1)
                last.then_inc(S["w2_used"], 1)

            up(0, 0, 0)
            up(1, 1, 0)
            down(0, 0, 0, first=True)
            with pe.Fori(0, (n - 2) // 2) as j:
                up(2 * j + 2, 0, j + 1)
                down(2 * j + 1, 1, j)
                up(2 * j + 3, 1, j + 1)
                down(2 * j + 2, 0, j + 1)
            if n % 2:
                up(n - 1, 0, n // 2)
                down(n - 2, 1, n // 2 - 1)
                down(n - 1, 0, n // 2, final=True)
            else:
                down(n - 1, 1, n // 2 - 1, final=True)

        def act_chunk(act, base, width):
            def step(c, half, j):
                act.wait_ge(S["h13_psum"], base + c + AHEAD + 1)
                act.wait_ge(S["f_hT_ready"], base + c + 1)
                act.activation(fth[half][:, 0:2 * width], psum[2 * half][:, 0:2 * width], ACT.Tanh,
                               scale=0.5).then_inc(S["f_tanh"], 1)
            return step

        def dve_chunk(dve, base, width):
            def step(c, half, j):
                n = 2 * width
                dve.wait_ge(S["f_tanh"], base + c + 1)
                dve.scalar_tensor_tensor(fs[half][:, 0:n], fth[half][:, 0:n], 1.0, psum[2 * half][:, 0:n],
                                         ALU.add, ALU.mult).then_inc(S["f_h_ready"], 1)
                dve.wait_ge(S["w2_used"], base + c + 1)
                dve.wait_ge(S["f_h_ready"], base + c + 1)
                dve.tensor_tensor(hT[half][:, 0:n], fs[half][:, 0:n], psum[2 * half + 1][:, 0:n],
                                  ALU.mult).then_inc(S["f_hT_ready"], 1)
            return step

        def dense_block():
            with nc.Block() as block:
                @block.sync
                def _(sp):
                    over_chunks(sp, DENSE_CHUNKS, load_chunk(
                        sp, lambda u: dense_units[bass.ds(u, 1), :, :].rearrange("l p c -> p (l c)"), 0, 0))
                    sp.wait_ge(S["w2_used"], DENSE_CHUNKS + AHEAD)

                @block.tensor
                def _(pe):
                    pe.sem_inc(S["h13_psum"], AHEAD)
                    pe.sem_inc(S["w2_used"], AHEAD)
                    norm_pe(pe)
                    pe.wait_ge(S["xraw_ready"], 4)

                    def product(lhsT, w, first, final):
                        for t in range(TT):
                            for n in range(2):
                                last = pe.matmul(psum[4 + 2 * t + n][:, :], lhsT[:, t * P:(t + 1) * P],
                                                 w[:, n * 512:(n + 1) * 512], start=first, stop=final)
                        return last

                    pe_chunks(pe, DENSE_CHUNKS, 0, 0, xraw, SEQ, product)

                @block.scalar
                def _(act):
                    norm_act(act, Order(act, S["act_own"]))
                    over_chunks(act, DENSE_CHUNKS, act_chunk(act, 0, SEQ))

                @block.gpsimd
                def _(pool):
                    norm_pool(pool, Order(pool, S["pool_own"]))

                @block.vector
                def _(dve):
                    o = Order(dve, S["dve_own"])
                    dve.sem_inc(S["f_hT_ready"], AHEAD)
                    norm_dve(dve, o, par_of("norm_ffn"))
                    over_chunks(dve, DENSE_CHUNKS, dve_chunk(dve, 0, SEQ))
                    dve.wait_ge(S["w2_used"], DENSE_CHUNKS + AHEAD)
                    for t in range(TT):
                        for n in range(2):
                            v = h[:, t, n * 512:(n + 1) * 512]
                            o.run(dve.scalar_tensor_tensor(v, psum[4 + 2 * t + n][:, :], 0.5, v, ALU.mult, ALU.add))
                    o.settle()

        def moe_block():
            n = MOE_CHUNKS
            kinds = ("w1", "w3", "w2")

            def half_of(view, f):
                return view[:, f * UNIT // 2:(f + 1) * UNIT // 2]

            with nc.Block() as block:
                @block.sync
                def _(sp):
                    def load(row, i, slot):
                        sp.dma_start(ffn_raw[2 * i + slot], moe_units[row, :, :].rearrange("l p c -> p (l c)")
                                     ).then_inc(slot_loaded[2 * i + slot], 16)

                    def load_free(i, expert, c, q, slot):
                        sp.wait_ge(S[kinds[i] + "_lo"], 2 * q - 2)
                        load(bass.ds((expert * n + c) * 3 + i, 1), i, slot)

                    def load_next(expert, c, q, slot, expert2, c2):
                        load_free(2, expert, c, q, slot)
                        for i in range(2):
                            load_free(i, expert2, c2, q + 2, slot)

                    for c in range(2):
                        for i in range(3):
                            load(slice(3 * c + i, 3 * c + i + 1), i, c)
                    for i in range(2):
                        sp.wait_ge(S[kinds[i] + "_lo"], 2)
                        load(slice(6 + i, 7 + i), i, 0)
                    sp.wait_ge(S["table_ready"], 1)
                    total = sp.value_load(table_i[0:1, PASSES + 1:PASSES + 2], min_val=EXPERTS, max_val=PASSES)
                    with sp.Fori(0, PASSES) as p:
                        expert = sp.value_load(table_i[0:1, bass.ds(p, 1)], min_val=0, max_val=EXPERTS - 1)
                        after = sp.value_load(table_i[0:1, bass.ds(p + 1, 1)], min_val=0, max_val=EXPERTS - 1)
                        with sp.If(p < total):
                            q0 = p * n
                            for i in range(2):
                                load_free(i, expert, 3, q0 + 3, 1)
                            with sp.Fori(0, (n - 4) // 2) as j:
                                for k in range(2):
                                    c = 2 * j + 2 + k
                                    load_next(expert, c, q0 + c, k, expert, c + 2)
                            for k in range(2):
                                load_next(expert, n - 2 + k, q0 + n - 2 + k, k, after, k)
                            load_next(after, 0, q0 + n, 0, after, 2)
                            load_free(2, after, 1, q0 + n + 1, 1)
                        with sp.Else():
                            sp.nop()
                    for count, slots in ((1, (1, 3, 4, 5)), (2, (0, 2))):
                        for slot in slots:
                            sp.wait_ge(slot_loaded[slot], total * (n // 2 * 16) + count * 16)
                        sp.sem_inc(S["loads_over"], 1)

                @block.tensor
                def _(pe):
                    pe.sem_inc(S["w2_used"], 1)
                    norm_pe(pe)
                    pe.wait_ge(S["xraw_ready"], 4)
                    r = par_of("router").rearrange("p (k e) -> p k e", k=KD)
                    for t in range(TT):
                        for k in range(KD):
                            last = pe.matmul(psum[0][:, 8 * t:8 * t + 8], xraw[:, k, t * P:(t + 1) * P], r[:, k, :],
                                             start=(k == 0), stop=(k == KD - 1))
                    last.then_inc(S["rt_psum"], 1)
                    pe.wait_ge(S["rt_member"], 1)
                    m = member.rearrange("p (t e) -> p t e", t=TT)
                    pe.matmul(psum[1][:, 0:8], trix, m[:, 0, :], start=True, stop=True)
                    pe.matmul(psum[1][:, 8:16], ones, m[:, 0, :], start=True, stop=False)
                    pe.matmul(psum[1][:, 8:16], trix, m[:, 1, :], start=False, stop=True)
                    pe.matmul(psum[1][:, 16:24], ones, m[:, 0, :], start=True, stop=False)
                    pe.matmul(psum[1][:, 16:24], ones, m[:, 1, :], start=False, stop=True).then_inc(S["rank_psum"], 1)
                    pe.wait_ge(S["table_ready"], 1)
                    total = pe.value_load(table_i[0:1, PASSES + 1:PASSES + 2], min_val=EXPERTS, max_val=PASSES)

                    def gather(p):
                        for k in range(KD):
                            for t in range(TT):
                                last = pe.matmul(psum[6 + k // 4][:, (k % 4) * P:(k % 4 + 1) * P],
                                                 xs[:, t, k * P:(k + 1) * P], sel[:, t, :], start=(t == 0),
                                                 stop=(t == TT - 1))
                        last.then_inc(S["gather_psum"], 1)

                    def scatter(t, p):
                        pe.wait_ge(S["y_ready"], p * 2 + 2)
                        pe.wait_ge(S["selT_ready"], p + 1)
                        pe.wait_ge(S["scat_taken"], p * 4 + 2 * t + 2)
                        for m in range(2):
                            last = pe.matmul(psum[6 + m][:, :], selgT[:, t * P:(t + 1) * P],
                                             yexp[:, m * 512:(m + 1) * 512], start=True, stop=True)
                        last.then_inc(S["scat_psum"], 1)

                    def up(i, par_, q):
                        w = [v.rearrange("p (k c) -> p k c", k=KD) for v in w_parts[i]]
                        x = (xsel_hi, xsel_lo)
                        product3(pe, psum[par_ if i == 0 else 2][:, 0:CHUNK],
                                 lambda a, b, k: (x[b][:, k, :], w[a][:, k, :]), KD,
                                 S[kinds[i] + "_hi"], S[kinds[i] + "_lo"], q * 2 + 1
                                 ).then_inc(S[("h1_psum", "h3_psum")[i]], 1)

                    def turn(par_, q):
                        pe.wait_ge(S["f_h_ready"], q + 1)
                        for f in range(2):
                            last = pe.transpose(psum[3][:, f * P:(f + 1) * P], hf[par_][:, f * P:(f + 1) * P],
                                                ident)
                        last.then_inc(S["hT_psum"], 1)

                    def down(par_, q, first=False, final=False):
                        w = [v.rearrange("p (f c) -> p f c", f=2) for v in w_parts[2]]
                        x = (ht_hi[par_], ht_lo[par_])
                        pe.wait_ge(S["f_lo_ready"], q + 1)
                        for i, (a, b) in enumerate(((0, 0), (0, 1), (1, 0))):
                            for f in range(2):
                                if b == 0:
                                    pe.wait_ge(S["w2_lo" if a else "w2_hi"], q * 2 + f + 1)
                                for m in range(2):
                                    last = pe.matmul(psum[4 + m][:, :], x[b][:, f * P:(f + 1) * P],
                                                     w[a][:, f, m * 512:(m + 1) * 512],
                                                     start=first and i == 0 and f == 0, stop=final and i == 2 and f == 1)
                        last.then_inc(S["w2_used"], 1)

                    def step(par_, q):
                        up(0, par_, q)
                        turn(1 - par_, q - 1)
                        up(1, par_, q)
                        down(1 - par_, q - 1)

                    pe.wait_ge(S["sel_ready"], 1)
                    gather(0)
                    with pe.Fori(0, PASSES) as p:
                        with pe.If(p < total):
                            q0 = p * n
                            pe.wait_ge(S["xsel_lo_ready"], p * 2 + 2)
                            up(0, 0, q0)
                            scatter(0, p)
                            up(1, 0, q0)
                            scatter(1, p)
                            up(0, 1, q0 + 1)
                            turn(0, q0)
                            pe.wait_ge(S["scat_taken"], p * 4 + 6)
                            for t in range(TT):
                                last = pe.transpose(psum[6][:, t * P:(t + 1) * P], selg[:, t, :], ident)
                            last.then_inc(S["selT_psum"], 1)
                            up(1, 1, q0 + 1)
                            down(0, q0, first=True)
                            with pe.Fori(0, (n - 2) // 2) as j:
                                for k in range(2):
                                    step(k, q0 + 2 * j + 2 + k)
                            pe.wait_ge(S["sel_ready"], p + 2)
                            pe.wait_ge(S["selT_ready"], p + 2)
                            gather(p + 1)
                            turn(1, q0 + n - 1)
                            down(1, q0 + n - 1, final=True)
                        with pe.Else():
                            pe.nop()
                    for t in range(TT):
                        scatter(t, total)

                @block.scalar
                def _(act):
                    norm_act(act, Order(act, S["act_own"]))

                    def split_hi(i, q, slot, loads):
                        act.wait_ge(slot_loaded[2 * i + slot], loads * 16)
                        for f in range(2):
                            act.activation(half_of(w_parts[i][0], f), half_of(ffn_raw[2 * i + slot], f),
                                           ACT.Copy).then_inc(S[kinds[i] + "_hi"], 1)

                    for i in range(2):
                        split_hi(i, 0, 0, 1)
                    for m in range(2):
                        act.activation(yexp[:, m * 512:(m + 1) * 512], con[:, 0:512], ACT.Copy,
                                       scale=0.0).then_inc(S["y_ready"], 1)
                    act.activation(selgT, con[:, 0:SEQ], ACT.Copy, scale=0.0).then_inc(S["selT_ready"], 1)
                    act.wait_ge(S["rt_arg"], 1)
                    act.activation(em, dm, ACT.Exp).then_inc(S["rt_exp"], 1)
                    act.wait_ge(S["table_ready"], 1)
                    total = act.value_load(table_i[0:1, PASSES + 1:PASSES + 2], min_val=EXPERTS, max_val=PASSES)

                    def xsel_split(p):
                        for m in range(2):
                            act.wait_ge(S["xsel_ready"], p * 2 + m + 1)
                            act.activation(xsel_hi[:, 4 * m:4 * m + 4, :], xsel[:, 4 * m:4 * m + 4, :],
                                           ACT.Copy).then_inc(S["xsel_hi_ready"], 1)

                    def hidden_hi(par_, q):
                        act.wait_ge(S["hT_psum"], q + 1)
                        act.activation(ht_hi[par_], psum[3][:, 0:CHUNK], ACT.Copy).then_inc(S["f_hi_ready"], 1)

                    def step(par_, q, pairs, first=False, p=None):
                        act.wait_ge(S["h1_psum"], q + 1)
                        act.activation(fth[par_][:, 0:CHUNK], psum[par_][:, 0:CHUNK], ACT.Tanh,
                                       scale=0.5).then_inc(S["f_tanh"], 1)
                        if not first:
                            hidden_hi(1 - par_, q - 1)
                        split_hi(0, q + 1, 1 - par_, pairs + 1 + par_)
                        act.wait_ge(S["h3_psum"], q + 1)
                        split_hi(1, q + 1, 1 - par_, pairs + 1 + par_)
                        act.wait_ge(S["w2_used"], q + 1)
                        split_hi(2, q, par_, pairs + 1)

                    xsel_split(0)
                    with act.Fori(0, PASSES) as p:
                        with act.If(p < total):
                            q0, pairs = p * n, p * (n // 2)
                            step(0, q0, pairs, first=True)
                            step(1, q0 + 1, pairs)
                            act.wait_ge(S["selT_psum"], p + 1)
                            act.activation(selgT, psum[6][:, 0:SEQ], ACT.Copy).then_inc(S["selT_ready"], 1)
                            with act.Fori(0, (n - 2) // 2) as j:
                                for k in range(2):
                                    step(k, q0 + 2 * j + 2 + k, pairs + j + 1)
                            hidden_hi(1, q0 + n - 1)
                            xsel_split(p + 1)
                            act.wait_ge(S["w2_used"], q0 + n + 1)
                            for m in range(2):
                                act.activation(yexp[:, m * 512:(m + 1) * 512], psum[4 + m][:, :],
                                               ACT.Copy).then_inc(S["y_ready"], 1)
                        with act.Else():
                            act.nop()

                @block.gpsimd
                def _(pool):
                    norm_pool(pool, Order(pool, S["pool_own"]))
                    pool.wait_ge(S["table_ready"], 1)
                    total = pool.value_load(table_i[0:1, PASSES + 1:PASSES + 2], min_val=EXPERTS, max_val=PASSES)
                    with pool.Fori(0, PASSES) as p:
                        with pool.If(p < total):
                            with pool.Fori(0, n // 2) as j:
                                for k in range(2):
                                    for f in range(2):
                                        pool.wait_ge(S["w2_hi"], (p * n + 2 * j + k) * 2 + f + 1)
                                        pool.tensor_tensor(half_of(w_parts[2][1], f), half_of(ffn_raw[4 + k], f),
                                                           half_of(w_parts[2][0], f).bitcast(F32),
                                                           ALU.subtract).then_inc(S["w2_lo"], 1)
                        with pool.Else():
                            pool.nop()

                @block.vector
                def _(dve):
                    o = Order(dve, S["dve_own"])
                    dve.sem_inc(S["scat_taken"], 2)
                    norm_dve(dve, o, par_of("norm_ffn"))
                    o.settle()
                    eidx = con[:, C_EIDX:C_EIDX + EXPERTS]
                    erev = con[:, C_EREV:C_EREV + EXPERTS]

                    def te(c):
                        return c.rearrange("p (t e) -> p t e", t=TT)

                    def each_t(row):
                        return row.unsqueeze(1).to_broadcast([P, TT, EXPERTS])

                    def each_e(c):
                        return c.unsqueeze(2).to_broadcast([P, TT, EXPERTS])

                    def best(src, value, chosen):
                        o.step(dve.tensor_reduce(value, te(src), AX, ALU.max))
                        o.step(dve.tensor_tensor(te(eq), te(src), each_e(value), ALU.is_equal))
                        o.step(dve.tensor_tensor(te(eq), te(eq), each_t(erev), ALU.mult))
                        o.step(dve.tensor_reduce(fi, te(eq), AX, ALU.max))
                        o.step(dve.tensor_tensor(te(chosen), each_t(erev), each_e(fi), ALU.is_equal))

                    dve.wait_ge(S["rt_psum"], 1)
                    o.step(dve.tensor_copy(lg, psum[0][:, 0:16]))
                    best(lg, m0, one1)
                    o.step(dve.scalar_tensor_tensor(lg, one1, -3.0e38, lg, ALU.mult, ALU.add))
                    best(lg, m1, one2)
                    o.run(dve.tensor_tensor(member, one1, one2, ALU.add), S["rt_member"])
                    o.step(dve.tensor_tensor(dm, m1, m0, ALU.subtract), S["rt_arg"])
                    dve.wait_ge(S["rt_exp"], 1)
                    o.step(dve.tensor_scalar(p0, em, 1.0, None, ALU.add))
                    o.step(dve.reciprocal(p0, p0))
                    o.step(dve.tensor_tensor(p1, em, p0, ALU.mult))
                    o.step(dve.tensor_tensor(te(one1), te(one1), each_e(p0), ALU.mult))
                    o.step(dve.tensor_tensor(te(one2), te(one2), each_e(p1), ALU.mult))
                    o.step(dve.tensor_tensor(gsel, one1, one2, ALU.add))
                    dve.wait_ge(S["rank_psum"], 1)
                    o.step(dve.scalar_tensor_tensor(vslot, psum[1][:, 0:16], 1.0, member, ALU.add, ALU.mult))
                    o.step(dve.tensor_scalar(vslot, vslot, -1.0, None, ALU.add))
                    o.step(dve.tensor_scalar(over, psum[1][:, 16:24], float(P), None, ALU.is_gt))
                    o.step(dve.memset(onesE, 1.0))
                    o.step(dve.tensor_tensor_scan(incl, onesE, over, 0.0, ALU.mult, ALU.add))
                    o.step(dve.tensor_tensor(pos, incl, over, ALU.subtract))
                    so = slot_of.rearrange("p (t q) -> p t q", t=TT)
                    go = gate_of.rearrange("p (t q) -> p t q", t=TT)
                    o.run(dve.tensor_copy(so[:, :, 0:EXPERTS], te(vslot)))
                    o.run(dve.tensor_copy(go[:, :, 0:EXPERTS], te(gsel)))
                    o.run(dve.tensor_copy(table[:, 0:EXPERTS], eidx))
                    o.run(dve.memset(so[:, :, PASSES:PASSES + 1], -1.0))
                    o.run(dve.memset(go[:, :, PASSES:PASSES + 1], 0.0))
                    o.run(dve.memset(table[:, PASSES:PASSES + 1], 0.0))
                    o.run(dve.tensor_scalar(table[:, PASSES + 1:PASSES + 2], incl[:, EXPERTS - 1:EXPERTS], float(EXPERTS),
                                            None, ALU.add))
                    for q in range(OVERFLOWS):
                        sq = selq[:, q * EXPERTS:(q + 1) * EXPERTS]
                        o.step(dve.scalar_tensor_tensor(sq, pos, float(q), over, ALU.is_equal, ALU.mult))
                        o.step(dve.tensor_tensor(tmp8, sq, eidx, ALU.mult))
                        o.step(dve.tensor_reduce(table[:, EXPERTS + q:EXPERTS + q + 1], tmp8, AX, ALU.add))
                        for src, dst, shift in ((vslot, so, -float(P)), (gsel, go, 0.0)):
                            o.step(dve.tensor_tensor(te(pick), te(src), each_t(sq), ALU.mult))
                            o.step(dve.tensor_reduce(fi, te(pick), AX, ALU.add))
                            o.step(dve.tensor_scalar(dst[:, :, EXPERTS + q], fi, shift, None, ALU.add))
                    o.settle()
                    o.step(dve.tensor_copy(table_i[:, :], table), S["table_ready"])
                    total = dve.value_load(table_i[0:1, PASSES + 1:PASSES + 2], min_val=EXPERTS, max_val=PASSES)
                    iota = con[:, C_IOTA:C_IOTA + P]
                    gain = par_of("norm_ffn")

                    def select(p):
                        for t in range(TT):
                            dve.tensor_scalar(sel[:, t, :], iota, so[:, t, bass.ds(p, 1)], None, ALU.is_equal)
                        for t in range(TT):
                            ins = dve.tensor_scalar(selg[:, t, :], iota, so[:, t, bass.ds(p, 1)],
                                                    go[:, t, bass.ds(p, 1)], ALU.is_equal, ALU.mult)
                        ins.then_inc(S["sel_ready"], 1)

                    def xsel_gain(p):
                        dve.wait_ge(S["gather_psum"], p + 1)
                        for m in range(2):
                            dve.tensor_tensor(xsel[:, 4 * m:4 * m + 4, :],
                                              psum[6 + m][:, :].rearrange("p (k s) -> p k s", k=4),
                                              gain[:, 4 * m:4 * m + 4].unsqueeze(2).to_broadcast([P, 4, P]),
                                              ALU.mult).then_inc(S["xsel_ready"], 1)

                    def xsel_split(p):
                        for m in range(2):
                            dve.wait_ge(S["xsel_hi_ready"], p * 2 + m + 1)
                            cut = (slice(None), slice(4 * m, 4 * m + 4), slice(None))
                            dve.tensor_tensor(xsel_lo[cut], xsel[cut], xsel_hi[cut].bitcast(F32),
                                              ALU.subtract).then_inc(S["xsel_lo_ready"], 1)

                    def split_lo(i, q, slot):
                        for f in range(2):
                            dve.wait_ge(S[kinds[i] + "_hi"], q * 2 + f + 1)
                            dve.tensor_tensor(half_of(w_parts[i][1], f), half_of(ffn_raw[2 * i + slot], f),
                                              half_of(w_parts[i][0], f).bitcast(F32),
                                              ALU.subtract).then_inc(S[kinds[i] + "_lo"], 1)

                    def hidden_lo(par_, q):
                        dve.wait_ge(S["f_hi_ready"], q + 1)
                        dve.tensor_tensor(ht_lo[par_], psum[3][:, 0:CHUNK], ht_hi[par_].bitcast(F32),
                                          ALU.subtract).then_inc(S["f_lo_ready"], 1)

                    def scatter_add(t, p):
                        dve.wait_ge(S["scat_psum"], p * 2 + t + 1)
                        for m in range(2):
                            v = h[:, t, m * 512:(m + 1) * 512]
                            dve.scalar_tensor_tensor(v, psum[6 + m][:, :], 0.5, v, ALU.mult,
                                                     ALU.add).then_inc(S["scat_taken"], 1)

                    def step(par_, q, first_pass=None):
                        dve.wait_ge(S["f_tanh"], q + 1)
                        dve.scalar_tensor_tensor(fs[par_][:, 0:CHUNK], fth[par_][:, 0:CHUNK], 1.0,
                                                 psum[par_][:, 0:CHUNK], ALU.add, ALU.mult
                                                 ).then_inc(S["f_s_ready"], 1)
                        if first_pass is None:
                            hidden_lo(1 - par_, q - 1)
                        split_lo(0, q + 1, 1 - par_)
                        if first_pass is not None:
                            scatter_add(0, first_pass)
                        dve.wait_ge(S["h3_psum"], q + 1)
                        dve.wait_ge(S["f_s_ready"], q + 1)
                        dve.tensor_tensor(hf[par_], fs[par_][:, 0:CHUNK], psum[2][:, 0:CHUNK],
                                          ALU.mult).then_inc(S["f_h_ready"], 1)
                        split_lo(1, q + 1, 1 - par_)
                        if first_pass is not None:
                            scatter_add(1, first_pass)

                    select(0)
                    for i in range(2):
                        split_lo(i, 0, 0)
                    xsel_gain(0)
                    xsel_split(0)
                    with dve.Fori(0, PASSES) as p:
                        with dve.If(p < total):
                            q0 = p * n
                            step(0, q0, first_pass=p)
                            step(1, q0 + 1)
                            dve.wait_ge(S["gather_psum"], p + 1)
                            dve.wait_ge(S["selT_psum"], p + 1)
                            select(p + 1)
                            with dve.Fori(0, (n - 2) // 2) as j:
                                for k in range(2):
                                    step(k, q0 + 2 * j + 2 + k)
                            xsel_gain(p + 1)
                            hidden_lo(1, q0 + n - 1)
                            xsel_split(p + 1)
                        with dve.Else():
                            dve.nop()
                    for t in range(TT):
                        scatter_add(t, total)

        with nc.Fori(0, LAYERS) as layer:
            mixer_block(layer)
            clear_semaphores()
            with nc.If(layer < 1):
                dense_block()
            with nc.Else():
                moe_block()
            clear_semaphores()

        with nc.Block() as block:
            gain_row = raw[0][:, 0:DM]

            @block.sync
            def _(sp):
                sp.dma_start(gain_row, norm_final).then_inc(S["in_loaded"], 16)
                for t in range(TT):
                    sp.wait_ge(S["xs_ready"], t + 1)
                    sp.dma_start(out[t * P:(t + 1) * P, :], xs[:, t, :]).then_inc(S["out_stored"], 16)
                sp.wait_ge(S["out_stored"], TT * 16)

            @block.scalar
            def _(act):
                norm_act(act, Order(act, S["act_own"]))

            @block.gpsimd
            def _(pool):
                norm_pool(pool, Order(pool, S["pool_own"]))

            @block.vector
            def _(dve):
                dve.wait_ge(S["in_loaded"], 16)
                dve.wait_ge(S["rstd_ready"], 1)
                for t in range(TT):
                    dve.scalar_tensor_tensor(xs[:, t, :], h[:, t, :], rstd[:, t:t + 1], gain_row, ALU.mult,
                                             ALU.mult).then_inc(S["xs_ready"], 1)


def _constants(np):
    c = np.zeros((P, C_COLS), np.float32)
    j, i = np.arange(P)[:, None], np.arange(P)[None, :]
    c[:, C_IDENT:C_IDENT + P] = j == i
    c[:, C_ONES:C_ONES + P] = 1
    c[:, C_TRI:C_TRI + P] = j <= i
    c[:, C_TRIX:C_TRIX + P] = j < i
    c[:, C_CAUSAL + P:C_CAUSAL + 2 * P] = np.where(i <= j, 0, NEG)
    c[:, C_NEGT:C_NEGT + P] = np.where(j <= i, 0, NEG)
    for s in range(LEVELS):
        size = 1 << s
        c[:, C_LEVEL + s * P:C_LEVEL + (s + 1) * P] = (i // size % 2 == 1) & (j // size == i // size - 1)
    c[:, C_IOTA:C_IOTA + P] = i
    c[:, C_EIDX:C_EIDX + EXPERTS] = np.arange(EXPERTS)
    c[:, C_EREV:C_EREV + EXPERTS] = EXPERTS - np.arange(EXPERTS)
    c[:, C_HALF:] = -0.5
    return c


def _units(np, w, cols):
    rows, n = w.shape
    return w.reshape(rows // P, P, n // cols, cols).transpose(2, 1, 0, 3).reshape(n // cols, P, -1)


def _chunks(np, w1, w3, w2):
    a, b = _units(np, w1, CHUNK), _units(np, w3, CHUNK)
    c = w2.reshape(-1, CHUNK // P, P, DM).transpose(0, 2, 1, 3).reshape(a.shape[0], P, -1)
    return np.stack([a, b, c], 1).reshape(-1, P, UNIT)


def _layer_params(np, v, layer):
    parts = {}

    def channels(a, n):
        return a.reshape(n, P, -1).transpose(1, 0, 2).reshape(P, -1)

    def rows(a):
        return np.broadcast_to(a.reshape(1, -1), (P, a.size))

    lam_init = 0.8 - 0.6 * math.exp(-0.3 * layer)
    parts["norm_mix"] = channels(v["norm_mix"][layer], KD)
    parts["norm_ffn"] = channels(v["norm_ffn"][layer], KD)
    parts["c_conv_w"] = channels(v["c_conv_w"][layer].T, NB)
    parts["c_conv_b"] = channels(v["c_conv_b"][layer], NB)
    parts["c_b_a"] = channels(v["c_b_a"][layer].reshape(-1), NB)
    parts["c_b_x"] = channels(v["c_b_x"][layer].reshape(-1), NB)
    parts["c_lambda"] = channels(v["c_lambda"][layer], NB)
    parts["d_conv_w"] = channels(v["d_conv_w"][layer].T, 3 * NB)
    parts["b_gate"] = channels(v["b_gate"][layer].reshape(-1), BRANCHES * KD)
    parts["a_subln"] = rows(v["a_subln"][layer])
    parts["d_norm"] = rows(v["d_norm"][layer])
    parts["lam"] = rows(np.stack([v[n][layer] for n in ("lam_q1", "lam_k1", "lam_q2", "lam_k2")]))
    parts["d_A_log"] = rows(v["d_A_log"][layer])
    parts["d_dt_bias"] = rows(v["d_dt_bias"][layer])
    parts["w_ba"] = channels(v["w_in"][layer][:, 12 * MIX:], KD)
    parts["lam_init"] = np.full((P, 1), lam_init, np.float32)
    parts["out_scale"] = np.full((P, 1), 1.0 - lam_init, np.float32)
    moe = layer % 2 == 1
    parts["router"] = channels(v["router"][layer // 2], KD) if moe else np.zeros((P, KD * EXPERTS), np.float32)
    return np.concatenate([parts[n] for n, _ in PARTS], 1)


def kernel(**inputs):
    import numpy as np
    import concourse.bacc as bacc
    from concourse.bass_utils import run_bass_kernel_spmd

    v = {k: np.asarray(a) for k, a in inputs.items()}
    arrays = {"x": v["x"].reshape(SEQ, DM), "consts": _constants(np),
              "params": np.stack([_layer_params(np, v, layer) for layer in range(LAYERS)])}
    cd = np.zeros((LAYERS, P, 2, NB, P), np.float32)
    for g, name in enumerate(("c_w_a", "c_w_x")):
        w = v[name].reshape(LAYERS, NB, 2, 64, 64)
        for half in range(2):
            s = slice(64 * half, 64 * half + 64)
            cd[:, s, g, :, s] = w[:, :, half].transpose(0, 2, 1, 3)
    arrays["cdiag"] = cd.reshape(LAYERS, P, -1)
    mix = []
    for layer in range(LAYERS):
        w_in = _units(np, v["w_in"][layer][:, :12 * MIX], UC)
        per = MIX // UC
        order = [b * per + i for b in (6, 7, 8, 9, 10, 11, 0, 1, 2, 3, 4, 5) for i in range(per)]
        mix += [w_in[order], _units(np, v["w_gate"][layer].reshape(DM, -1), UC)]
        mix += [_units(np, v["w_branch"][layer][n], 2 * UC) for n in BRANCH_ORDER]
        mix += [_units(np, v["w_out"][layer], UC)]
    arrays["mix_units"] = np.concatenate(mix).reshape(LAYERS, MIX_UNITS, P, UNIT)
    arrays["dense_units"] = _chunks(np, v["ffn_w1"][0], v["ffn_w3"][0], v["ffn_w2"][0])
    arrays["moe_units"] = np.concatenate([_chunks(np, v["moe_w1"][0][e], v["moe_w3"][0][e], v["moe_w2"][0][e])
                                          for e in range(EXPERTS)])
    arrays["norm_final"] = np.ascontiguousarray(np.broadcast_to(v["norm_final"][None], (P, DM)))

    nc = bacc.Bacc("TRN2", target_bir_lowering=False, num_devices=1)
    aps = {n: nc.dram_tensor(n, a.shape, F32, kind="ExternalInput").ap() for n, a in arrays.items()}
    out = nc.dram_tensor("out", (SEQ, DM), F32, kind="ExternalOutput").ap()
    hybrid_trunk(nc, **aps, out=out)
    got = run_bass_kernel_spmd(nc, [arrays], core_ids=[0])
    return got.results[0]["out"].reshape(1, SEQ, DM)
```

```python
import math
from contextlib import ExitStack

import concourse.bass as bass
from concourse import mybir

F32 = mybir.dt.float32
F32R = mybir.dt.float32r
I32 = mybir.dt.int32
ALU = mybir.AluOpType
ACT = mybir.ActivationFunctionType
AX = mybir.AxisListType.X

P = 128
LAYERS, SEQ, DM = 2, 256, 1024
TT = SEQ // P
KD = DM // P
MIX = 512
NB = MIX // P
HEADS = 4
BRANCHES = 4
TAPS = 4
UC = 256
UNIT = KD * UC
MIX_SLOTS, FFN_SLOTS = 2, 6
NEG = -1.0e30
LRU_C = 8.0
EXPERTS, TOP_K = 8, 2
FFN, FFE = 2816, 3584
CHUNK = UC
DENSE_CHUNKS, MOE_CHUNKS = FFN // CHUNK, FFE // CHUNK
OVERFLOWS = (TOP_K * SEQ) // (P + 1)
PASSES = EXPERTS + OVERFLOWS

U_C, U_D, U_Z, U_A, U_B, U_GATE = 0, 4, 10, 12, 18, 24
U_BR = U_GATE + BRANCHES * DM // UC
U_OUT = U_BR + BRANCHES * 2
MIX_UNITS = U_OUT + DM // UC
BRANCH_ORDER = (2, 0, 1, 3)
ATTN = 2 * HEADS * TT

LEVELS = 7

C_IDENT, C_ONES, C_TRI, C_TRIX, C_CAUSAL, C_NEGT = 0, 128, 256, 384, 512, 768
C_LEVEL = 896
C_IOTA = C_LEVEL + LEVELS * P
C_EIDX, C_EREV = C_IOTA + P, C_IOTA + P + EXPERTS
C_HALF = C_EREV + EXPERTS
C_COLS = C_HALF + 32

PARTS = [("norm_mix", KD), ("norm_ffn", KD), ("c_conv_w", NB * TAPS), ("c_conv_b", NB),
         ("c_b_a", NB), ("c_b_x", NB), ("c_lambda", NB), ("d_conv_w", 3 * NB * TAPS),
         ("b_gate", BRANCHES * KD), ("a_subln", P), ("d_norm", P), ("lam", 256),
         ("d_A_log", HEADS), ("d_dt_bias", HEADS), ("w_ba", KD * 8), ("lam_init", 1),
         ("out_scale", 1), ("router", KD * EXPERTS)]
PCOL, _at = {}, 0
for _name, _n in PARTS:
    PCOL[_name] = (_at, _n)
    _at += _n
P_COLS = _at


class Order:

    def __init__(self, eng, own):
        self.eng, self.own, self.count, self.open = eng, own, {}, []

    def run(self, ins, sem=None):
        sem = self.own if sem is None else sem
        ins.then_inc(sem, 1)
        self.count[sem.name] = self.count.get(sem.name, 0) + 1
        if sem not in self.open:
            self.open.append(sem)

    def settle(self):
        for sem in self.open:
            self.eng.wait_ge(sem, self.count[sem.name])
        self.open = []

    def step(self, ins, sem=None):
        self.run(ins, sem)
        self.settle()


def mixer_schedule():
    wait = ("-", 0)
    chain = [("d_tok", 0), wait, ("d_tok", 1), wait, ("d_back", 0), ("d_cum", 0), wait, ("d_kk", 0)]
    for s in range(LEVELS):
        chain += [("inv_p", s), ("inv_x", s)]
    chain += [("d_v0", 0), ("d_s", 0), ("d_ks", 0), ("d_v1", 0), ("d_o", 0), wait, wait, ("d_oT", 0)]
    attn = [[("attn", i)] for i in range(ATTN + 3)]
    last_a = ATTN // 2 - 1 + 3
    attn[last_a + 1].append(("a_sq", 0))
    attn[last_a + 3].append(("a_scale", 0))
    attn[last_a + 5].append(("at_oT", 0))
    attn += [[("at_oT", 1)]]
    at_half = {2 * U_Z: [("ba", 0)]}

    def put(half, *steps):
        for i, step in enumerate(steps):
            at_half.setdefault(half + i, []).append(step)

    put(3, ("lambdas", 0))
    put(4, *[("c_conv", tap) for tap in range(TAPS)])
    put(10, ("c_gates", 0), ("c_decay", 0), ("c_coef", 0), ("c_scan", 0))
    put(8, ("c_gelu_arg", 0), ("c_gelu_tanh", 0), ("c_gelu", 0))
    for g in range(3):
        put(2 * (U_D + 2 + 2 * g), *[("d_conv", TAPS * g + tap) for tap in range(TAPS)])
    for g in range(2):
        put(2 * (U_D + 4 + 2 * g), ("d_tanh", g), ("d_silu", g))
    out = [("norm", 0)]
    for half in range(2 * U_BR):
        out += at_half.get(half, [])
        if half >= 2 * U_A and chain:
            out.append(chain.pop(0))
        elif half >= 2 * U_GATE and attn:
            out += attn.pop(0)
        if half == 2 * U_BR - 1:
            out.append(("stage", 0))
        out.append(("proj", half))
    for left in attn:
        out += left
    for j in range(BRANCHES * 4):
        out.append(("branch", j))
        if j % 4 == 0 and j < 12:
            out.append(("stage", j // 4 + 1))
    out += [("out", j) for j in range(DM // UC)]
    return out


def lo_by_pool(u):
    return 2 <= u < U_A or u > U_GATE


def lo_count(half):
    return sum(1 for i in range(half + 1) if lo_by_pool(i // 2) == lo_by_pool(half // 2))


def product3(pe, out, operands, n, hi_ready=None, lo_ready=None, count=None, lo_at=None):
    if lo_at is None:
        lo_at = count
    for i, (a, b) in enumerate(((0, 0), (0, 1), (1, 0))):
        for k in range(n):
            if k % (n // 2) == 0 and b == 0 and count is not None:
                pe.wait_ge(lo_ready if a else hi_ready, (lo_at if a else count) + k // (n // 2))
            lhsT, rhs = operands(a, b, k)
            last = pe.matmul(out, lhsT, rhs, start=(i == 0 and k == 0), stop=(i == 2 and k == n - 1))
    return last


def hybrid_trunk(nc, x, consts, params, cdiag, mix_units, dense_units, moe_units, norm_final, out):
    with ExitStack() as ctx:
        def sb(name, shape, dt=F32):
            return ctx.enter_context(nc.sbuf_tensor(name, shape, dt))

        sem_list = []

        def sem(name):
            s = ctx.enter_context(nc.semaphore(name))
            sem_list.append(s)
            return s

        con = sb("con", [P, C_COLS])
        par = sb("par", [P, P_COLS])
        h = sb("h", [P, TT, DM])
        raw = [sb(f"raw{i}", [P, UNIT])[:, :] for i in range(MIX_SLOTS)]
        w_hi = [sb(f"w_hi{i}", [P, UNIT])[:, :].bitcast(F32R) for i in range(2)]
        w_lo = [sb(f"w_lo{i}", [P, UNIT])[:, :].bitcast(F32R) for i in range(2)]
        x_hi, x_lo = (sb(n, [P, KD, SEQ])[:, :, :].bitcast(F32R) for n in ("x_hi", "x_lo"))
        st_hi, st_lo = (sb(n, [P, 4 * SEQ])[:, :].bitcast(F32R) for n in ("st_hi", "st_lo"))
        ht_hi, ht_lo = ([v[:, i * CHUNK:(i + 1) * CHUNK].bitcast(F32R) for i in range(2)]
                        for v in (sb("ht_hi", [P, 2 * CHUNK]), sb("ht_lo", [P, 2 * CHUNK])))
        small = sb("small", [P, 512])
        gates = sb("gates", [P, BRANCHES * KD, SEQ])
        oT_c = sb("oT_c", [P, NB, SEQ])
        work_c = sb("work_c", [P, 6, NB, SEQ])
        work_d = sb("work_d", [P, 12 * (SEQ + 3)])
        work_e = sb("work_e", [P, 3, NB * SEQ])
        dcv = sb("dcv", [P, 12, SEQ])
        zt = sb("zt", [P, TT, MIX])
        dexp = sb("dexp", [P, TT, HEADS, P])
        sm = sb("sm", [P, 2, 2, SEQ])
        wT = sb("wT", [P, 2, SEQ])

        def in_gates(b0, b1):
            return gates[:, b0:b1, :].rearrange("p k t -> p (k t)")

        xs = in_gates(0, 8).rearrange("p (a d) -> p a d", a=TT)
        xraw = gates[:, 8:16, :]
        cgate = gates[:, 16:20, :]
        cdg = in_gates(20, 24).rearrange("p (g c) -> p g c", g=8)
        cpad = in_gates(24, 29)[:, 0:NB * (SEQ + 3)].rearrange("p (b t) -> p b t", b=NB)
        dtmp, dusel = (in_gates(b, b + 4).rearrange("p (t h d) -> p t h d", t=TT, h=HEADS) for b in (24, 28))
        ot = zt[:, :, :].rearrange("p t (h d) -> p t h d", h=HEADS)

        banks_all = ctx.enter_context(nc.psum_tensor("banks_all", [P, 8, 512], F32))
        psum = [banks_all[:, i, :] for i in range(8)]

        ident = con[:, C_IDENT:C_IDENT + P]
        ones = con[:, C_ONES:C_ONES + P]
        tri = con[:, C_TRI:C_TRI + P]
        trix = con[:, C_TRIX:C_TRIX + P]
        neg_t = con[:, C_NEGT:C_NEGT + P]

        def par_of(name):
            a, n = PCOL[name]
            return par[:, a:a + n]

        c_xc, c_r, c_i, c_a, c_t, c_g = (work_c[:, i, :, :] for i in range(6))
        aq, ak, bq, bk = (work_c[:, i, :, :] for i in (0, 1, 3, 4))
        av, bv = (work_c[:, i, :, :].rearrange("p b t -> p (b t)").rearrange("p (a d) -> p a d", a=TT)
                  for i in (2, 5))
        acc = work_c[:, 0:2, :, :].rearrange("p a b t -> p (a b) t")
        acc_tmp = work_c[:, 2, 0:2, :]
        dpad = work_d[:, :].rearrange("p (b t) -> p b t", b=12)

        def heads_of(view):
            return view.rearrange("p (t h d) -> p t h d", t=TT, h=HEADS)

        SZ = TT * HEADS * P
        dX, dY, dP = (heads_of(work_d[:, i * SZ:(i + 1) * SZ]) for i in range(3))
        ot_b = dX
        dth = work_e[:, :, :]
        ktok, vtok, dU = (heads_of(work_e[:, i, :]) for i in range(3))
        qtok = heads_of(work_d[:, 0:SZ])
        dK = dcv[:, 4:8, :]
        dQ = dcv[:, 0:4, :]
        tail = dcv[:, 8:12, :].rearrange("p b t -> p (b t)")
        dR = tail[:, 0:512].rearrange("p (h d) -> p h d", h=HEADS)
        dS = tail[:, 512:1024].rearrange("p (h d) -> p h d", h=HEADS)
        oT = [view.rearrange("p (b t) -> p b t", b=NB) if view is not None else oT_c[:, :, :]
              for view in (work_e[:, 0, :], work_e[:, 1, :], None, work_e[:, 2, :])]
        staged = [tuple(v.rearrange("p (b t) -> p b t", b=NB) for v in (st_hi, st_lo)),
                  (x_hi[:, 0:NB, :], x_lo[:, 0:NB, :])]
        acc_parts = [tuple(v[:, 2 * q:2 * q + 2, :] for v in (staged[0] if q < 2 else (x_hi, x_lo)))
                     for q in range(4)]
        ffn_raw = raw + [work_c[:, 2 * i:2 * i + 2, :, :].rearrange("p a b t -> p (a b t)") for i in range(3)]
        ffn_raw += [dcv[:, 0:8, :].rearrange("p b t -> p (b t)")]
        fth = [in_gates(28, 32)[:, i * 512:(i + 1) * 512] for i in range(2)]
        fs = [in_gates(24, 28)[:, i * 512:(i + 1) * 512] for i in range(2)]
        hf = [zt[:, i, 0:CHUNK] for i in range(2)]
        w_parts = [(w_hi[0], w_lo[0]), (w_hi[1], w_lo[1]),
                   tuple(v.rearrange("p k t -> p (k t)") for v in (x_hi, x_lo))]
        xsel_hi, xsel_lo = (v.rearrange("p (k s) -> p k s", k=KD) for v in (st_hi, st_lo))
        sel = sm[:, 0, :, 0:P]
        selg = sm[:, 1, :, 0:P]
        selgT = wT[:, 0, :]
        xsel = in_gates(16, 20).rearrange("p (k s) -> p k s", k=KD)
        yexp = in_gates(20, 24)

        at = [0]

        def cols(n):
            at[0] += n
            return small[:, at[0] - n:at[0]]

        ss, rstd, rtmp = cols(16), cols(16), cols(16)
        half_b, half_ba, half_bx = cols(32), cols(NB), cols(NB)
        sp_z, sp_y, sp_s, sp_s2, sp_p = cols(8), cols(8), cols(8), cols(8), cols(8)
        lru, nlru = cols(NB), cols(NB)
        lam_prod, lam_sum, lam_e, lam_neg = cols(P), cols(2), cols(2), cols(1)
        ba, beta, expA, dg = cols(16), cols(8), cols(4), cols(8)
        gcum, darg, dfac = cols(8), cols(16), cols(16)
        a_scale_row = cols(P)
        mx, nmx, sums, rec, rec2 = (cols(2) for _ in range(5))
        rec_b = cols(4)
        assert at[0] <= 512
        at2 = [0]

        def cols2(n):
            at2[0] += n
            return work_d[:, at2[0] - n:at2[0]]

        lg, eq, one1, one2, pick, gsel, member, vslot = (cols2(16) for _ in range(8))
        m0, m1, dm, em, p0, p1, fi = (cols2(2) for _ in range(7))
        cnt, over, pos, incl, tmp8, onesE = (cols2(EXPERTS) for _ in range(6))
        selq = cols2(OVERFLOWS * EXPERTS)
        slot_of, gate_of = cols2(TT * (PASSES + 1)), cols2(TT * (PASSES + 1))
        table = cols2(PASSES + 2)
        table_i = sb("table_i", [P, PASSES + 2], I32)

        names = """in_loaded small_loaded act_own dve_own pool_own
            sumsq_ready rstd_ready xs_ready xT_psum xraw_ready x_hi_ready x_lo_ready
            unit_hi unit_lo unit_lo_pool unit_done proj_evac st_hi_ready st_lo_ready acc_hi_ready acc_lo_ready
            sp_arg sp_exp c_conv_ready c_gates_psum c_tanh c_a_t c_coef c_sqrt c_gelu_arg c_gelu_tanh
            ba_psum ba_cols ba_act dg_ready
            d_conv_ready d_tanh_ready d_silu_ready d_tok_psum d_tok_ready d_ss_ready d_rs_ready
            d_unit_ready d_back_psum d_T_ready d_cum_psum d_args_ready d_exp_ready d_ub_ready
            d_kk_psum d_u_ready dusel_ready inv_p_psum inv_p_ready inv_x_psum xy_ready
            r0_ready v0_psum v0_ready s_psum s_ready ks_psum ks_taken r1_ready v1_psum v1_ready
            o_psum o_ss_ready o_rs_ready z_tanh d_out_ready d_oT_psum
            at_s_psum at_s_taken at_max_ready at_exp_ready at_w_ready at_t_psum at_t_ready at_o_psum
            at_o_taken a_ss_ready a_rs_ready a_out_ready at_oT_psum lam_arg lam_exp
            c_out_ready oA_ready oB_ready oD_ready br_psum br_taken acc_ready
            f_tanh f_h_ready w2_used f_out_taken
            h1_psum h3_psum hT_psum f_s_ready f_hi_ready f_lo_ready
            loads_over w1_hi w1_lo w3_hi w3_lo w2_hi w2_lo xsel_ready xsel_hi_ready xsel_lo_ready
            rt_psum rt_arg rt_exp rt_member rank_psum table_ready
            sel_ready gather_psum selT_psum selT_ready y_ready scat_psum scat_taken out_stored"""
        S = {}
        for name in names.split():
            S[name] = sem(name)
        slot_loaded = [sem(f"slot_loaded{i}") for i in range(FFN_SLOTS)]

        def clear_semaphores():
            nums = sorted(s.num for s in sem_list)
            assert nums == list(range(nums[0], nums[-1] + 1))
            with nc.Block() as block:
                @block.sync
                def _(sp):
                    sp.sem_clear(range(nums[0], nums[-1] + 1))

        with nc.Block() as block:
            @block.sync
            def _(sp):
                sp.dma_start(con[:, :], consts).then_inc(S["in_loaded"], 16)
                sp.dma_start(h[:, :, :], x.rearrange("(t p) d -> p t d", p=P)).then_inc(S["in_loaded"], 16)
                sp.wait_ge(S["in_loaded"], 32)
        clear_semaphores()

        def norm_act(act, o):
            for t in range(TT):
                o.run(act.activation(in_gates(8, 12), h[:, t, :], ACT.Square,
                                     scale=DM ** -0.5, accum_out=ss[:, t:t + 1]), S["sumsq_ready"])
                o.settle()

        def pool_rsqrt(pool, o, n, scale, eps, ready):
            o.step(pool.tensor_scalar(rtmp[:, 0:n], ss[:, 0:n], scale, eps, ALU.mult, ALU.add))
            o.run(pool.tensor_tensor(rstd[:, 0:n], rtmp[:, 0:n], con[:, C_HALF:C_HALF + n], ALU.pow), ready)

        def norm_pool(pool, o):
            pool.wait_ge(S["sumsq_ready"], TT)
            pool_rsqrt(pool, o, TT, 1.0, 1e-6, S["rstd_ready"])

        def norm_pe(pe):
            pe.wait_ge(S["xs_ready"], TT)
            for q in range(2):
                for t in range(TT):
                    for k in range(4):
                        last = pe.transpose(psum[2 + 2 * q + t][:, k * P:(k + 1) * P],
                                            xs[:, t, (4 * q + k) * P:(4 * q + k + 1) * P], ident)
                    last.then_inc(S["xT_psum"], 1)

        def norm_dve(dve, o, gain, meanwhile=lambda: None):
            dve.wait_ge(S["rstd_ready"], 1)
            for t in range(TT):
                o.run(dve.tensor_scalar(xs[:, t, :], h[:, t, :], rstd[:, t:t + 1], None, ALU.mult),
                      S["xs_ready"])
            meanwhile()
            for q in range(2):
                for t in range(TT):
                    dve.wait_ge(S["xT_psum"], 2 * q + t + 1)
                    o.run(dve.tensor_tensor(
                        xraw[:, 4 * q:4 * q + 4, t * P:(t + 1) * P],
                        psum[2 + 2 * q + t][:, :].rearrange("p (k s) -> p k s", k=4),
                        gain[:, 4 * q:4 * q + 4].unsqueeze(2).to_broadcast([P, 4, P]), ALU.mult),
                        S["xraw_ready"])

        def norm_split_act(act, o):
            for q in range(2):
                for t in range(TT):
                    act.wait_ge(S["xraw_ready"], 2 * q + t + 1)
                    cut = (slice(None), slice(4 * q, 4 * q + 4), slice(t * P, (t + 1) * P))
                    o.run(act.activation(x_hi[cut], xraw[cut], ACT.Copy), S["x_hi_ready"])

        def norm_split_dve(dve, o):
            for q in range(2):
                for t in range(TT):
                    dve.wait_ge(S["x_hi_ready"], 2 * q + t + 1)
                    dve.wait_ge(S["xraw_ready"], 2 * q + t + 1)
                    cut = (slice(None), slice(4 * q, 4 * q + 4), slice(t * P, (t + 1) * P))
                    o.run(dve.tensor_tensor(x_lo[cut], xraw[cut], x_hi[cut].bitcast(F32), ALU.subtract),
                          S["x_lo_ready"])

        def x_arrives(pe, a, b, k):
            if a == 0 and k % 4 == 0:
                pe.wait_ge(S["x_lo_ready" if b else "x_hi_ready"], k // 2 + 2)

        def softplus_dve(dve, o, n, sem_arg, sem_exp, count):
            z, y, s, s2, p = (c[:, 0:n] for c in (sp_z, sp_y, sp_s, sp_s2, sp_p))
            o.step(dve.tensor_scalar(s, z, -1.0, None, ALU.mult))
            o.step(dve.tensor_tensor(y, z, s, ALU.max), sem_arg)
            dve.wait_ge(sem_exp, count)
            o.step(dve.tensor_scalar(s, y, 2.0, None, ALU.add))
            o.step(dve.reciprocal(s, s))
            o.step(dve.tensor_tensor(s, y, s, ALU.mult))
            o.step(dve.tensor_tensor(s2, s, s, ALU.mult))
            o.step(dve.tensor_scalar(p, s2, 1.0 / 17, None, ALU.mult))
            for k in range(7, 0, -1):
                o.step(dve.scalar_tensor_tensor(p, p, 1.0 / (2 * k + 1), s2, ALU.add, ALU.mult))
            o.step(dve.scalar_tensor_tensor(p, p, 1.0, s, ALU.add, ALU.mult))
            o.step(dve.tensor_scalar(z, z, 0.0, None, ALU.max))
            o.step(dve.scalar_tensor_tensor(p, p, 2.0, z, ALU.mult, ALU.add))

        SCHED = mixer_schedule()

        def lo_sem(u):
            return S["unit_lo_pool" if lo_by_pool(u) else "unit_lo"]

        def hb(view):
            return view[:, :].rearrange("p (h d) -> p h d", h=HEADS)

        def bc_row(col, n, width=P):
            return col.unsqueeze(2).to_broadcast([P, n, width])

        def select_level(eng, s):
            mask = con[:, C_LEVEL + s * P:C_LEVEL + (s + 1) * P]
            return eng.tensor_tensor(dusel.rearrange("p t h d -> p (t h) d"), dU.rearrange("p t h d -> p (t h) d"),
                                     mask.unsqueeze(1).to_broadcast([P, TT * HEADS, P]), ALU.mult)

        def mixer_block(layer):
            with nc.Block() as block:
                @block.sync
                def _(sp):
                    sp.dma_start(par[:, :], params[bass.ds(layer, 1), :, :].rearrange("l p c -> p (l c)")
                                 ).then_inc(S["small_loaded"], 16)
                    sp.dma_start(cdg[:, :, :], cdiag[bass.ds(layer, 1), :, :].rearrange("l p c -> p (l c)")
                                 .rearrange("p (g c) -> p g c", g=8)).then_inc(S["small_loaded"], 16)
                    for u in range(MIX_UNITS):
                        for f in range(2):
                            if u >= MIX_SLOTS:
                                sp.wait_ge(lo_sem(u - MIX_SLOTS), lo_count(2 * (u - MIX_SLOTS) + f))
                            cut = (slice(None), slice(f * UNIT // 2, (f + 1) * UNIT // 2))
                            sp.dma_start(raw[u % MIX_SLOTS][cut],
                                         mix_units[bass.ds(layer, 1), u, :, cut[1]].rearrange("l p c -> p (l c)")
                                         ).then_inc(slot_loaded[u % MIX_SLOTS * 2 + f], 16)

                @block.tensor
                def _(pe):
                    def unit(u, k):
                        return [w[u % 2].rearrange("p (k c) -> p k c", k=k) for w in (w_hi, w_lo)]

                    def proj(j):
                        u, f = divmod(j, 2)
                        w, x = unit(u, KD), (x_hi, x_lo)
                        bank = psum[u % 2]
                        if f == 0 and u >= 2:
                            pe.wait_ge(S["proj_evac"], u - 1)
                        if j == 0:
                            def operands(a, b, k):
                                x_arrives(pe, a, b, k)
                                return w[a][:, k, 0:P], x[b][:, k, :]
                        elif U_Z <= u < U_A or u in (16, 17, 22, 23):
                            def operands(a, b, k):
                                return x[b][:, k, f * P:(f + 1) * P], w[a][:, k, :]
                        else:
                            def operands(a, b, k):
                                return w[a][:, k, f * P:(f + 1) * P], x[b][:, k, :]
                        last = product3(pe, bank[:, f * UC:(f + 1) * UC], operands, KD,
                                        S["unit_hi"], lo_sem(u), 2 * u + 1, lo_count(2 * u))
                        if f == 1:
                            last.then_inc(S["unit_done"], 1)

                    def c_gates(_):
                        pe.wait_ge(S["c_conv_ready"], 1)
                        pe.wait_ge(S["small_loaded"], 32)
                        for g in range(2):
                            for m in range(NB):
                                last = pe.matmul(psum[2 + 2 * g + m // 2][:, (m % 2) * SEQ:(m % 2 + 1) * SEQ],
                                                 cdg[:, 4 * g + m, :], c_xc[:, m, :], start=True, stop=True)
                            last.then_inc(S["c_gates_psum"], 1)

                    def ba_cols(_):
                        pe.wait_ge(S["c_tanh"], 8)
                        w = par_of("w_ba").rearrange("p (k c) -> p k c", k=KD)
                        for t in range(TT):
                            for k in range(KD):
                                last = pe.matmul(psum[2][:, 8 * t:8 * t + 8], xraw[:, k, t * P:(t + 1) * P],
                                                 w[:, k, :], start=(k == 0), stop=(k == KD - 1))
                        last.then_inc(S["ba_psum"], 1)

                    def d_tok(part):
                        for g, t in (((0, 0), (0, 1), (1, 0), (1, 1)), ((2, 0), (2, 1)))[part]:
                            n = 2 * g + t
                            pe.wait_ge(S["d_silu_ready"], g + 1)
                            if n == 5:
                                pe.wait_ge(S["d_tok_ready"], 1)
                            for hd in range(HEADS):
                                last = pe.transpose(psum[3 + n % 5][:, hd * P:(hd + 1) * P],
                                                    dcv[:, 4 * g + hd, t * P:(t + 1) * P], ident)
                            last.then_inc(S["d_tok_psum"], 1)

                    def d_back(_):
                        pe.wait_ge(S["d_tok_ready"], 6)
                        pe.wait_ge(S["ba_cols"], 1)
                        for g in range(2):
                            for t in range(TT):
                                n = 2 * g + t
                                pe.wait_ge(S["d_unit_ready"], n + 1)
                                src = (qtok, ktok)[g]
                                for hd in range(HEADS):
                                    last = pe.transpose(psum[2 + n][:, hd * P:(hd + 1) * P],
                                                        src[:, t, hd, :], ident)
                                last.then_inc(S["d_back_psum"], 1)

                    def d_cum(_):
                        pe.wait_ge(S["dg_ready"], 1)
                        pe.wait_ge(S["d_T_ready"], 4)
                        for t in range(TT):
                            pe.matmul(psum[6][:, 4 * t:4 * t + 4], tri, dg[:, 4 * t:4 * t + 4], start=True, stop=True)
                        for t in range(TT):
                            for hd in range(HEADS):
                                c = 4 * t + hd
                                pe.matmul(psum[2 + t][:, hd * P:(hd + 1) * P],
                                          dg[:, c:c + 1].to_broadcast([P, P]), tri, start=True, stop=True)
                        for t in range(TT):
                            for hd in range(HEADS):
                                c = 4 * t + hd
                                last = pe.matmul(psum[4 + t][:, hd * P:(hd + 1) * P],
                                                 beta[:, c:c + 1].to_broadcast([P, P]), ident, start=True, stop=True)
                        last.then_inc(S["d_cum_psum"], 1)

                    def d_kk(_):
                        pe.wait_ge(S["d_args_ready"], 4)
                        for t in range(TT):
                            for hd in range(HEADS):
                                last = pe.matmul(psum[2 + t][:, hd * P:(hd + 1) * P], dK[:, hd, t * P:(t + 1) * P],
                                                 dK[:, hd, t * P:(t + 1) * P], start=True, stop=True)
                            last.then_inc(S["d_kk_psum"], 1)
                        for t in range(TT):
                            for hd in range(HEADS):
                                last = pe.matmul(psum[6 + t][:, hd * P:(hd + 1) * P], dK[:, hd, t * P:(t + 1) * P],
                                                 dQ[:, hd, t * P:(t + 1) * P], start=True, stop=True)
                            last.then_inc(S["d_kk_psum"], 1)

                    def inv_p(s):
                        pe.wait_ge(S["dusel_ready"], s + 1)
                        if s == 0:
                            pe.wait_ge(S["d_u_ready"], 4)
                        for t in range(TT):
                            if s:
                                pe.wait_ge(S["xy_ready"], 2 * (s - 1) + t + 1)
                            for hd in range(HEADS):
                                bank = psum[2 + t][:, hd * P:(hd + 1) * P]
                                if s == 0:
                                    last = pe.transpose(bank, dusel[:, t, hd, :], ident)
                                else:
                                    last = pe.matmul(bank, dusel[:, t, hd, :], dX[:, t, hd, :],
                                                     start=True, stop=True)
                            last.then_inc(S["inv_p_psum"], 1)

                    def inv_x(s):
                        if s == 0:
                            return
                        for t in range(TT):
                            pe.wait_ge(S["inv_p_ready"], 2 * (s - 1) + t + 1)
                            if s == 1:
                                pe.wait_ge(S["d_ub_ready"], 2)
                            if s < LEVELS - 1:
                                for hd in range(HEADS):
                                    pe.matmul(psum[2 + t][:, hd * P:(hd + 1) * P], dY[:, t, hd, :],
                                              dP[:, t, hd, :], start=True, stop=True)
                            for hd in range(HEADS):
                                last = pe.matmul(psum[4 + t][:, hd * P:(hd + 1) * P], dP[:, t, hd, :],
                                                 dY[:, t, hd, :], start=True, stop=True)
                            last.then_inc(S["inv_x_psum"], 1)

                    def d_v0(_):
                        pe.wait_ge(S["r0_ready"], 1)
                        pe.wait_ge(S["xy_ready"], 2 * LEVELS)
                        for hd in range(HEADS):
                            last = pe.matmul(psum[2][:, hd * P:(hd + 1) * P], dY[:, 0, hd, :], dR[:, hd, :],
                                             start=True, stop=True)
                        last.then_inc(S["v0_psum"], 1)

                    def d_s(_):
                        pe.wait_ge(S["v0_ready"], 1)
                        for hd in range(HEADS):
                            last = pe.matmul(psum[3][:, hd * P:(hd + 1) * P], ktok[:, 0, hd, :], dP[:, 0, hd, :],
                                             start=True, stop=True)
                        last.then_inc(S["s_psum"], 1)

                    def d_ks(_):
                        pe.wait_ge(S["s_ready"], 1)
                        for bank, src in ((2, dK), (4, dQ)):
                            for hd in range(HEADS):
                                last = pe.matmul(psum[bank][:, hd * P:(hd + 1) * P], src[:, hd, P:2 * P],
                                                 dS[:, hd, :], start=True, stop=True)
                        last.then_inc(S["ks_psum"], 1)

                    def d_v1(_):
                        pe.wait_ge(S["r1_ready"], 1)
                        for hd in range(HEADS):
                            last = pe.matmul(psum[3][:, hd * P:(hd + 1) * P], dY[:, 1, hd, :], dR[:, hd, :],
                                             start=True, stop=True)
                        last.then_inc(S["v1_psum"], 1)

                    def d_o(_):
                        pe.wait_ge(S["v1_ready"], 1)
                        pe.wait_ge(S["ks_taken"], 1)
                        for t, bank in ((0, 2), (1, 5)):
                            for hd in range(HEADS):
                                last = pe.matmul(psum[bank][:, hd * P:(hd + 1) * P], dexp[:, t, hd, :],
                                                 dP[:, t, hd, :], start=True, stop=True)
                        last.then_inc(S["o_psum"], 1)

                    def to_features(src, banks, ready):
                        for t in range(TT):
                            for hd in range(HEADS):
                                last = pe.transpose(psum[banks[t]][:, hd * P:(hd + 1) * P], src[:, t, hd, :], ident)
                            last.then_inc(ready, 1)

                    def d_oT(_):
                        pe.wait_ge(S["d_out_ready"], 1)
                        to_features(dtmp, (3, 4), S["d_oT_psum"])

                    def attn(i):
                        if i >= 3:
                            b, hd, qt = (i - 3) // 8, (i - 3) % 8 // 2, (i - 3) % 2
                            v = (av, bv)[b]
                            pe.wait_ge(S["at_t_ready"], i - 2)
                            if i == 3:
                                pe.wait_ge(S["oD_ready"], TT)
                            else:
                                pe.wait_ge(S["at_o_taken"], i - 3)
                            for kb in range(qt + 1):
                                last = pe.matmul(psum[4][:, 0:P], wT[:, (i - 3) % 2, kb * P:(kb + 1) * P],
                                                 v[:, kb, hd * P:(hd + 1) * P], start=(kb == 0), stop=(kb == qt))
                            last.then_inc(S["at_o_psum"], 1)
                        if 2 <= i < ATTN + 2:
                            pe.wait_ge(S["at_w_ready"], i - 1)
                            if i == 2:
                                pe.wait_ge(S["d_u_ready"], 4)
                            else:
                                pe.wait_ge(S["at_t_ready"], i - 2)
                            for kb in range(i % 2 + 1):
                                last = pe.transpose(psum[7][:, kb * P:(kb + 1) * P],
                                                    sm[:, i % 2, 0, kb * P:(kb + 1) * P], ident)
                            last.then_inc(S["at_t_psum"], 1)
                        if i < ATTN:
                            b, hd, qt = i // 8, (i % 8) // 2, i % 2
                            kw = (qt + 1) * P
                            pe.wait_ge(S["proj_evac"], U_A + 4 if b == 0 else U_GATE)
                            if i == 0:
                                pe.wait_ge(S["d_u_ready"], 4)
                                pe.wait_ge(S["o_ss_ready"], 1)
                            else:
                                pe.wait_ge(S["at_s_taken"], i)
                            if b == 0:
                                for c in range(2):
                                    rows = slice(64 * c, 64 * c + 64)
                                    last = pe.matmul(psum[5 + c][:, 0:kw],
                                                     aq[rows, hd, qt * P:(qt + 1) * P], ak[rows, hd, 0:kw],
                                                     start=True, stop=True)
                            else:
                                last = pe.matmul(psum[6][:, 0:kw], bq[:, hd, qt * P:(qt + 1) * P], bk[:, hd, 0:kw],
                                                 start=True, stop=True)
                            last.then_inc(S["at_s_psum"], 1)

                    def at_oT(b):
                        pe.wait_ge(S["a_out_ready"] if b == 0 else S["at_o_taken"], (1, ATTN)[b])
                        pe.wait_ge(S["oD_ready"] if b == 0 else S["oA_ready"], TT)
                        to_features((ot, ot_b)[b], (2, 3), S["at_oT_psum"])

                    def branch(j):
                        q = j % 4
                        u = U_BR + j // 2
                        w, x = unit(u, NB), staged[j // 4 % 2]
                        if j < 2:
                            pe.wait_ge(S["proj_evac"], U_BR - 1 + j)
                        else:
                            pe.wait_ge(S["br_taken"], j - 1)
                        pe.wait_ge(S["st_lo_ready"], j // 4 + 1)
                        for f in range(2):
                            b = 2 * (q % 2) + f
                            last = product3(pe, psum[j % 2][:, f * SEQ:(f + 1) * SEQ],
                                            lambda i, l, k: (w[i][:, k, b * P:(b + 1) * P], x[l][:, k, :]), NB,
                                            S["unit_hi"], lo_sem(u), 2 * u + 1, lo_count(2 * u))
                        if j % 2 == 0:
                            last.then_inc(S["br_psum"], 1)
                        else:
                            last.then_inc(S["unit_done"], 1)

                    def project_out(j):
                        u = U_OUT + j
                        w = unit(u, KD)
                        if j >= 2:
                            pe.wait_ge(S["f_out_taken"], j - 1)
                        else:
                            pe.wait_ge(S["br_taken"], BRANCHES * 4 - 1 + j)
                        pe.wait_ge(S["unit_hi"], 2 * u + 2)
                        pe.wait_ge(lo_sem(u), lo_count(2 * u + 1))
                        for t in range(TT):
                            for k in range(KD):
                                pe.wait_ge(S["acc_lo_ready"], k // 2 + 1)
                                for i, (a, b) in enumerate(((0, 0), (0, 1), (1, 0))):
                                    last = pe.matmul(psum[j % 2][:, t * UC:(t + 1) * UC],
                                                     acc_parts[k // 2][b][:, k % 2, t * P:(t + 1) * P], w[a][:, k, :],
                                                     start=(k == 0 and i == 0), stop=(k == KD - 1 and i == 2))
                        last.then_inc(S["unit_done"], 1)

                    steps = {"norm": lambda _: norm_pe(pe), "proj": proj, "c_gates": c_gates, "ba": ba_cols,
                             "d_tok": d_tok, "d_back": d_back, "d_cum": d_cum, "d_kk": d_kk, "inv_p": inv_p,
                             "inv_x": inv_x, "d_v0": d_v0, "d_s": d_s, "d_ks": d_ks, "d_v1": d_v1, "d_o": d_o,
                             "d_oT": d_oT, "attn": attn, "at_oT": at_oT, "branch": branch,
                             "out": project_out}
                    for what, i in SCHED:
                        if what in steps:
                            steps[what](i)

                @block.scalar
                def _(act):
                    o = Order(act, S["act_own"])

                    def copy(dst, src, ready=None, scale=1.0):
                        o.run(act.activation(dst, src, ACT.Copy, scale=scale), ready)

                    def split_hi(half):
                        u, f = divmod(half, 2)
                        if u < MIX_UNITS:
                            if u >= 2:
                                act.wait_ge(S["unit_done"], u - 1)
                            act.wait_ge(slot_loaded[u % MIX_SLOTS * 2 + f], 16 * (u // MIX_SLOTS + 1))
                            cut = (slice(None), slice(f * UNIT // 2, (f + 1) * UNIT // 2))
                            copy(w_hi[u % 2][cut], raw[u % MIX_SLOTS][cut], S["unit_hi"])

                    def prepare(_):
                        norm_act(act, o)
                        split_hi(0)
                        split_hi(1)
                        norm_split_act(act, o)
                        split_hi(2)

                    def lambdas(_):
                        act.wait_ge(S["sp_arg"], 1)
                        o.run(act.activation(sp_y[:, 0:NB], sp_y[:, 0:NB], ACT.Exp, scale=-1.0), S["sp_exp"])
                        act.wait_ge(S["lam_arg"], 2)
                        o.run(act.activation(lam_e, lam_sum, ACT.Exp), S["lam_exp"])
                        act.wait_ge(S["small_loaded"], 32)
                        o.run(act.activation(expA, par_of("d_A_log"), ACT.Exp), S["lam_exp"])

                    def proj(j):
                        u, f = divmod(j, 2)
                        split_hi(j + 3)
                        if f == 0:
                            return
                        act.wait_ge(S["unit_done"], u + 1)
                        bank = psum[u % 2][:, :].rearrange("p (b t) -> p b t", b=2)
                        ready = S["proj_evac"]
                        if u < U_C + 2:
                            copy(cpad[:, 2 * u:2 * u + 2, 3:3 + SEQ], bank, ready)
                        elif u < U_D:
                            copy(cgate[:, 2 * (u - 2):2 * (u - 2) + 2, :], bank, ready)
                        elif u < U_Z:
                            b = 2 * (u - U_D)
                            copy(dpad[:, b:b + 2, 3:3 + SEQ], bank, ready)
                        elif u < U_A:
                            c = UC * (u - U_Z)
                            copy(zt[:, :, c:c + UC], bank, ready)
                        elif u < U_GATE:
                            if u == U_A:
                                act.wait_ge(S["c_out_ready"], 1)
                            b, r = divmod(u - U_A, 6)
                            if r < 4:
                                dst = ((aq, ak), (bq, bk))[b][r // 2][:, 2 * (r % 2):2 * (r % 2) + 2, :]
                            else:
                                dst = (av, bv)[b][:, :, UC * (r - 4):UC * (r - 3)]
                            copy(dst, bank, ready)
                        else:
                            for f in range(2):
                                b = 2 * (u - U_GATE) + f
                                ins = act.activation(gates[:, b, :], bank[:, f, :], ACT.Tanh,
                                                     bias=half_b[:, b:b + 1], scale=0.5)
                                o.run(ins, ready if f else None)

                    def c_gelu_tanh(_):
                        act.wait_ge(S["c_gelu_arg"], 1)
                        o.run(act.activation(c_g, c_g, ACT.Tanh, scale=math.sqrt(2 / math.pi)), S["c_gelu_tanh"])

                    def d_tanh(g):
                        act.wait_ge(S["d_conv_ready"], g + 1)
                        o.run(act.activation(dth[:, g, :], dcv[:, 4 * g:4 * g + 4, :].rearrange("p b t -> p (b t)"),
                                             ACT.Tanh, scale=0.5), S["d_tanh_ready"])

                    def c_gates(_):
                        for g, (dst, bias) in enumerate(((c_r, half_ba), (c_i, half_bx))):
                            act.wait_ge(S["c_gates_psum"], g + 1)
                            for m in range(NB):
                                o.run(act.activation(dst[:, m, :],
                                                     psum[2 + 2 * g + m // 2][:, (m % 2) * SEQ:(m % 2 + 1) * SEQ],
                                                     ACT.Tanh, bias=bias[:, m:m + 1], scale=0.5), S["c_tanh"])

                    def c_decay(_):
                        o.settle()
                        for m in range(NB):
                            o.run(act.activation(c_a[:, m, :], c_r[:, m, :], ACT.Exp,
                                                 bias=nlru[:, m:m + 1], scale=nlru[:, m:m + 1]), S["c_a_t"])
                            o.run(act.activation(c_t[:, m, :], c_r[:, m, :], ACT.Tanh,
                                                 bias=lru[:, m:m + 1], scale=lru[:, m:m + 1]), S["c_a_t"])

                    def c_coef(_):
                        act.wait_ge(S["c_coef"], 1)
                        o.run(act.activation(c_t, c_t, ACT.Sqrt, scale=0.25), S["c_sqrt"])

                    def ba_act(_):
                        act.wait_ge(S["ba_cols"], 1)
                        b3 = ba.rearrange("p (t c) -> p t c", t=TT)
                        o.run(act.activation(beta.rearrange("p (t c) -> p t c", t=TT), b3[:, :, 0:HEADS],
                                             ACT.Tanh, scale=0.5), S["ba_act"])
                        act.wait_ge(S["sp_arg"], 2)
                        o.run(act.activation(sp_y, sp_y, ACT.Exp, scale=-1.0), S["sp_exp"])

                    def d_tok(part):
                        if part == 0:
                            d_tanh(2)
                        for n in ((0, 1, 2, 3), (4, 5))[part]:
                            g, t = divmod(n, 2)
                            act.wait_ge(S["d_tok_psum"], n + 1)
                            act.wait_ge(S["d_silu_ready"], 3)
                            copy((qtok, ktok, vtok)[g][:, t], hb(psum[3 + n % 5]), S["d_tok_ready"],
                                 scale=0.5 if g == 2 else 1.0)

                    def d_back(_):
                        for n in range(4):
                            g, t = divmod(n, 2)
                            act.wait_ge(S["d_back_psum"], n + 1)
                            act.wait_ge(S["d_tok_psum"], 6)
                            copy((dQ, dK)[g][:, :, t * P:(t + 1) * P], hb(psum[2 + n]), S["d_T_ready"])

                    def d_cum(_):
                        act.wait_ge(S["d_args_ready"], 4)
                        o.run(act.activation(dexp[:, :, :, :], dexp[:, :, :, :], ACT.Exp), S["d_exp_ready"])
                        o.run(act.activation(dfac, darg, ACT.Exp), S["d_exp_ready"])

                    def inv_p(s):
                        if s == 0:
                            return
                        for t in range(TT):
                            act.wait_ge(S["inv_p_psum"], 2 * s + t + 1)
                            copy(dP[:, t], hb(psum[2 + t]), S["inv_p_ready"])

                    def d_v0(_):
                        act.wait_ge(S["v0_psum"], 1)
                        act.wait_ge(S["inv_x_psum"], 2 * (LEVELS - 1))
                        copy(dP[:, 0], hb(psum[2]), S["v0_ready"])

                    def d_s(_):
                        act.wait_ge(S["s_psum"], 1)
                        copy(dS, hb(psum[3]), S["s_ready"])

                    def d_v1(_):
                        act.wait_ge(S["v1_psum"], 1)
                        copy(dP[:, 1], hb(psum[3]), S["v1_ready"])

                    def d_o(_):
                        act.wait_ge(S["proj_evac"], U_A)
                        act.wait_ge(S["d_u_ready"], 4)
                        act.wait_ge(S["xy_ready"], 2 * LEVELS)
                        o.run(act.activation(dusel.rearrange("p t h d -> p (t h d)"),
                                             zt[:, :, :].rearrange("p t d -> p (t d)"), ACT.Tanh, scale=0.5),
                              S["z_tanh"])

                    def from_psum(n, banks, psum_ready):
                        for t in range(TT):
                            act.wait_ge(psum_ready[0], psum_ready[1] + t + 1)
                            copy(oT[n][:, :, t * P:(t + 1) * P], hb(psum[banks[t]]),
                                 {0: S["oA_ready"], 1: S["oB_ready"], 3: S["oD_ready"]}[n])

                    def attn(i):
                        if 2 <= i < ATTN + 2:
                            kw = (i % 2 + 1) * P
                            act.wait_ge(S["at_t_psum"], i - 1)
                            if i >= 4:
                                act.wait_ge(S["at_o_psum"], i - 3)
                            copy(wT[:, i % 2, 0:kw], psum[7][:, 0:kw], S["at_t_ready"])
                        if i < ATTN:
                            kw = (i % 2 + 1) * P
                            act.wait_ge(S["at_max_ready"], i + 1)
                            for c in range(2 if i < 8 else 1):
                                o.run(act.activation(sm[:, i % 2, c, 0:kw], sm[:, i % 2, c, 0:kw], ACT.Exp,
                                                     bias=nmx[:, c:c + 1], accum_out=sums[:, c:c + 1]),
                                      S["at_exp_ready"])

                    def at_oT(b):
                        from_psum(b, (2, 3), (S["at_oT_psum"], 2 * b))

                    def d_oT(_):
                        from_psum(3, (3, 4), (S["d_oT_psum"], 0))

                    def stage(m):
                        n = BRANCH_ORDER[m]
                        if n == 2:
                            act.wait_ge(S["c_out_ready"], 1)
                        if m >= 1:
                            act.wait_ge(S["unit_done"], U_BR + 2 * (m - 1))
                        o.settle()
                        copy(staged[m % 2][0], oT[n], S["st_hi_ready"])

                    def branch(j):
                        split_hi(2 * U_BR + j + 3)
                        if j >= 12:
                            q = j - 12
                            act.wait_ge(S["unit_done"], U_BR + 6)
                            act.wait_ge(S["acc_ready"], q + 1)
                            copy(acc_parts[q][0], acc[:, 2 * q:2 * q + 2, :], S["acc_hi_ready"])

                    def project_out(j):
                        split_hi(2 * (U_OUT + j) + 3)
                        split_hi(2 * (U_OUT + j) + 4)

                    steps = {"stage": stage, "branch": branch, "out": project_out, "lambdas": lambdas,
                             "c_decay": c_decay, "c_coef": c_coef, "c_gelu_tanh": c_gelu_tanh, "d_tanh": d_tanh,
                             "norm": prepare, "proj": proj, "c_gates": c_gates, "ba": ba_act, "d_tok": d_tok,
                             "d_back": d_back, "d_cum": d_cum, "inv_p": inv_p, "d_v0": d_v0, "d_s": d_s,
                             "d_v1": d_v1, "d_o": d_o, "attn": attn, "at_oT": at_oT, "d_oT": d_oT}
                    for what, i in SCHED:
                        if what in steps:
                            steps[what](i)

                @block.gpsimd
                def _(pool):
                    o = Order(pool, S["pool_own"])

                    def split_lo(half):
                        u, f = divmod(half, 2)
                        if u < MIX_UNITS and lo_by_pool(u):
                            pool.wait_ge(S["unit_hi"], half + 1)
                            cut = (slice(None), slice(f * UNIT // 2, (f + 1) * UNIT // 2))
                            o.run(pool.tensor_tensor(w_lo[u % 2][cut], raw[u % MIX_SLOTS][cut],
                                                     w_hi[u % 2][cut].bitcast(F32), ALU.subtract),
                                  S["unit_lo_pool"])

                    def project_out(j):
                        split_lo(2 * (U_OUT + j) + 3)
                        split_lo(2 * (U_OUT + j) + 4)

                    def inv_p(s):
                        if s >= 2:
                            pool.wait_ge(S["inv_p_psum"], 2 * s)
                            o.run(select_level(pool, s), S["dusel_ready"])

                    def d_tok(part):
                        if part == 1:
                            pool.wait_ge(S["d_ss_ready"], 1)
                            pool_rsqrt(pool, o, 16, 0.25, 1e-6, S["d_rs_ready"])

                    def d_o(_):
                        pool.wait_ge(S["o_ss_ready"], 1)
                        pool_rsqrt(pool, o, 8, 1.0 / P, 1e-6, S["o_rs_ready"])

                    def a_sq(_):
                        pool.wait_ge(S["a_ss_ready"], 1)
                        pool_rsqrt(pool, o, 8, 1.0 / P, 1e-5, S["a_rs_ready"])

                    steps = {"norm": lambda _: norm_pool(pool, o), "d_tok": d_tok, "inv_p": inv_p,
                             "d_o": d_o, "a_sq": a_sq, "proj": lambda j: split_lo(j + 3),
                             "branch": lambda j: split_lo(2 * U_BR + j + 3), "out": project_out}
                    for what, i in SCHED:
                        if what in steps:
                            steps[what](i)

                @block.vector
                def _(dve):
                    o = Order(dve, S["dve_own"])
                    TMPD = dtmp

                    def split_lo(half):
                        u, f = divmod(half, 2)
                        if u < MIX_UNITS and not lo_by_pool(u):
                            dve.wait_ge(S["unit_hi"], half + 1)
                            cut = (slice(None), slice(f * UNIT // 2, (f + 1) * UNIT // 2))
                            o.run(dve.tensor_tensor(w_lo[u % 2][cut], raw[u % MIX_SLOTS][cut],
                                                    w_hi[u % 2][cut].bitcast(F32),
                                                    ALU.subtract), S["unit_lo"])

                    def prepare(_):
                        dve.wait_ge(S["small_loaded"], 32)
                        o.run(dve.tensor_scalar(half_b, par_of("b_gate"), 0.5, None, ALU.mult))
                        o.run(dve.tensor_scalar(half_ba, par_of("c_b_a"), 0.5, None, ALU.mult))
                        o.run(dve.tensor_scalar(half_bx, par_of("c_b_x"), 0.5, None, ALU.mult))
                        o.run(dve.memset(dpad[:, :, 0:3], 0.0))
                        o.run(dve.memset(cpad[:, :, 0:3], 0.0))
                        norm_dve(dve, o, par_of("norm_mix"), lambda: split_lo(0))
                        norm_split_dve(dve, o)
                        split_lo(1)
                        split_lo(2)

                    def lambdas(_):
                        o.settle()
                        o.step(dve.tensor_scalar(sp_z[:, 0:NB], par_of("c_lambda"), -1.0, None, ALU.mult))
                        softplus_dve(dve, o, NB, S["sp_arg"], S["sp_exp"], 1)
                        o.run(dve.tensor_scalar(lru, sp_p[:, 0:NB], LRU_C / 2, None, ALU.mult))
                        o.run(dve.tensor_scalar(nlru, sp_p[:, 0:NB], -LRU_C / 2, None, ALU.mult))
                        lam4 = par_of("lam").rearrange("p (a b c) -> p a b c", a=2, b=2)
                        o.step(dve.tensor_tensor(lam_prod.rearrange("p (a c) -> p a c", a=2), lam4[:, :, 0, :],
                                                 lam4[:, :, 1, :], ALU.mult))
                        for c in range(2):
                            o.run(dve.tensor_reduce(lam_sum[:, c:c + 1], lam_prod[:, 64 * c:64 * c + 64], AX, ALU.add),
                                  S["lam_arg"])
                        dve.wait_ge(S["lam_exp"], 2)
                        o.step(dve.tensor_tensor(lam_neg, lam_e[:, 1:2], lam_e[:, 0:1], ALU.subtract))
                        o.step(dve.tensor_tensor(lam_neg, lam_neg, par_of("lam_init"), ALU.subtract))
                        o.run(dve.tensor_scalar(a_scale_row, par_of("a_subln"), par_of("out_scale"), None, ALU.mult))
                        o.settle()

                    def conv(dst, src, w, n0, n1, bias, tap, ready):
                        o.settle()
                        for b in range(n0, n1):
                            col = w[:, b * TAPS + tap:b * TAPS + tap + 1]
                            if tap == 0 and bias is None:
                                ins = dve.tensor_scalar(dst[:, b, :], src[:, b, 0:SEQ], col, None, ALU.mult)
                            elif tap == 0:
                                ins = dve.tensor_scalar(dst[:, b, :], src[:, b, 0:SEQ], col, bias[:, b:b + 1],
                                                        ALU.mult, ALU.add)
                            else:
                                ins = dve.scalar_tensor_tensor(dst[:, b, :], src[:, b, tap:tap + SEQ], col,
                                                               dst[:, b, :], ALU.mult, ALU.add)
                            o.run(ins, ready if tap == TAPS - 1 and b == n1 - 1 else None)

                    def c_conv(tap):
                        if tap == 0:
                            dve.wait_ge(S["proj_evac"], 2)
                        conv(c_xc, cpad, par_of("c_conv_w"), 0, NB, par_of("c_conv_b"), tap, S["c_conv_ready"])

                    def d_conv(i):
                        g, tap = divmod(i, TAPS)
                        if tap == 0:
                            dve.wait_ge(S["proj_evac"], U_D + 2 * g + 2)
                        conv(dcv, dpad, par_of("d_conv_w"), 4 * g, 4 * g + 4, None, tap, S["d_conv_ready"])

                    def c_gelu_arg(_):
                        dve.wait_ge(S["proj_evac"], 4)
                        o.step(dve.tensor_tensor(c_g, cgate, cgate, ALU.mult))
                        o.step(dve.tensor_scalar(c_g, c_g, 0.044715, 1.0, ALU.mult, ALU.add))
                        o.step(dve.tensor_tensor(c_g, c_g, cgate, ALU.mult), S["c_gelu_arg"])

                    def c_gelu(_):
                        dve.wait_ge(S["c_gelu_tanh"], 1)
                        o.step(dve.scalar_tensor_tensor(c_g, c_g, 1.0, cgate, ALU.add, ALU.mult))

                    def silu(g):
                        dve.wait_ge(S["d_tanh_ready"], g + 1)
                        o.settle()
                        v = dcv[:, 4 * g:4 * g + 4, :].rearrange("p b t -> p (b t)")
                        o.step(dve.scalar_tensor_tensor(v, dth[:, g, :], 1.0, v, ALU.add, ALU.mult),
                               S["d_silu_ready"])

                    def c_gates(_):
                        dve.wait_ge(S["c_tanh"], 8)
                        o.run(dve.scalar_tensor_tensor(c_i, c_i, 1.0, c_xc, ALU.add, ALU.mult))

                    def c_coef(_):
                        o.settle()
                        dve.wait_ge(S["c_a_t"], 8)
                        o.step(dve.tensor_tensor(c_r, c_a, c_a, ALU.mult))
                        o.step(dve.tensor_scalar(c_r, c_r, 1.0, None, ALU.add))
                        o.step(dve.scalar_tensor_tensor(c_t, c_t, 1.0e-30, c_r, ALU.max, ALU.mult), S["c_coef"])

                    def c_scan(_):
                        dve.wait_ge(S["c_sqrt"], 1)
                        o.step(dve.tensor_tensor(c_i, c_i, c_t, ALU.mult))
                        for m in range(NB):
                            o.run(dve.tensor_tensor_scan(c_r[:, m, :], c_a[:, m, :], c_i[:, m, :], 0.0,
                                                         ALU.mult, ALU.add))
                        o.settle()
                        o.run(dve.scalar_tensor_tensor(oT_c[:, :, :], c_r, 0.5, c_g, ALU.mult, ALU.mult),
                              S["c_out_ready"])

                    def ba_dve(_):
                        dve.wait_ge(S["ba_psum"], 1)
                        o.step(dve.tensor_copy(ba, psum[2][:, 0:16]), S["ba_cols"])
                        b3 = ba.rearrange("p (t c) -> p t c", t=TT)
                        z3 = sp_z.rearrange("p (t c) -> p t c", t=TT)
                        bias = par_of("d_dt_bias").unsqueeze(1).to_broadcast([P, TT, HEADS])
                        o.step(dve.tensor_tensor(z3, b3[:, :, HEADS:], bias, ALU.add))
                        softplus_dve(dve, o, 8, S["sp_arg"], S["sp_exp"], 2)
                        dve.wait_ge(S["ba_act"], 1)
                        o.step(dve.tensor_scalar(beta, beta, 0.5, 0.5, ALU.mult, ALU.add))
                        o.run(dve.scalar_tensor_tensor(
                            dg.rearrange("p (t c) -> p t c", t=TT), sp_p.rearrange("p (t c) -> p t c", t=TT), -1.0,
                            expA.unsqueeze(1).to_broadcast([P, TT, HEADS]), ALU.mult, ALU.mult), S["dg_ready"])

                    def d_tok(part):
                        if part == 0:
                            silu(2)
                            for n in range(4):
                                g, t = divmod(n, 2)
                                dve.wait_ge(S["d_tok_ready"], n + 1)
                                src = (qtok, ktok)[g][:, t]
                                o.step(dve.tensor_tensor(TMPD[:, t], src, src, ALU.mult))
                                o.step(dve.tensor_reduce(ss[:, 4 * n:4 * n + 4], TMPD[:, t], AX, ALU.add),
                                       S["d_ss_ready"] if n == 3 else None)
                            return
                        dve.wait_ge(S["d_rs_ready"], 1)
                        o.run(dve.tensor_scalar(rtmp[:, 0:8], rstd[:, 0:8], 0.5 * P ** -0.5, None, ALU.mult))
                        o.step(dve.tensor_scalar(rtmp[:, 8:16], rstd[:, 8:16], 0.5, None, ALU.mult))
                        for n in range(4):
                            g, t = divmod(n, 2)
                            v = (qtok, ktok)[g][:, t]
                            o.run(dve.tensor_tensor(v, v, bc_row(rtmp[:, 4 * n:4 * n + 4], HEADS), ALU.mult),
                                  S["d_unit_ready"])

                    def d_cum(_):
                        dve.wait_ge(S["d_cum_psum"], 1)
                        o.step(dve.tensor_copy(gcum, psum[6][:, 0:8]))
                        for t in range(TT):
                            for hd in range(HEADS):
                                c = 4 * t + hd
                                o.run(dve.scalar_tensor_tensor(dexp[:, t, hd, :], psum[2 + t][:, hd * P:(hd + 1) * P],
                                                               gcum[:, c:c + 1], neg_t, ALU.subtract, ALU.add),
                                      S["d_args_ready"] if hd == HEADS - 1 else None)
                        o.run(dve.tensor_copy(darg[:, 0:8], gcum))
                        for t in range(TT):
                            o.run(dve.tensor_tensor(darg[:, 8 + 4 * t:12 + 4 * t], hb(psum[2 + t])[:, :, P - 1],
                                                    gcum[:, 4 * t:4 * t + 4], ALU.subtract), S["d_args_ready"])
                        dve.wait_ge(S["d_exp_ready"], 2)
                        for t in range(TT):
                            o.run(dve.tensor_tensor(dU[:, t], dexp[:, t], hb(psum[4 + t]), ALU.mult), S["d_ub_ready"])
                        o.settle()
                        dve.wait_ge(S["d_tok_ready"], 6)
                        dve.wait_ge(S["d_back_psum"], 4)
                        o.run(dve.tensor_tensor(dR, vtok[:, 0], bc_row(beta[:, 0:4], HEADS), ALU.mult), S["r0_ready"])
                        o.run(dve.tensor_tensor(ktok[:, 0], ktok[:, 0], bc_row(dfac[:, 8:12], HEADS), ALU.mult))

                    def d_kk(_):
                        o.settle()
                        for t in range(TT):
                            dve.wait_ge(S["d_kk_psum"], t + 1)
                            o.run(dve.tensor_tensor(dU[:, t], dU[:, t], hb(psum[2 + t]), ALU.mult), S["d_u_ready"])
                        o.settle()
                        o.run(select_level(dve, 0), S["dusel_ready"])
                        for t in range(TT):
                            dve.wait_ge(S["d_kk_psum"], 2 + t + 1)
                            o.run(dve.tensor_tensor(dexp[:, t], dexp[:, t], hb(psum[6 + t]), ALU.mult), S["d_u_ready"])

                    def inv_x(s):
                        o.settle()
                        if s == 0:
                            eye = ident.unsqueeze(1).to_broadcast([P, HEADS, P])
                            for t in range(TT):
                                dve.wait_ge(S["inv_p_psum"], t + 1)
                                o.run(dve.tensor_tensor(dX[:, t], eye, hb(psum[2 + t]), ALU.subtract))
                                o.run(dve.tensor_tensor(dY[:, t], eye, dusel[:, t], ALU.subtract), S["xy_ready"])
                            o.settle()
                            o.run(select_level(dve, 1), S["dusel_ready"])
                            return
                        for t in range(TT):
                            dve.wait_ge(S["inv_x_psum"], 2 * (s - 1) + t + 1)
                            if s < LEVELS - 1:
                                o.run(dve.tensor_tensor(dX[:, t], dX[:, t], hb(psum[2 + t]), ALU.subtract))
                                o.settle()
                            o.run(dve.tensor_tensor(dY[:, t], dY[:, t], hb(psum[4 + t]), ALU.subtract), S["xy_ready"])

                    def d_ks(_):
                        o.settle()
                        dve.wait_ge(S["ks_psum"], 1)
                        dve.wait_ge(S["v0_psum"], 1)
                        o.step(dve.tensor_tensor(TMPD[:, 0], hb(psum[2]), bc_row(dfac[:, 4:8], HEADS), ALU.mult))
                        o.step(dve.tensor_tensor(TMPD[:, 0], vtok[:, 1], TMPD[:, 0], ALU.subtract))
                        o.step(dve.tensor_tensor(dR, TMPD[:, 0], bc_row(beta[:, 4:8], HEADS), ALU.mult), S["r1_ready"])
                        o.step(dve.tensor_tensor(TMPD[:, 1], hb(psum[4]), bc_row(dfac[:, 4:8], HEADS), ALU.mult),
                               S["ks_taken"])

                    def d_o(_):
                        dve.wait_ge(S["o_psum"], 1)
                        o.run(dve.tensor_copy(TMPD[:, 0], hb(psum[2])))
                        o.step(dve.tensor_tensor(TMPD[:, 1], hb(psum[5]), TMPD[:, 1], ALU.add))
                        sq = dX
                        o.step(dve.tensor_tensor(sq, TMPD, TMPD, ALU.mult))
                        o.step(dve.tensor_reduce(ss[:, 0:8], sq.rearrange("p t h d -> p (t h) d"), AX, ALU.add),
                               S["o_ss_ready"])
                        dve.wait_ge(S["z_tanh"], 1)
                        z2 = zt[:, :, :].rearrange("p t d -> p (t d)")
                        o.run(dve.scalar_tensor_tensor(z2, dusel.rearrange("p t h d -> p (t h d)"), 1.0,
                                                       z2, ALU.add, ALU.mult))
                        dve.wait_ge(S["o_rs_ready"], 1)
                        o.step(dve.tensor_scalar(rtmp[:, 0:8], rstd[:, 0:8], 0.5, None, ALU.mult))
                        v = TMPD.rearrange("p t h d -> p (t h) d")
                        o.step(dve.tensor_tensor(v, v, bc_row(rtmp[:, 0:8], 8), ALU.mult))
                        o.step(dve.tensor_tensor(v, v, par_of("d_norm").unsqueeze(1).to_broadcast([P, 8, P]), ALU.mult))
                        o.step(dve.tensor_tensor(v, v, z2.rearrange("p (n d) -> p n d", n=8), ALU.mult),
                               S["d_out_ready"])

                    def attn(i):
                        if i >= 3:
                            b, hd, qt = (i - 3) // 8, (i - 3) % 8 // 2, (i - 3) % 2
                            o.settle()
                            dve.wait_ge(S["at_o_psum"], i - 2)
                            if b == 0:
                                o.run(dve.tensor_copy(ot[:, qt, hd, :], psum[4][:, 0:P]), S["at_o_taken"])
                            else:
                                o.run(dve.tensor_scalar(ot_b[:, qt, hd, :], psum[4][:, 0:P],
                                                        rec_b[:, (i - 3) % 4:(i - 3) % 4 + 1], None, ALU.mult),
                                      S["at_o_taken"])
                        if i >= ATTN:
                            return
                        qt, b = i % 2, i // 8
                        kw, nc_ = (qt + 1) * P, 2 - b
                        o.settle()
                        dve.wait_ge(S["at_s_psum"], i + 1)
                        if i >= 2:
                            dve.wait_ge(S["at_t_psum"], i - 1)
                        mask = con[:, C_CAUSAL + SEQ - kw:C_CAUSAL + SEQ]
                        s = sm[:, i % 2, 0:nc_, 0:kw]
                        src = banks_all[:, 5 + b:7, 0:kw]
                        scale = (64 if b == 0 else P) ** -0.5
                        o.step(dve.scalar_tensor_tensor(s, src, scale, mask.unsqueeze(1).to_broadcast([P, nc_, kw]),
                                                        ALU.mult, ALU.add), S["at_s_taken"])
                        o.step(dve.tensor_reduce(mx[:, 0:nc_], s, AX, ALU.max))
                        o.step(dve.tensor_scalar(nmx[:, 0:nc_], mx[:, 0:nc_], -1.0, None, ALU.mult), S["at_max_ready"])
                        dve.wait_ge(S["at_exp_ready"], 2 * i + 2 if b == 0 else 16 + i - 8 + 1)
                        if b == 0:
                            o.step(dve.reciprocal(rec[:, 0:2], sums[:, 0:2]))
                            o.run(dve.tensor_scalar(rec2[:, 0:1], rec[:, 1:2], lam_neg, None, ALU.mult))
                            o.step(dve.tensor_scalar(s[:, 0, :], s[:, 0, :], rec[:, 0:1], None, ALU.mult))
                            o.step(dve.scalar_tensor_tensor(s[:, 0, :], s[:, 1, :], rec2[:, 0:1], s[:, 0, :],
                                                            ALU.mult, ALU.add), S["at_w_ready"])
                        else:
                            o.step(dve.reciprocal(rec_b[:, i % 4:i % 4 + 1], sums[:, 0:1]), S["at_w_ready"])

                    def a_sq(_):
                        o.settle()
                        o.step(dve.tensor_tensor(dY, ot, ot, ALU.mult))
                        o.step(dve.tensor_reduce(ss[:, 0:8], dY.rearrange("p t h d -> p (t h) d"), AX, ALU.add),
                               S["a_ss_ready"])

                    def a_scale(_):
                        o.settle()
                        dve.wait_ge(S["a_rs_ready"], 1)
                        v = ot.rearrange("p t h d -> p (t h) d")
                        o.step(dve.tensor_tensor(v, v, bc_row(rstd[:, 0:8], 8), ALU.mult))
                        o.run(dve.tensor_tensor(v, v, a_scale_row.unsqueeze(1).to_broadcast([P, 8, P]), ALU.mult),
                              S["a_out_ready"])

                    def branch(j):
                        n, q = BRANCH_ORDER[j // 4], j % 4
                        split_lo(2 * U_BR + j + 3)
                        if j % 2 == 0:
                            dve.wait_ge(S["br_psum"], j // 2 + 1)
                        else:
                            dve.wait_ge(S["unit_done"], U_BR + j // 2 + 1)
                        src = psum[j % 2][:, :].rearrange("p (b t) -> p b t", b=2)
                        g = gates[:, KD * n + 2 * q:KD * n + 2 * q + 2, :]
                        a = acc[:, 2 * q:2 * q + 2, :]
                        if j == 0:
                            o.settle()
                            dve.wait_ge(S["proj_evac"], U_BR)
                            dve.wait_ge(S["at_o_psum"], 8)
                        if j < 4:
                            o.run(dve.scalar_tensor_tensor(a, g, 1.0, src, ALU.add, ALU.mult), S["br_taken"])
                        else:
                            o.settle()
                            o.run(dve.scalar_tensor_tensor(acc_tmp, g, 1.0, src, ALU.add, ALU.mult), S["br_taken"])
                            o.settle()
                            o.run(dve.tensor_tensor(a, a, acc_tmp, ALU.add),
                                  S["acc_ready"] if j >= 12 else None)
                        if j > 12:
                            acc_lo(q - 1)
                        if j == 15:
                            acc_lo(q)

                    def stage(m):
                        dve.wait_ge(S["st_hi_ready"], m + 1)
                        dve.wait_ge(S["c_out_ready"], 1)
                        hi, lo = staged[m % 2]
                        o.run(dve.tensor_tensor(lo, oT[BRANCH_ORDER[m]], hi.bitcast(F32), ALU.subtract),
                              S["st_lo_ready"])

                    def acc_lo(q):
                        dve.wait_ge(S["acc_ready"], q + 1)
                        dve.wait_ge(S["acc_hi_ready"], q + 1)
                        hi, lo = acc_parts[q]
                        o.run(dve.tensor_tensor(lo, acc[:, 2 * q:2 * q + 2, :], hi.bitcast(F32), ALU.subtract),
                              S["acc_lo_ready"])

                    def project_out(j):
                        split_lo(2 * (U_OUT + j) + 3)
                        split_lo(2 * (U_OUT + j) + 4)
                        dve.wait_ge(S["unit_done"], U_OUT + j + 1)
                        v = h[:, :, j * UC:(j + 1) * UC]
                        o.run(dve.scalar_tensor_tensor(v, psum[j % 2][:, :].rearrange("p (t c) -> p t c", t=TT), 0.5,
                                                       v, ALU.mult, ALU.add), S["f_out_taken"])

                    steps = {"stage": stage, "lambdas": lambdas, "c_coef": c_coef, "c_scan": c_scan, "c_conv": c_conv,
                             "d_conv": d_conv, "c_gelu_arg": c_gelu_arg, "c_gelu": c_gelu, "d_silu": silu,
                             "proj": lambda j: split_lo(j + 3),
                             "norm": prepare, "c_gates": c_gates, "ba": ba_dve, "d_tok": d_tok,
                             "d_cum": d_cum, "d_kk": d_kk, "inv_x": inv_x, "d_ks": d_ks, "d_o": d_o, "attn": attn,
                             "a_sq": a_sq, "a_scale": a_scale, "branch": branch, "out": project_out}
                    for what, i in SCHED:
                        if what in steps:
                            steps[what](i)
                    o.settle()

        def half_of(view, f):
            return view[:, f * UNIT // 2:(f + 1) * UNIT // 2]

        def dense_block():
            n = DENSE_CHUNKS
            assert n % 2

            def steps(eng, step, first, final):
                first()
                step(1, 1, 0)
                with eng.Fori(1, (n - 1) // 2) as j:
                    step(2 * j, 0, j)
                    step(2 * j + 1, 1, j)
                final()

            def place(c_par, j, i):
                r = 3 * c_par - 1 + i
                return r % 6, j + r // 6, r % 2

            with nc.Block() as block:
                @block.sync
                def _(sp):
                    def load(k, row, c_par, j, i):
                        if not isinstance(k, int) or k >= 6:
                            sp.wait_ge(S["unit_lo"], k * 2 - 10)
                        slot = place(c_par, j, i)[0]
                        rows = slice(row, row + 1) if isinstance(row, int) else bass.ds(row, 1)
                        sp.dma_start(ffn_raw[slot], dense_units[rows, :, :].rearrange("l p c -> p (l c)")
                                     ).then_inc(slot_loaded[slot], 16)

                    def step(c, c_par, j):
                        for i, row in enumerate((3 * c, 3 * c + 1, 3 * c - 1)):
                            load(3 * c - 1 + i, row, c_par, j, i)

                    def first():
                        for i in range(2):
                            load(i, i, 0, 0, 1 + i)

                    def final():
                        step(n - 1, 0, (n - 1) // 2)
                        load(3 * n - 1, 3 * n - 1, 0, (n - 1) // 2, 3)

                    steps(sp, step, first, final)

                @block.tensor
                def _(pe):
                    norm_pe(pe)

                    def up(i, c_par, k, pair, start=False):
                        w = [v[pair].rearrange("p (k c) -> p k c", k=KD) for v in (w_hi, w_lo)]
                        x = (x_hi, x_lo)
                        for f in range(2):
                            def operands(a, b, k):
                                if start and f == 0:
                                    x_arrives(pe, a, b, k)
                                return w[a][:, k, f * P:(f + 1) * P], x[b][:, k, :]

                            last = product3(pe, psum[2 * i + c_par][:, f * SEQ:(f + 1) * SEQ], operands, KD,
                                            S["unit_hi"], S["unit_lo"], k * 2 + 1)
                        last.then_inc(S["unit_done"], 1)

                    def down(c_par, c, k, pair, first=False, final=False):
                        w = [v[pair].rearrange("p (f c) -> p f c", f=2) for v in (w_hi, w_lo)]
                        x = [v[:, c_par * 512:(c_par + 1) * 512].rearrange("p (f t) -> p f t", f=2)
                             for v in (st_hi, st_lo)]
                        pe.wait_ge(S["f_lo_ready"], c + 1)
                        for i, (a, b) in enumerate(((0, 0), (0, 1), (1, 0))):
                            for f in range(2):
                                if b == 0:
                                    pe.wait_ge(S["unit_lo" if a else "unit_hi"], k * 2 + f + 1)
                                for t in range(TT):
                                    for m in range(2):
                                        last = pe.matmul(psum[4 + 2 * t + m][:, :], x[b][:, f, t * P:(t + 1) * P],
                                                         w[a][:, f, m * 512:(m + 1) * 512],
                                                         start=first and i == 0 and f == 0,
                                                         stop=final and i == 2 and f == 1)
                        last.then_inc(S["unit_done"], 1)

                    def step(c, c_par, j):
                        for i in range(2):
                            up(i, c_par, 3 * c - 1 + i, place(c_par, j, i)[2])
                        down(1 - c_par, c - 1, 3 * c + 1, place(c_par, j, 2)[2], first=isinstance(c, int) and c == 1)

                    def first():
                        for i in range(2):
                            up(i, 0, i, i, start=i == 0)

                    def final():
                        step(n - 1, 0, (n - 1) // 2)
                        down(0, n - 1, 3 * n - 1, (3 * n - 1) % 2, final=True)

                    steps(pe, step, first, final)

                @block.scalar
                def _(act):
                    norm_act(act, Order(act, S["act_own"]))

                    def split_hi(k, slot, loads, pair):
                        act.wait_ge(slot_loaded[slot], (loads + 1) * 16)
                        for f in range(2):
                            act.activation(half_of(w_hi[pair], f), half_of(ffn_raw[slot], f),
                                           ACT.Copy).then_inc(S["unit_hi"], 1)

                    def step(c, c_par, j, more=True):
                        act.wait_ge(S["unit_done"], 3 * c)
                        act.activation(fth[c_par], psum[c_par][:, :], ACT.Tanh, scale=0.5).then_inc(S["f_tanh"], 1)
                        split_hi(3 * c + 1, *place(c_par, j, 2))
                        act.wait_ge(S["unit_done"], 3 * c + 1)
                        split_hi(3 * c + 2, *place(c_par, j, 3))
                        hidden_hi(c, c_par)
                        if more:
                            act.wait_ge(S["unit_done"], 3 * c + 2)
                            split_hi(3 * c + 3, *place(c_par, j, 4))

                    def hidden_hi(c, c_par):
                        act.wait_ge(S["f_h_ready"], c + 1)
                        act.activation(st_hi[:, c_par * 512:(c_par + 1) * 512], zt[:, c_par, :],
                                       ACT.Copy).then_inc(S["f_hi_ready"], 1)

                    def first():
                        o = Order(act, S["act_own"])
                        split_hi(0, 0, 0, 0)
                        norm_split_act(act, o)
                        split_hi(1, 1, 0, 1)
                        act.wait_ge(S["unit_done"], 1)
                        act.activation(fth[0], psum[0][:, :], ACT.Tanh, scale=0.5).then_inc(S["f_tanh"], 1)
                        split_hi(2, 2, 0, 0)
                        act.wait_ge(S["unit_done"], 2)
                        split_hi(3, 3, 0, 1)
                        hidden_hi(0, 0)

                    steps(act, step, first, lambda: step(n - 1, 0, (n - 1) // 2, more=False))

                @block.gpsimd
                def _(pool):
                    norm_pool(pool, Order(pool, S["pool_own"]))

                @block.vector
                def _(dve):
                    o = Order(dve, S["dve_own"])

                    def split_lo(k, slot, loads, pair, halves=(0, 1)):
                        for f in halves:
                            dve.wait_ge(S["unit_hi"], k * 2 + f + 1)
                            dve.tensor_tensor(half_of(w_lo[pair], f), half_of(ffn_raw[slot], f),
                                              half_of(w_hi[pair], f).bitcast(F32), ALU.subtract
                                              ).then_inc(S["unit_lo"], 1)

                    def gate(c, c_par):
                        dve.wait_ge(S["f_tanh"], c + 1)
                        dve.scalar_tensor_tensor(fs[c_par], fth[c_par], 1.0, psum[c_par][:, :], ALU.add,
                                                 ALU.mult).then_inc(S["f_s_ready"], 1)

                    def hidden(c, c_par, w3_done):
                        dve.wait_ge(S["unit_done"], w3_done)
                        dve.wait_ge(S["f_s_ready"], c + 1)
                        dve.tensor_tensor(zt[:, c_par, :], fs[c_par], psum[2 + c_par][:, :],
                                          ALU.mult).then_inc(S["f_h_ready"], 1)

                    def hidden_lo(c, c_par):
                        dve.wait_ge(S["f_hi_ready"], c + 1)
                        dve.wait_ge(S["f_h_ready"], c + 1)
                        cut = (slice(None), slice(c_par * 512, (c_par + 1) * 512))
                        dve.tensor_tensor(st_lo[cut], zt[:, c_par, :], st_hi[cut].bitcast(F32),
                                          ALU.subtract).then_inc(S["f_lo_ready"], 1)

                    def step(c, c_par, j, more=True):
                        gate(c, c_par)
                        split_lo(3 * c + 1, *place(c_par, j, 2))
                        hidden(c, c_par, 3 * c + 1)
                        split_lo(3 * c + 2, *place(c_par, j, 3))
                        hidden_lo(c, c_par)
                        if more:
                            split_lo(3 * c + 3, *place(c_par, j, 4))

                    def first():
                        norm_dve(dve, o, par_of("norm_ffn"), lambda: split_lo(0, 0, 0, 0, halves=(0,)))
                        norm_split_dve(dve, o)
                        split_lo(0, 0, 0, 0, halves=(1,))
                        split_lo(1, 1, 0, 1)
                        gate(0, 0)
                        split_lo(2, 2, 0, 0)
                        hidden(0, 0, 2)
                        split_lo(3, 3, 0, 1)
                        hidden_lo(0, 0)

                    steps(dve, step, first, lambda: step(n - 1, 0, (n - 1) // 2, more=False))
                    dve.wait_ge(S["unit_done"], 3 * n)
                    for t in range(TT):
                        for m in range(2):
                            v = h[:, t, m * 512:(m + 1) * 512]
                            o.run(dve.scalar_tensor_tensor(v, psum[4 + 2 * t + m][:, :], 0.5, v, ALU.mult, ALU.add))
                    o.settle()

        def moe_block():
            n = MOE_CHUNKS
            kinds = ("w1", "w3", "w2")

            with nc.Block() as block:
                @block.sync
                def _(sp):
                    def load(row, i, slot):
                        sp.dma_start(ffn_raw[2 * i + slot], moe_units[row, :, :].rearrange("l p c -> p (l c)")
                                     ).then_inc(slot_loaded[2 * i + slot], 16)

                    def load_free(i, expert, c, q, slot):
                        sp.wait_ge(S[kinds[i] + "_lo"], 2 * q - 2)
                        load(bass.ds((expert * n + c) * 3 + i, 1), i, slot)

                    def load_next(expert, c, q, slot, expert2, c2):
                        load_free(2, expert, c, q, slot)
                        for i in range(2):
                            load_free(i, expert2, c2, q + 2, slot)

                    for c in range(2):
                        for i in range(3):
                            load(slice(3 * c + i, 3 * c + i + 1), i, c)
                    for i in range(2):
                        sp.wait_ge(S[kinds[i] + "_lo"], 2)
                        load(slice(6 + i, 7 + i), i, 0)
                    sp.wait_ge(S["table_ready"], 1)
                    total = sp.value_load(table_i[0:1, PASSES + 1:PASSES + 2], min_val=EXPERTS, max_val=PASSES)
                    with sp.Fori(0, PASSES) as p:
                        expert = sp.value_load(table_i[0:1, bass.ds(p, 1)], min_val=0, max_val=EXPERTS - 1)
                        after = sp.value_load(table_i[0:1, bass.ds(p + 1, 1)], min_val=0, max_val=EXPERTS - 1)
                        with sp.If(p < total):
                            q0 = p * n
                            for i in range(2):
                                load_free(i, expert, 3, q0 + 3, 1)
                            with sp.Fori(0, (n - 4) // 2) as j:
                                for k in range(2):
                                    c = 2 * j + 2 + k
                                    load_next(expert, c, q0 + c, k, expert, c + 2)
                            for k in range(2):
                                load_next(expert, n - 2 + k, q0 + n - 2 + k, k, after, k)
                            load_next(after, 0, q0 + n, 0, after, 2)
                            load_free(2, after, 1, q0 + n + 1, 1)
                        with sp.Else():
                            sp.nop()
                    for count, slots in ((1, (1, 3, 4, 5)), (2, (0, 2))):
                        for slot in slots:
                            sp.wait_ge(slot_loaded[slot], total * (n // 2 * 16) + count * 16)
                        sp.sem_inc(S["loads_over"], 1)

                @block.tensor
                def _(pe):
                    pe.sem_inc(S["w2_used"], 1)
                    norm_pe(pe)
                    pe.wait_ge(S["xraw_ready"], 4)
                    r = par_of("router").rearrange("p (k e) -> p k e", k=KD)
                    for t in range(TT):
                        for k in range(KD):
                            last = pe.matmul(psum[0][:, 8 * t:8 * t + 8], xraw[:, k, t * P:(t + 1) * P], r[:, k, :],
                                             start=(k == 0), stop=(k == KD - 1))
                    last.then_inc(S["rt_psum"], 1)
                    pe.wait_ge(S["rt_member"], 1)
                    m = member.rearrange("p (t e) -> p t e", t=TT)
                    pe.matmul(psum[1][:, 0:8], trix, m[:, 0, :], start=True, stop=True)
                    pe.matmul(psum[1][:, 8:16], ones, m[:, 0, :], start=True, stop=False)
                    pe.matmul(psum[1][:, 8:16], trix, m[:, 1, :], start=False, stop=True)
                    pe.matmul(psum[1][:, 16:24], ones, m[:, 0, :], start=True, stop=False)
                    pe.matmul(psum[1][:, 16:24], ones, m[:, 1, :], start=False, stop=True).then_inc(S["rank_psum"], 1)
                    def gather(p):
                        for k in range(KD):
                            for t in range(TT):
                                last = pe.matmul(psum[6 + k // 4][:, (k % 4) * P:(k % 4 + 1) * P],
                                                 xs[:, t, k * P:(k + 1) * P], sel[:, t, :], start=(t == 0),
                                                 stop=(t == TT - 1))
                        last.then_inc(S["gather_psum"], 1)

                    def scatter(t, p):
                        pe.wait_ge(S["y_ready"], p * 2 + 2)
                        pe.wait_ge(S["selT_ready"], p + 1)
                        pe.wait_ge(S["scat_taken"], p * 4 + 2 * t + 2)
                        for m in range(2):
                            last = pe.matmul(psum[6 + m][:, :], selgT[:, t * P:(t + 1) * P],
                                             yexp[:, m * 512:(m + 1) * 512], start=True, stop=True)
                        last.then_inc(S["scat_psum"], 1)

                    def up(i, par_, q):
                        w = [v.rearrange("p (k c) -> p k c", k=KD) for v in w_parts[i]]
                        x = (xsel_hi, xsel_lo)
                        product3(pe, psum[par_ if i == 0 else 2][:, 0:CHUNK],
                                 lambda a, b, k: (x[b][:, k, :], w[a][:, k, :]), KD,
                                 S[kinds[i] + "_hi"], S[kinds[i] + "_lo"], q * 2 + 1
                                 ).then_inc(S[("h1_psum", "h3_psum")[i]], 1)

                    def turn(par_, q):
                        pe.wait_ge(S["f_h_ready"], q + 1)
                        for f in range(2):
                            last = pe.transpose(psum[3][:, f * P:(f + 1) * P], hf[par_][:, f * P:(f + 1) * P],
                                                ident)
                        last.then_inc(S["hT_psum"], 1)

                    def down(par_, q, first=False, final=False):
                        w = [v.rearrange("p (f c) -> p f c", f=2) for v in w_parts[2]]
                        x = (ht_hi[par_], ht_lo[par_])
                        pe.wait_ge(S["f_lo_ready"], q + 1)
                        for i, (a, b) in enumerate(((0, 0), (0, 1), (1, 0))):
                            for f in range(2):
                                if b == 0:
                                    pe.wait_ge(S["w2_lo" if a else "w2_hi"], q * 2 + f + 1)
                                for m in range(2):
                                    last = pe.matmul(psum[4 + m][:, :], x[b][:, f * P:(f + 1) * P],
                                                     w[a][:, f, m * 512:(m + 1) * 512],
                                                     start=first and i == 0 and f == 0,
                                                     stop=final and i == 2 and f == 1)
                        last.then_inc(S["w2_used"], 1)

                    def step(par_, q):
                        up(0, par_, q)
                        turn(1 - par_, q - 1)
                        up(1, par_, q)
                        down(1 - par_, q - 1)

                    pe.wait_ge(S["sel_ready"], 1)
                    gather(0)
                    pe.wait_ge(S["table_ready"], 1)
                    total = pe.value_load(table_i[0:1, PASSES + 1:PASSES + 2], min_val=EXPERTS, max_val=PASSES)
                    with pe.Fori(0, PASSES) as p:
                        with pe.If(p < total):
                            q0 = p * n
                            pe.wait_ge(S["xsel_lo_ready"], p * 2 + 2)
                            up(0, 0, q0)
                            scatter(0, p)
                            up(1, 0, q0)
                            scatter(1, p)
                            up(0, 1, q0 + 1)
                            turn(0, q0)
                            pe.wait_ge(S["scat_taken"], p * 4 + 6)
                            for t in range(TT):
                                last = pe.transpose(psum[6][:, t * P:(t + 1) * P], selg[:, t, :], ident)
                            last.then_inc(S["selT_psum"], 1)
                            up(1, 1, q0 + 1)
                            down(0, q0, first=True)
                            with pe.Fori(0, (n - 2) // 2) as j:
                                for k in range(2):
                                    step(k, q0 + 2 * j + 2 + k)
                            pe.wait_ge(S["sel_ready"], p + 2)
                            pe.wait_ge(S["selT_ready"], p + 2)
                            gather(p + 1)
                            turn(1, q0 + n - 1)
                            down(1, q0 + n - 1, final=True)
                        with pe.Else():
                            pe.nop()
                    for t in range(TT):
                        scatter(t, total)

                @block.scalar
                def _(act):
                    norm_act(act, Order(act, S["act_own"]))

                    def split_hi(i, q, slot, loads):
                        act.wait_ge(slot_loaded[2 * i + slot], loads * 16)
                        for f in range(2):
                            act.activation(half_of(w_parts[i][0], f), half_of(ffn_raw[2 * i + slot], f),
                                           ACT.Copy).then_inc(S[kinds[i] + "_hi"], 1)

                    for i in range(2):
                        split_hi(i, 0, 0, 1)
                    for m in range(2):
                        act.activation(yexp[:, m * 512:(m + 1) * 512], con[:, 0:512], ACT.Copy,
                                       scale=0.0).then_inc(S["y_ready"], 1)
                    act.activation(selgT, con[:, 0:SEQ], ACT.Copy, scale=0.0).then_inc(S["selT_ready"], 1)
                    act.wait_ge(S["rt_arg"], 1)
                    act.activation(em, dm, ACT.Exp).then_inc(S["rt_exp"], 1)

                    def xsel_split(p):
                        for m in range(2):
                            act.wait_ge(S["xsel_ready"], p * 2 + m + 1)
                            act.activation(xsel_hi[:, 4 * m:4 * m + 4, :], xsel[:, 4 * m:4 * m + 4, :],
                                           ACT.Copy).then_inc(S["xsel_hi_ready"], 1)

                    def hidden_hi(par_, q):
                        act.wait_ge(S["hT_psum"], q + 1)
                        act.activation(ht_hi[par_], psum[3][:, 0:CHUNK], ACT.Copy).then_inc(S["f_hi_ready"], 1)

                    def step(par_, q, pairs, first=False, p=None):
                        act.wait_ge(S["h1_psum"], q + 1)
                        act.activation(fth[par_][:, 0:CHUNK], psum[par_][:, 0:CHUNK], ACT.Tanh,
                                       scale=0.5).then_inc(S["f_tanh"], 1)
                        if not first:
                            hidden_hi(1 - par_, q - 1)
                        split_hi(0, q + 1, 1 - par_, pairs + 1 + par_)
                        act.wait_ge(S["h3_psum"], q + 1)
                        split_hi(1, q + 1, 1 - par_, pairs + 1 + par_)
                        act.wait_ge(S["w2_used"], q + 1)
                        split_hi(2, q, par_, pairs + 1)

                    xsel_split(0)
                    act.wait_ge(S["table_ready"], 1)
                    total = act.value_load(table_i[0:1, PASSES + 1:PASSES + 2], min_val=EXPERTS, max_val=PASSES)
                    with act.Fori(0, PASSES) as p:
                        with act.If(p < total):
                            q0, pairs = p * n, p * (n // 2)
                            step(0, q0, pairs, first=True)
                            step(1, q0 + 1, pairs)
                            act.wait_ge(S["selT_psum"], p + 1)
                            act.activation(selgT, psum[6][:, 0:SEQ], ACT.Copy).then_inc(S["selT_ready"], 1)
                            with act.Fori(0, (n - 2) // 2) as j:
                                for k in range(2):
                                    step(k, q0 + 2 * j + 2 + k, pairs + j + 1)
                            hidden_hi(1, q0 + n - 1)
                            xsel_split(p + 1)
                            act.wait_ge(S["w2_used"], q0 + n + 1)
                            for m in range(2):
                                act.activation(yexp[:, m * 512:(m + 1) * 512], psum[4 + m][:, :],
                                               ACT.Copy).then_inc(S["y_ready"], 1)
                        with act.Else():
                            act.nop()

                @block.gpsimd
                def _(pool):
                    norm_pool(pool, Order(pool, S["pool_own"]))
                    pool.wait_ge(S["table_ready"], 1)
                    total = pool.value_load(table_i[0:1, PASSES + 1:PASSES + 2], min_val=EXPERTS, max_val=PASSES)
                    with pool.Fori(0, PASSES) as p:
                        with pool.If(p < total):
                            with pool.Fori(0, n // 2) as j:
                                for k in range(2):
                                    for f in range(2):
                                        pool.wait_ge(S["w2_hi"], (p * n + 2 * j + k) * 2 + f + 1)
                                        pool.tensor_tensor(half_of(w_parts[2][1], f), half_of(ffn_raw[4 + k], f),
                                                           half_of(w_parts[2][0], f).bitcast(F32),
                                                           ALU.subtract).then_inc(S["w2_lo"], 1)
                        with pool.Else():
                            pool.nop()

                @block.vector
                def _(dve):
                    o = Order(dve, S["dve_own"])
                    dve.sem_inc(S["scat_taken"], 2)
                    iota = con[:, C_IOTA:C_IOTA + P]
                    gain = par_of("norm_ffn")

                    def select(p):
                        for t in range(TT):
                            dve.tensor_scalar(sel[:, t, :], iota, so[:, t, bass.ds(p, 1)], None, ALU.is_equal)
                        for t in range(TT):
                            ins = dve.tensor_scalar(selg[:, t, :], iota, so[:, t, bass.ds(p, 1)],
                                                    go[:, t, bass.ds(p, 1)], ALU.is_equal, ALU.mult)
                        ins.then_inc(S["sel_ready"], 1)

                    def xsel_gain(p):
                        dve.wait_ge(S["gather_psum"], p + 1)
                        for m in range(2):
                            dve.tensor_tensor(xsel[:, 4 * m:4 * m + 4, :],
                                              psum[6 + m][:, :].rearrange("p (k s) -> p k s", k=4),
                                              gain[:, 4 * m:4 * m + 4].unsqueeze(2).to_broadcast([P, 4, P]),
                                              ALU.mult).then_inc(S["xsel_ready"], 1)

                    def xsel_split(p):
                        for m in range(2):
                            dve.wait_ge(S["xsel_hi_ready"], p * 2 + m + 1)
                            cut = (slice(None), slice(4 * m, 4 * m + 4), slice(None))
                            dve.tensor_tensor(xsel_lo[cut], xsel[cut], xsel_hi[cut].bitcast(F32),
                                              ALU.subtract).then_inc(S["xsel_lo_ready"], 1)

                    def split_lo(i, q, slot, halves=(0, 1)):
                        for f in halves:
                            dve.wait_ge(S[kinds[i] + "_hi"], q * 2 + f + 1)
                            dve.tensor_tensor(half_of(w_parts[i][1], f), half_of(ffn_raw[2 * i + slot], f),
                                              half_of(w_parts[i][0], f).bitcast(F32),
                                              ALU.subtract).then_inc(S[kinds[i] + "_lo"], 1)

                    def hidden_lo(par_, q):
                        dve.wait_ge(S["f_hi_ready"], q + 1)
                        dve.tensor_tensor(ht_lo[par_], psum[3][:, 0:CHUNK], ht_hi[par_].bitcast(F32),
                                          ALU.subtract).then_inc(S["f_lo_ready"], 1)

                    def scatter_add(t, p):
                        dve.wait_ge(S["scat_psum"], p * 2 + t + 1)
                        for m in range(2):
                            v = h[:, t, m * 512:(m + 1) * 512]
                            dve.scalar_tensor_tensor(v, psum[6 + m][:, :], 0.5, v, ALU.mult,
                                                     ALU.add).then_inc(S["scat_taken"], 1)

                    def step(par_, q, first_pass=None):
                        dve.wait_ge(S["f_tanh"], q + 1)
                        dve.scalar_tensor_tensor(fs[par_][:, 0:CHUNK], fth[par_][:, 0:CHUNK], 1.0,
                                                 psum[par_][:, 0:CHUNK], ALU.add, ALU.mult
                                                 ).then_inc(S["f_s_ready"], 1)
                        if first_pass is None:
                            hidden_lo(1 - par_, q - 1)
                        split_lo(0, q + 1, 1 - par_)
                        if first_pass is not None:
                            scatter_add(0, first_pass)
                        dve.wait_ge(S["h3_psum"], q + 1)
                        dve.wait_ge(S["f_s_ready"], q + 1)
                        dve.tensor_tensor(hf[par_], fs[par_][:, 0:CHUNK], psum[2][:, 0:CHUNK],
                                          ALU.mult).then_inc(S["f_h_ready"], 1)
                        split_lo(1, q + 1, 1 - par_)
                        if first_pass is not None:
                            scatter_add(1, first_pass)

                    norm_dve(dve, o, par_of("norm_ffn"), lambda: split_lo(0, 0, 0, halves=(0,)))
                    split_lo(0, 0, 0, halves=(1,))
                    o.settle()
                    eidx = con[:, C_EIDX:C_EIDX + EXPERTS]
                    erev = con[:, C_EREV:C_EREV + EXPERTS]

                    def te(c):
                        return c.rearrange("p (t e) -> p t e", t=TT)

                    def each_t(row):
                        return row.unsqueeze(1).to_broadcast([P, TT, EXPERTS])

                    def each_e(c):
                        return c.unsqueeze(2).to_broadcast([P, TT, EXPERTS])

                    def best(src, value, chosen):
                        o.step(dve.tensor_reduce(value, te(src), AX, ALU.max))
                        o.step(dve.tensor_tensor(te(eq), te(src), each_e(value), ALU.is_equal))
                        o.step(dve.tensor_tensor(te(eq), te(eq), each_t(erev), ALU.mult))
                        o.step(dve.tensor_reduce(fi, te(eq), AX, ALU.max))
                        o.step(dve.tensor_tensor(te(chosen), each_t(erev), each_e(fi), ALU.is_equal))

                    dve.wait_ge(S["rt_psum"], 1)
                    o.step(dve.tensor_copy(lg, psum[0][:, 0:16]))
                    best(lg, m0, one1)
                    o.step(dve.scalar_tensor_tensor(lg, one1, -3.0e38, lg, ALU.mult, ALU.add))
                    best(lg, m1, one2)
                    o.run(dve.tensor_tensor(member, one1, one2, ALU.add), S["rt_member"])
                    o.step(dve.tensor_tensor(dm, m1, m0, ALU.subtract), S["rt_arg"])
                    dve.wait_ge(S["rt_exp"], 1)
                    o.step(dve.tensor_scalar(p0, em, 1.0, None, ALU.add))
                    o.step(dve.reciprocal(p0, p0))
                    o.step(dve.tensor_tensor(p1, em, p0, ALU.mult))
                    o.step(dve.tensor_tensor(te(one1), te(one1), each_e(p0), ALU.mult))
                    o.step(dve.tensor_tensor(te(one2), te(one2), each_e(p1), ALU.mult))
                    o.step(dve.tensor_tensor(gsel, one1, one2, ALU.add))
                    dve.wait_ge(S["rank_psum"], 1)
                    o.step(dve.scalar_tensor_tensor(vslot, psum[1][:, 0:16], 1.0, member, ALU.add, ALU.mult))
                    o.step(dve.tensor_scalar(vslot, vslot, -1.0, None, ALU.add))
                    so = slot_of.rearrange("p (t q) -> p t q", t=TT)
                    go = gate_of.rearrange("p (t q) -> p t q", t=TT)
                    o.run(dve.tensor_copy(so[:, :, 0:EXPERTS], te(vslot)))
                    o.run(dve.tensor_copy(go[:, :, 0:EXPERTS], te(gsel)))
                    o.settle()
                    select(0)
                    o.step(dve.tensor_scalar(over, psum[1][:, 16:24], float(P), None, ALU.is_gt))
                    o.step(dve.memset(onesE, 1.0))
                    o.step(dve.tensor_tensor_scan(incl, onesE, over, 0.0, ALU.mult, ALU.add))
                    o.step(dve.tensor_tensor(pos, incl, over, ALU.subtract))
                    o.run(dve.tensor_copy(table[:, 0:EXPERTS], eidx))
                    o.run(dve.memset(so[:, :, PASSES:PASSES + 1], -1.0))
                    o.run(dve.memset(go[:, :, PASSES:PASSES + 1], 0.0))
                    o.run(dve.memset(table[:, PASSES:PASSES + 1], 0.0))
                    o.run(dve.tensor_scalar(table[:, PASSES + 1:PASSES + 2], incl[:, EXPERTS - 1:EXPERTS],
                                            float(EXPERTS), None, ALU.add))
                    for q in range(OVERFLOWS):
                        sq = selq[:, q * EXPERTS:(q + 1) * EXPERTS]
                        o.step(dve.scalar_tensor_tensor(sq, pos, float(q), over, ALU.is_equal, ALU.mult))
                        o.step(dve.tensor_tensor(tmp8, sq, eidx, ALU.mult))
                        o.step(dve.tensor_reduce(table[:, EXPERTS + q:EXPERTS + q + 1], tmp8, AX, ALU.add))
                        for src, dst, shift in ((vslot, so, -float(P)), (gsel, go, 0.0)):
                            o.step(dve.tensor_tensor(te(pick), te(src), each_t(sq), ALU.mult))
                            o.step(dve.tensor_reduce(fi, te(pick), AX, ALU.add))
                            o.step(dve.tensor_scalar(dst[:, :, EXPERTS + q], fi, shift, None, ALU.add))
                    o.settle()
                    o.step(dve.tensor_copy(table_i[:, :], table), S["table_ready"])
                    xsel_gain(0)
                    xsel_split(0)
                    split_lo(1, 0, 0)
                    total = dve.value_load(table_i[0:1, PASSES + 1:PASSES + 2], min_val=EXPERTS, max_val=PASSES)
                    with dve.Fori(0, PASSES) as p:
                        with dve.If(p < total):
                            q0 = p * n
                            step(0, q0, first_pass=p)
                            step(1, q0 + 1)
                            dve.wait_ge(S["gather_psum"], p + 1)
                            dve.wait_ge(S["selT_psum"], p + 1)
                            select(p + 1)
                            with dve.Fori(0, (n - 2) // 2) as j:
                                for k in range(2):
                                    step(k, q0 + 2 * j + 2 + k)
                            xsel_gain(p + 1)
                            hidden_lo(1, q0 + n - 1)
                            xsel_split(p + 1)
                        with dve.Else():
                            dve.nop()
                    for t in range(TT):
                        scatter_add(t, total)

        with nc.Fori(0, LAYERS) as layer:
            mixer_block(layer)
            clear_semaphores()
            with nc.If(layer < 1):
                dense_block()
            with nc.Else():
                moe_block()
            clear_semaphores()

        with nc.Block() as block:
            gain_row = raw[0][:, 0:DM]

            @block.sync
            def _(sp):
                sp.dma_start(gain_row, norm_final).then_inc(S["in_loaded"], 16)
                for t in range(TT):
                    sp.wait_ge(S["xs_ready"], t + 1)
                    sp.dma_start(out[t * P:(t + 1) * P, :], xs[:, t, :]).then_inc(S["out_stored"], 16)
                sp.wait_ge(S["out_stored"], TT * 16)

            @block.scalar
            def _(act):
                norm_act(act, Order(act, S["act_own"]))

            @block.gpsimd
            def _(pool):
                norm_pool(pool, Order(pool, S["pool_own"]))

            @block.vector
            def _(dve):
                dve.wait_ge(S["in_loaded"], 16)
                dve.wait_ge(S["rstd_ready"], 1)
                for t in range(TT):
                    dve.scalar_tensor_tensor(xs[:, t, :], h[:, t, :], rstd[:, t:t + 1], gain_row, ALU.mult,
                                             ALU.mult).then_inc(S["xs_ready"], 1)


def _constants(np):
    c = np.zeros((P, C_COLS), np.float32)
    j, i = np.arange(P)[:, None], np.arange(P)[None, :]
    c[:, C_IDENT:C_IDENT + P] = j == i
    c[:, C_ONES:C_ONES + P] = 1
    c[:, C_TRI:C_TRI + P] = j <= i
    c[:, C_TRIX:C_TRIX + P] = j < i
    c[:, C_CAUSAL + P:C_CAUSAL + 2 * P] = np.where(i <= j, 0, NEG)
    c[:, C_NEGT:C_NEGT + P] = np.where(j <= i, 0, NEG)
    for s in range(LEVELS):
        size = 1 << s
        c[:, C_LEVEL + s * P:C_LEVEL + (s + 1) * P] = (i // size % 2 == 1) & (j // size == i // size - 1)
    c[:, C_IOTA:C_IOTA + P] = i
    c[:, C_EIDX:C_EIDX + EXPERTS] = np.arange(EXPERTS)
    c[:, C_EREV:C_EREV + EXPERTS] = EXPERTS - np.arange(EXPERTS)
    c[:, C_HALF:] = -0.5
    return c


def _units(np, w, cols):
    rows, n = w.shape
    return w.reshape(rows // P, P, n // cols, cols).transpose(2, 1, 0, 3).reshape(n // cols, P, -1)


def _chunks(np, w1, w3, w2):
    a, b = _units(np, w1, CHUNK), _units(np, w3, CHUNK)
    c = w2.reshape(-1, CHUNK // P, P, DM).transpose(0, 2, 1, 3).reshape(a.shape[0], P, -1)
    return np.stack([a, b, c], 1).reshape(-1, P, UNIT)


def _layer_params(np, v, layer):
    parts = {}

    def channels(a, n):
        return a.reshape(n, P, -1).transpose(1, 0, 2).reshape(P, -1)

    def rows(a):
        return np.broadcast_to(a.reshape(1, -1), (P, a.size))

    lam_init = 0.8 - 0.6 * math.exp(-0.3 * layer)
    parts["norm_mix"] = channels(v["norm_mix"][layer], KD)
    parts["norm_ffn"] = channels(v["norm_ffn"][layer], KD)
    parts["c_conv_w"] = channels(v["c_conv_w"][layer].T, NB)
    parts["c_conv_b"] = channels(v["c_conv_b"][layer], NB)
    parts["c_b_a"] = channels(v["c_b_a"][layer].reshape(-1), NB)
    parts["c_b_x"] = channels(v["c_b_x"][layer].reshape(-1), NB)
    parts["c_lambda"] = channels(v["c_lambda"][layer], NB)
    parts["d_conv_w"] = channels(v["d_conv_w"][layer].T, 3 * NB)
    parts["b_gate"] = channels(v["b_gate"][layer].reshape(-1), BRANCHES * KD)
    parts["a_subln"] = rows(v["a_subln"][layer])
    parts["d_norm"] = rows(v["d_norm"][layer])
    parts["lam"] = rows(np.stack([v[n][layer] for n in ("lam_q1", "lam_k1", "lam_q2", "lam_k2")]))
    parts["d_A_log"] = rows(v["d_A_log"][layer])
    parts["d_dt_bias"] = rows(v["d_dt_bias"][layer])
    parts["w_ba"] = channels(v["w_in"][layer][:, 12 * MIX:], KD)
    parts["lam_init"] = np.full((P, 1), lam_init, np.float32)
    parts["out_scale"] = np.full((P, 1), 1.0 - lam_init, np.float32)
    moe = layer % 2 == 1
    parts["router"] = channels(v["router"][layer // 2], KD) if moe else np.zeros((P, KD * EXPERTS), np.float32)
    return np.concatenate([parts[n] for n, _ in PARTS], 1)


def kernel(**inputs):
    import numpy as np
    import concourse.bacc as bacc
    from concourse.bass_utils import run_bass_kernel_spmd

    v = {k: np.asarray(a) for k, a in inputs.items()}
    arrays = {"x": v["x"].reshape(SEQ, DM), "consts": _constants(np),
              "params": np.stack([_layer_params(np, v, layer) for layer in range(LAYERS)])}
    cd = np.zeros((LAYERS, P, 2, NB, P), np.float32)
    for g, name in enumerate(("c_w_a", "c_w_x")):
        w = v[name].reshape(LAYERS, NB, 2, 64, 64)
        for half in range(2):
            s = slice(64 * half, 64 * half + 64)
            cd[:, s, g, :, s] = w[:, :, half].transpose(0, 2, 1, 3)
    arrays["cdiag"] = cd.reshape(LAYERS, P, -1)
    mix = []
    for layer in range(LAYERS):
        w_in = _units(np, v["w_in"][layer][:, :12 * MIX], UC)
        per = MIX // UC
        order = [b * per + i for b in (6, 7, 8, 9, 10, 11, 0, 1, 2, 3, 4, 5) for i in range(per)]
        mix += [w_in[order], _units(np, v["w_gate"][layer].reshape(DM, -1), UC)]
        mix += [_units(np, v["w_branch"][layer][n], 2 * UC) for n in BRANCH_ORDER]
        mix += [_units(np, v["w_out"][layer], UC)]
    arrays["mix_units"] = np.concatenate(mix).reshape(LAYERS, MIX_UNITS, P, UNIT)
    arrays["dense_units"] = _chunks(np, v["ffn_w1"][0], v["ffn_w3"][0], v["ffn_w2"][0])
    arrays["moe_units"] = np.concatenate([_chunks(np, v["moe_w1"][0][e], v["moe_w3"][0][e], v["moe_w2"][0][e])
                                          for e in range(EXPERTS)])
    arrays["norm_final"] = np.ascontiguousarray(np.broadcast_to(v["norm_final"][None], (P, DM)))

    nc = bacc.Bacc("TRN2", target_bir_lowering=False, num_devices=1)
    aps = {n: nc.dram_tensor(n, a.shape, F32, kind="ExternalInput").ap() for n, a in arrays.items()}
    out = nc.dram_tensor("out", (SEQ, DM), F32, kind="ExternalOutput").ap()
    hybrid_trunk(nc, **aps, out=out)
    got = run_bass_kernel_spmd(nc, [arrays], core_ids=[0])
    return got.results[0]["out"].reshape(1, SEQ, DM)
```
